# Optimizing a Trainium2 kernel written in Bass

```python
import math
import jax
import jax.numpy as jnp
from jax import lax
import numpy as np

D_MODEL = 1024
BATCH = 1
SEQ = 512
DEPTH = 2
DEC_BATCH = 8
DEC_SEQ = 1
PAST_LEN = 1024
PAGE_SIZE = 128

ROPE_THETA = 10000.0
LN_EPS = 1e-5
NEG_INF = -1e30
ALPHA = (2 * DEPTH) ** 0.25
BETA = (8 * DEPTH) ** -0.25
N_EVEN = (DEPTH + 1) // 2
N_ODD = DEPTH // 2

WINDOW = 128
SWA_HEADS = 8
SWA_KV_HEADS = 2
SWA_HEAD_DIM = 64
SWA_GROUP = SWA_HEADS // SWA_KV_HEADS
RET_HEADS = 8
RET_DK = 64
RET_DV = 64
RET_CHUNK = 128
SWA_Q_W = SWA_HEADS * SWA_HEAD_DIM
SWA_KV_W = SWA_KV_HEADS * SWA_HEAD_DIM
RET_QK_W = RET_HEADS * RET_DK
RET_V_W = RET_HEADS * RET_DV
EVEN_SPLITS = (SWA_Q_W, SWA_KV_W, SWA_KV_W, RET_QK_W, RET_QK_W, RET_V_W, RET_V_W)
EVEN_IN_W = SWA_Q_W + 2 * SWA_KV_W + 2 * RET_QK_W + 2 * RET_V_W
EVEN_OUT_W = SWA_Q_W + RET_V_W
MLA_HEADS = 8
MLA_Q_RANK = 256
MLA_KV_RANK = 128
MLA_NOPE = 64
MLA_ROPE = 32
MLA_V = 64
MLA_IN_W = MLA_Q_RANK + MLA_KV_RANK + MLA_ROPE
MLA_ROW_W = MLA_KV_RANK + MLA_ROPE
Q_BLOCK = 128
N_MEM = 256
MEM_HEADS = 4
MEM_HEAD_DIM = 64
MEM_W = MEM_HEADS * MEM_HEAD_DIM
MOE_GROUPS = 4
MOE_PER_GROUP = 4
MOE_EXPERTS = MOE_GROUPS * MOE_PER_GROUP
MOE_TOP_K = 2
D_EXPERT = 256

kernel_name = 'hybrid_swa_retention_mla_hmoe_step'

def layer_norm(x, g, b):
    xf = x.astype(jnp.float32)
    mu = jnp.mean(xf, axis=-1, keepdims=True)
    var = jnp.mean(jnp.square(xf - mu), axis=-1, keepdims=True)
    return ((xf - mu) * lax.rsqrt(var + LN_EPS) * g + b).astype(x.dtype)

def rms_norm(x, g):
    xf = x.astype(jnp.float32)
    ms = jnp.mean(jnp.square(xf), axis=-1, keepdims=True)
    return (xf * lax.rsqrt(ms + LN_EPS) * g).astype(x.dtype)

def rope(x, pos):
    d = x.shape[-1]
    inv = ROPE_THETA ** (-jnp.arange(0, d, 2, dtype=jnp.float32) / d)
    ang = pos.astype(jnp.float32)[:, None] * inv[None, :]
    cos = jnp.cos(ang)[:, None, :]
    sin = jnp.sin(ang)[:, None, :]
    x1, x2 = jnp.split(x.astype(jnp.float32), 2, axis=-1)
    return jnp.concatenate([x1 * cos - x2 * sin, x1 * sin + x2 * cos], axis=-1).astype(x.dtype)

def sink_softmax(scores, mask, sink):
    s = jnp.where(mask, scores, NEG_INF)
    m = jnp.maximum(jnp.max(s, axis=-1, keepdims=True), sink)
    p = jnp.exp(s - m)
    den = jnp.sum(p, axis=-1, keepdims=True) + jnp.exp(sink - m)
    return p / den

def even_project(x, pos, w_in):
    B, S, _ = x.shape
    offs = [int(o) for o in np.cumsum(EVEN_SPLITS)[:-1]]
    qa, ka, va, qr, kr, vr, g = jnp.split(x @ w_in, offs, axis=-1)
    qa = rope(qa.reshape(B, S, SWA_HEADS, SWA_HEAD_DIM), pos)
    ka = rope(ka.reshape(B, S, SWA_KV_HEADS, SWA_HEAD_DIM), pos)
    va = va.reshape(B, S, SWA_KV_HEADS, SWA_HEAD_DIM)
    qr = rope(qr.reshape(B, S, RET_HEADS, RET_DK), pos)
    kr = rope(kr.reshape(B, S, RET_HEADS, RET_DK), pos) * (RET_DK ** -0.5)
    vr = vr.reshape(B, S, RET_HEADS, RET_DV)
    return qa, ka, va, qr, kr, vr, g

def swa_prompt(q, k, v, sink):
    B, S, H, Dh = q.shape
    nb = S // WINDOW
    qb = q.reshape(B, nb, WINDOW, SWA_KV_HEADS, SWA_GROUP, Dh)
    kb = k.reshape(B, nb, WINDOW, SWA_KV_HEADS, Dh)
    vb = v.reshape(B, nb, WINDOW, SWA_KV_HEADS, Dh)
    kk = jnp.concatenate([jnp.concatenate([jnp.zeros_like(kb[:, :1]), kb[:, :-1]], axis=1), kb], axis=2)
    vv = jnp.concatenate([jnp.concatenate([jnp.zeros_like(vb[:, :1]), vb[:, :-1]], axis=1), vb], axis=2)
    scores = jnp.einsum('bnqkgd,bnskd->bnkgqs', qb, kk).astype(jnp.float32) * (Dh ** -0.5)
    qi = jnp.arange(WINDOW)[:, None]
    si = jnp.arange(2 * WINDOW)[None, :]
    diff = qi + WINDOW - si
    band = (diff >= 0) & (diff < WINDOW)
    valid = (jnp.arange(nb)[:, None, None] > 0) | (si >= WINDOW)[None]
    mask = (band[None] & valid)[None, :, None, None]
    sk = sink.astype(jnp.float32).reshape(SWA_KV_HEADS, SWA_GROUP)[None, None, :, :, None, None]
    p = sink_softmax(scores, mask, sk)
    o = jnp.einsum('bnkgqs,bnskd->bnqkgd', p.astype(vv.dtype), vv)
    return o.reshape(B, S, H * Dh)

def swa_sample(q, k, v, buf_k, buf_v, sink):
    B, T, H, Dh = q.shape
    kk = jnp.concatenate([buf_k, k], axis=1)
    vv = jnp.concatenate([buf_v, v], axis=1)
    qg = q.reshape(B, T, SWA_KV_HEADS, SWA_GROUP, Dh)
    scores = jnp.einsum('bqkgd,bskd->bkgqs', qg, kk).astype(jnp.float32) * (Dh ** -0.5)
    qpos = PAST_LEN + jnp.arange(T)
    kpos = PAST_LEN - WINDOW + jnp.arange(WINDOW + T)
    diff = qpos[:, None] - kpos[None, :]
    mask = (diff >= 0) & (diff < WINDOW)
    sk = sink.astype(jnp.float32).reshape(SWA_KV_HEADS, SWA_GROUP)[None, :, :, None, None]
    p = sink_softmax(scores, mask, sk)
    o = jnp.einsum('bkgqs,bskd->bqkgd', p.astype(vv.dtype), vv).reshape(B, T, H * Dh)
    return o, kk[:, -WINDOW:], vv[:, -WINDOW:]

def ret_log_gamma():
    return jnp.log1p(-jnp.exp2(-5.0 - jnp.arange(RET_HEADS, dtype=jnp.float32)))

def retention_chunk(q, k, v, s0, log_gamma):
    L = q.shape[1]
    idx = jnp.arange(L, dtype=jnp.float32)
    diff = idx[:, None] - idx[None, :]
    intra = jnp.where(diff[None] >= 0, jnp.exp(jnp.maximum(diff, 0.0)[None] * log_gamma[:, None, None]), 0.0).astype(q.dtype)
    q_decay = jnp.exp((idx[:, None] + 1.0) * log_gamma[None, :]).astype(q.dtype)
    k_decay = jnp.exp((L - 1.0 - idx)[:, None] * log_gamma[None, :]).astype(q.dtype)
    s_decay = jnp.exp(L * log_gamma).astype(q.dtype)
    scores = jnp.einsum('blhd,bshd->bhls', q, k) * intra[None]
    o = jnp.einsum('bhls,bshe->blhe', scores, v) + jnp.einsum('blhd,bhde->blhe', q * q_decay[None, :, :, None], s0)
    s_new = s0 * s_decay[None, :, None, None] + jnp.einsum('bshd,bshe->bhde', k * k_decay[None, :, :, None], v)
    return o, s_new

def retention_prompt(q, k, v, log_gamma):
    B, S, H, dk = q.shape
    dv = v.shape[-1]
    nc = S // RET_CHUNK

    def chunks(a):
        return a.reshape(B, nc, RET_CHUNK, H, a.shape[-1]).transpose(1, 0, 2, 3, 4)

    def step(s, xs):
        qc, kc, vc = xs
        o, s = retention_chunk(qc, kc, vc, s, log_gamma)
        return s, o

    s0 = jnp.zeros((B, H, dk, dv), v.dtype)
    s_fin, o = lax.scan(step, s0, (chunks(q), chunks(k), chunks(v)))
    return o.transpose(1, 0, 2, 3, 4).reshape(B, S, H, dv), s_fin

def even_output(o_swa, o_ret, g, gn_g, gn_b, w_out):
    B, S = o_ret.shape[:2]
    of = o_ret.astype(jnp.float32)
    mu = jnp.mean(of, axis=-1, keepdims=True)
    var = jnp.mean(jnp.square(of - mu), axis=-1, keepdims=True)
    on = ((of - mu) * lax.rsqrt(var + LN_EPS)).reshape(B, S, RET_V_W) * gn_g + gn_b
    gated = (on * jax.nn.silu(g.astype(jnp.float32))).astype(o_swa.dtype)
    return jnp.concatenate([o_swa, gated], axis=-1) @ w_out

def mla_project(x, pos, w_in, q_norm, kv_norm, w_uq, w_uk):
    B, S, _ = x.shape
    cq, ckv, kr = jnp.split(x @ w_in, [MLA_Q_RANK, MLA_Q_RANK + MLA_KV_RANK], axis=-1)
    cq = rms_norm(cq, q_norm)
    ckv = rms_norm(ckv, kv_norm)
    kr = rope(kr[:, :, None, :], pos)[:, :, 0]
    q = (cq @ w_uq).reshape(B, S, MLA_HEADS, MLA_NOPE + MLA_ROPE)
    q_nope, q_rope = jnp.split(q, [MLA_NOPE], axis=-1)
    q_rope = rope(q_rope, pos)
    q_lat = jnp.einsum('bshn,chn->bshc', q_nope, w_uk)
    rows = jnp.concatenate([ckv, kr], axis=-1)
    return q_lat, q_rope, rows

def mla_attend(q_lat, q_rope, rows, mask):
    ckv = rows[..., :MLA_KV_RANK]
    kr = rows[..., MLA_KV_RANK:]
    s = (jnp.einsum('bqhc,bkc->bhqk', q_lat, ckv) + jnp.einsum('bqhr,bkr->bhqk', q_rope, kr)).astype(jnp.float32)
    s = jnp.where(mask, s * ((MLA_NOPE + MLA_ROPE) ** -0.5), NEG_INF)
    p = jax.nn.softmax(s, axis=-1).astype(rows.dtype)
    return jnp.einsum('bhqk,bkc->bqhc', p, ckv)

def mla_prompt(q_lat, q_rope, rows):
    B, S = q_lat.shape[:2]
    nq = S // Q_BLOCK

    def blocks(a):
        return a.reshape(B, nq, Q_BLOCK, a.shape[2], a.shape[3]).transpose(1, 0, 2, 3, 4)

    kpos = jnp.arange(S)

    def one(args):
        qlb, qrb, n = args
        qpos = n * Q_BLOCK + jnp.arange(Q_BLOCK)
        return mla_attend(qlb, qrb, rows, kpos[None, :] <= qpos[:, None])

    ctx = lax.map(one, (blocks(q_lat), blocks(q_rope), jnp.arange(nq)))
    return ctx.transpose(1, 0, 2, 3, 4).reshape(B, S, MLA_HEADS, MLA_KV_RANK)

def mla_sample(q_lat, q_rope, rows_new, pool, page_table):
    Bd, T = q_lat.shape[:2]
    past = pool[page_table].reshape(Bd, -1, pool.shape[-1])
    P = past.shape[1]
    allr = jnp.concatenate([past, rows_new], axis=1)
    mask = jnp.arange(P + T)[None, :] <= P + jnp.arange(T)[:, None]
    return mla_attend(q_lat, q_rope, allr, mask)

def mla_output(ctx, w_uv, w_out):
    B, S = ctx.shape[:2]
    o = jnp.einsum('bqhc,chv->bqhv', ctx, w_uv).reshape(B, S, MLA_HEADS * MLA_V)
    return o @ w_out

def mem_kv(mem, w_k, w_v):
    B, M, _ = mem.shape
    return (mem @ w_k).reshape(B, M, MEM_HEADS, MEM_HEAD_DIM), (mem @ w_v).reshape(B, M, MEM_HEADS, MEM_HEAD_DIM)

def mem_attend(x, mk, mv, w_q, w_o):
    B, S, _ = x.shape
    q = (x @ w_q).reshape(B, S, MEM_HEADS, MEM_HEAD_DIM)
    s = jnp.einsum('bqhd,bkhd->bhqk', q, mk).astype(jnp.float32) * (MEM_HEAD_DIM ** -0.5)
    p = jax.nn.softmax(s, axis=-1).astype(mv.dtype)
    o = jnp.einsum('bhqk,bkhd->bqhd', p, mv).reshape(B, S, MEM_W)
    return o @ w_o

def hier_moe(x, w_group, b_group, w_router, b_router, w_in, w_out):
    shp = x.shape
    t = x.reshape(-1, shp[-1])
    n = t.shape[0]
    g_logit = (t @ w_group + b_group).astype(jnp.float32)
    g_prob = jax.nn.softmax(g_logit, axis=-1)
    g_idx = jnp.argmax(g_logit, axis=-1)
    g_gate = jnp.take_along_axis(g_prob, g_idx[:, None], axis=-1)
    e_logit = (t @ w_router + b_router).astype(jnp.float32).reshape(n, MOE_GROUPS, MOE_PER_GROUP)
    e_logit = jnp.take_along_axis(e_logit, g_idx[:, None, None], axis=1)[:, 0]
    top_p, top_i = lax.top_k(jax.nn.softmax(e_logit, axis=-1), MOE_TOP_K)
    top_p = top_p / jnp.sum(top_p, axis=-1, keepdims=True)
    local = jnp.sum(jax.nn.one_hot(top_i, MOE_PER_GROUP, dtype=jnp.float32) * top_p[..., None], axis=1)
    gates = (jax.nn.one_hot(g_idx, MOE_GROUPS, dtype=jnp.float32)[:, :, None] * local[:, None, :] * g_gate[:, :, None]).reshape(n, MOE_EXPERTS)
    h = jnp.einsum('td,edf->tef', t, w_in)
    a, b = jnp.split(h, 2, axis=-1)
    act = jax.nn.silu(a) * b * gates[..., None].astype(h.dtype)
    return jnp.einsum('tef,efd->td', act, w_out).reshape(shp)

def setup_inputs(seed: int = 0) -> dict:
    key = jax.random.key(seed)
    ks = iter(jax.random.split(key, 48))

    def nrm(shape, scale):
        return jax.random.normal(next(ks), shape, jnp.float32) * scale

    n_pages = PAST_LEN // PAGE_SIZE
    n_used = DEC_BATCH * n_pages
    n_pool = n_used + n_used // 4
    page_table = jax.random.permutation(next(ks), n_pool)[:n_used].reshape(DEC_BATCH, n_pages).astype(jnp.int32)
    return {
        'x_prompt': nrm((BATCH, SEQ, D_MODEL), 1.0),
        'x_sample': nrm((DEC_BATCH, DEC_SEQ, D_MODEL), 1.0),
        'mem_prompt': nrm((BATCH, N_MEM, D_MODEL), 1.0),
        'cache_swa_k': nrm((N_EVEN, DEC_BATCH, WINDOW, SWA_KV_HEADS, SWA_HEAD_DIM), 1.0),
        'cache_swa_v': nrm((N_EVEN, DEC_BATCH, WINDOW, SWA_KV_HEADS, SWA_HEAD_DIM), 1.0),
        'state_ret': nrm((N_EVEN, DEC_BATCH, RET_HEADS, RET_DK, RET_DV), 1.0),
        'cache_mla': nrm((N_ODD, n_pool, PAGE_SIZE, MLA_ROW_W), 1.0),
        'page_table': page_table,
        'cache_mem_k': nrm((DEPTH, DEC_BATCH, N_MEM, MEM_HEADS, MEM_HEAD_DIM), 1.0),
        'cache_mem_v': nrm((DEPTH, DEC_BATCH, N_MEM, MEM_HEADS, MEM_HEAD_DIM), 1.0),
        'w_in_even': nrm((N_EVEN, D_MODEL, EVEN_IN_W), D_MODEL ** -0.5),
        'swa_sink': nrm((N_EVEN, SWA_HEADS), 0.5),
        'ret_gn_g': 1.0 + nrm((N_EVEN, RET_V_W), 0.02),
        'ret_gn_b': nrm((N_EVEN, RET_V_W), 0.02),
        'w_out_even': nrm((N_EVEN, EVEN_OUT_W, D_MODEL), BETA * EVEN_OUT_W ** -0.5),
        'w_in_odd': nrm((N_ODD, D_MODEL, MLA_IN_W), D_MODEL ** -0.5),
        'mla_q_norm': 1.0 + nrm((N_ODD, MLA_Q_RANK), 0.02),
        'mla_kv_norm': 1.0 + nrm((N_ODD, MLA_KV_RANK), 0.02),
        'w_uq': nrm((N_ODD, MLA_Q_RANK, MLA_HEADS * (MLA_NOPE + MLA_ROPE)), MLA_Q_RANK ** -0.5),
        'w_uk': nrm((N_ODD, MLA_KV_RANK, MLA_HEADS, MLA_NOPE), MLA_KV_RANK ** -0.5),
        'w_uv': nrm((N_ODD, MLA_KV_RANK, MLA_HEADS, MLA_V), MLA_KV_RANK ** -0.5),
        'w_out_odd': nrm((N_ODD, MLA_HEADS * MLA_V, D_MODEL), BETA * (MLA_HEADS * MLA_V) ** -0.5),
        'w_mem_q': nrm((DEPTH, D_MODEL, MEM_W), D_MODEL ** -0.5),
        'w_mem_k': nrm((DEPTH, D_MODEL, MEM_W), D_MODEL ** -0.5),
        'w_mem_v': nrm((DEPTH, D_MODEL, MEM_W), D_MODEL ** -0.5),
        'w_mem_o': nrm((DEPTH, MEM_W, D_MODEL), BETA * MEM_W ** -0.5),
        'moe_w_group': nrm((DEPTH, D_MODEL, MOE_GROUPS), D_MODEL ** -0.5),
        'moe_b_group': nrm((DEPTH, MOE_GROUPS), 0.01),
        'moe_w_router': nrm((DEPTH, D_MODEL, MOE_EXPERTS), D_MODEL ** -0.5),
        'moe_b_router': nrm((DEPTH, MOE_EXPERTS), 0.01),
        'moe_w_in': nrm((DEPTH, MOE_EXPERTS, D_MODEL, 2 * D_EXPERT), D_MODEL ** -0.5),
        'moe_w_out': nrm((DEPTH, MOE_EXPERTS, D_EXPERT, D_MODEL), BETA * D_EXPERT ** -0.5),
        'ln_g': 1.0 + nrm((DEPTH, 3, D_MODEL), 0.02),
        'ln_b': nrm((DEPTH, 3, D_MODEL), 0.02),
    }

def reference(x_prompt, x_sample, mem_prompt, cache_swa_k, cache_swa_v, state_ret, cache_mla, page_table,
              cache_mem_k, cache_mem_v, w_in_even, swa_sink, ret_gn_g, ret_gn_b, w_out_even,
              w_in_odd, mla_q_norm, mla_kv_norm, w_uq, w_uk, w_uv, w_out_odd,
              w_mem_q, w_mem_k, w_mem_v, w_mem_o, moe_w_group, moe_b_group, moe_w_router, moe_b_router,
              moe_w_in, moe_w_out, ln_g, ln_b):
    pos_p = jnp.arange(x_prompt.shape[1])
    pos_s = PAST_LEN + jnp.arange(x_sample.shape[1])
    log_gamma = ret_log_gamma()
    xp, xs = x_prompt, x_sample
    swa_k_p, swa_v_p, ret_p, mla_p, mem_k_p, mem_v_p = [], [], [], [], [], []
    swa_k_s, swa_v_s, ret_s, mla_s = [], [], [], []
    for l in range(DEPTH):
        i = l // 2
        if l % 2 == 0:
            qa, ka, va, qr, kr, vr, g = even_project(xp, pos_p, w_in_even[i])
            o_a = swa_prompt(qa, ka, va, swa_sink[i])
            o_r, s_fin = retention_prompt(qr, kr, vr, log_gamma)
            mix_p = even_output(o_a, o_r, g, ret_gn_g[i], ret_gn_b[i], w_out_even[i])
            swa_k_p.append(ka[:, -WINDOW:])
            swa_v_p.append(va[:, -WINDOW:])
            ret_p.append(s_fin)
            qa, ka, va, qr, kr, vr, g = even_project(xs, pos_s, w_in_even[i])
            o_a, kbuf, vbuf = swa_sample(qa, ka, va, cache_swa_k[i], cache_swa_v[i], swa_sink[i])
            o_r, s_new = retention_chunk(qr, kr, vr, state_ret[i], log_gamma)
            mix_s = even_output(o_a, o_r, g, ret_gn_g[i], ret_gn_b[i], w_out_even[i])
            swa_k_s.append(kbuf)
            swa_v_s.append(vbuf)
            ret_s.append(s_new)
        else:
            q_lat, q_rope, rows = mla_project(xp, pos_p, w_in_odd[i], mla_q_norm[i], mla_kv_norm[i], w_uq[i], w_uk[i])
            mix_p = mla_output(mla_prompt(q_lat, q_rope, rows), w_uv[i], w_out_odd[i])
            mla_p.append(rows)
            q_lat, q_rope, rows = mla_project(xs, pos_s, w_in_odd[i], mla_q_norm[i], mla_kv_norm[i], w_uq[i], w_uk[i])
            mix_s = mla_output(mla_sample(q_lat, q_rope, rows, cache_mla[i], page_table), w_uv[i], w_out_odd[i])
            mla_s.append(rows)
        xp = layer_norm(ALPHA * xp + mix_p, ln_g[l, 0], ln_b[l, 0])
        xs = layer_norm(ALPHA * xs + mix_s, ln_g[l, 0], ln_b[l, 0])
        mk, mv = mem_kv(mem_prompt, w_mem_k[l], w_mem_v[l])
        mem_k_p.append(mk)
        mem_v_p.append(mv)
        xp = layer_norm(ALPHA * xp + mem_attend(xp, mk, mv, w_mem_q[l], w_mem_o[l]), ln_g[l, 1], ln_b[l, 1])
        xs = layer_norm(ALPHA * xs + mem_attend(xs, cache_mem_k[l], cache_mem_v[l], w_mem_q[l], w_mem_o[l]), ln_g[l, 1], ln_b[l, 1])
        xp = layer_norm(ALPHA * xp + hier_moe(xp, moe_w_group[l], moe_b_group[l], moe_w_router[l], moe_b_router[l], moe_w_in[l], moe_w_out[l]), ln_g[l, 2], ln_b[l, 2])
        xs = layer_norm(ALPHA * xs + hier_moe(xs, moe_w_group[l], moe_b_group[l], moe_w_router[l], moe_b_router[l], moe_w_in[l], moe_w_out[l]), ln_g[l, 2], ln_b[l, 2])
    return (xp, xs, jnp.stack(swa_k_p), jnp.stack(swa_v_p), jnp.stack(ret_p), jnp.stack(mla_p),
            jnp.stack(mem_k_p), jnp.stack(mem_v_p), jnp.stack(swa_k_s), jnp.stack(swa_v_s),
            jnp.stack(ret_s), jnp.stack(mla_s))


_drawn_inputs = setup_inputs


def setup_inputs(seed=0):
    import zlib

    import numpy as np

    out = dict(_drawn_inputs(seed))
    spreads = {}
    factors = {'cache_mla': 2.723,
     'swa_sink': 8.0,
     'ret_gn_g': 8.0,
     'ret_gn_b': 8.0,
     'mla_q_norm': 8.0,
     'mla_kv_norm': 3.103,
     'moe_b_group': 8.0,
     'moe_b_router': 8.0}
    for name, (base, spread) in spreads.items():
        noise = np.random.default_rng([zlib.crc32(name.encode()), seed]).standard_normal(out[name].shape)
        drawn = base * np.exp(spread * noise) if base else spread * noise
        out[name] = jnp.asarray(drawn.astype(out[name].dtype))
    for name, factor in factors.items():
        out[name] = (out[name] * factor).astype(out[name].dtype)
    return out
```

```python
from contextlib import ExitStack

import numpy as np

import concourse.bass as bass
from concourse import mybir

F32 = mybir.dt.float32
I32 = mybir.dt.int32
ALU = mybir.AluOpType
ACT = mybir.ActivationFunctionType
AX = mybir.AxisListType

P = 128
D = 1024
KD = D // P
SEQ = 512
DB = 8
T = SEQ + DB
HALF = T // 2
NT = 5
ROWS = [128, 128, 128, 128, 8]
PAST = 1024
DEPTH = 2
ALPHA = (2 * DEPTH) ** 0.25
EPS = 1e-5
NEG = -1e30
NE = 16
DE = 256
NPAGE = 8
ROW_W = 160
SLOTS = 5
ARENA = 21600
PIECE = 2048
EIN_W = 2816


def tile_cols(t):
    return slice(t * P, t * P + ROWS[t])


def shape_constants():
    f = np.float32
    pos = np.concatenate([np.arange(SEQ), np.full(DB, PAST)]).astype(f)
    inv64 = (f(10000.0) ** (-np.arange(0, 64, 2, dtype=f) / f(64))).astype(f)
    ang = (pos[None, :] * inv64[:, None]).astype(f)
    cos, sin = np.cos(ang).astype(f), np.sin(ang).astype(f)
    cos_f = np.tile(cos, (4, 1))
    sin_f = np.concatenate([-sin, sin, -sin, sin], 0)
    inv32 = (f(10000.0) ** (-np.arange(0, 32, 2, dtype=f) / f(32))).astype(f)
    ang2 = (pos[:, None] * inv32[None, :]).astype(f)
    c2, s2 = np.cos(ang2).astype(f), np.sin(ang2).astype(f)
    tab = np.zeros((NT * P, 64), f)
    tab[:T] = np.concatenate([c2, c2, -s2, s2], 1)
    rope_t = tab.reshape(NT, P, 64).transpose(1, 0, 2)
    q = np.arange(P)[:, None]
    s = np.arange(2 * P)[None, :]
    band = np.where((q + P - s >= 0) & (q + P - s < P), 0.0, NEG).astype(f)
    h = np.arange(8, dtype=f)
    lg = np.log1p(-np.exp2(f(-5.0) - h)).astype(f)
    by_bank = [0, 2, 4, 6, 1, 3, 5, 7]
    i = np.arange(P, dtype=f)
    diff = i[None, :] - i[:, None]
    decay = np.where(diff[:, None, :] >= 0,
                     np.exp(np.maximum(diff, 0)[:, None, :] * lg[None, :, None]), 0.0) * 0.125
    hp = (2 * np.arange(4)[None, :] + (np.arange(P) // 64)[:, None])
    qdec = np.exp((i[None, None, :] + 1) * lg[hp][:, :, None])
    kdec = np.exp((P - 1 - i)[:, None] * lg[None, :]) * 0.125
    sdec = np.exp(P * lg[hp])
    sdec1 = np.exp(lg[hp])
    bh = np.arange(64) // 8
    newmask = np.where(bh[:, None] == np.arange(8)[None, :], 0.0, NEG)
    vmask = np.eye(8)
    iota4 = np.tile(np.arange(4) - 8.0, (P, 1))
    small = np.zeros((P, 64), f)
    small[:, 0:8] = kdec
    small[:, 8:12] = sdec
    small[:, 12:16] = sdec1
    small[:64, 16:24] = newmask
    small[:8, 24:32] = vmask
    small[:, 32:36] = iota4
    small[:, 36:44] = -0.5
    return {
        "c_ident": np.eye(P, dtype=f),
        "c_cos": cos_f.astype(f), "c_sin": sin_f.astype(f),
        "c_rope": np.ascontiguousarray(rope_t, f),
        "c_band": band,
        "c_decay": np.ascontiguousarray(decay.astype(f)[:, by_bank]), "c_qdec": qdec.astype(f), "c_small": small,
    }


SWA_BLOCKS = [(n, 4 * kv, 4, 128 if n == 0 else 256) for n in range(4) for kv in range(2)]
MEM_BLOCKS = [(n, 0, 4, 256) for n in range(4)]
MLA_BLOCKS = [(n, h, 2, 128 * (n + 1)) for n in range(4) for h in range(0, 8, 2)]
MOE_BLOCKS = [(e, t) for e in range(NE) for t in range(NT)]


def pipelined(first, second, third, n):
    out = [(first, 0)] + ([(first, 1)] if n > 1 else [])
    for i in range(n):
        out.append((second, i))
        if i + 2 < n:
            out.append((first, i + 2))
        out.append((third, i))
    return out


def psum_jobs():
    jobs = []
    jobs += [("xT", -1, t) for t in range(NT)]
    jobs += [("memT", m) for m in range(2)]
    for l in range(DEPTH):
        jobs += [("mkv", l, m) for m in range(2)] + [("mkT", l)]
    jobs += [("qa", j) for j in range(4)] + [("ka", 0), ("ka", 1), ("va",)]
    jobs += [("qr", j) for j in range(4)] + [("kr", j) for j in range(4)]
    jobs += [(w, i, m) for w in ("vr", "g") for i in range(2) for m in range(2)]
    jobs += [("kaTok",)]
    jobs += [("swa" + s, i) for s, i in pipelined("S", "T", "O", len(SWA_BLOCKS))]
    jobs += [("kwT",), ("swS",), ("swR",), ("swT",), ("swO",)]
    for n in range(4):
        jobs += [("retS", n), ("retK", n), ("retO", n), ("retU", n)]
        if n:
            jobs += [("retG", n - 1)]
    jobs += [("skT",), ("retG", 3)] + [("sU", j) for j in range(4)] + [("sO",), ("sOt",), ("retG", 4)]
    for l in range(DEPTH):
        if l == 1:
            jobs += [("ukT",)]
            for t in range(NT):
                jobs += [("oin", t)] + ([("oinT", t - 1)] if t else [])
            jobs += [("oinT", 4)]
            jobs += [("qn", j) for j in range(4)]
            jobs += [("qrope", 0)]
            jobs += [("ql", h) for h in range(8)]
            for t in range(NT):
                jobs += ([("qrope", t)] if t else []) + ([("qrT", t - 1)] if t else [])
            jobs += [("qrT", 4)]
            jobs += [("mla" + s, i) for s, i in pipelined("S", "T", "O", len(MLA_BLOCKS))]
            jobs += [("pkT", 0), ("pkT", 1)]
            for b in range(DB):
                jobs += [("pcT", b)] + ([("pS", b - 1)] if b else [])
            jobs += [("pS", DB - 1), ("pR",), ("pN",), ("pT",), ("pO",)]
            jobs += [("uv", j) for j in range(4)]
        jobs += [("y", 3 * l, t) for t in range(NT)]
        jobs += [("xT", 3 * l, t) for t in range(NT)]
        jobs += [("mq", l, j) for j in range(2)]
        jobs += [("mem" + s, l, i) for s, i in pipelined("S", "T", "O", len(MEM_BLOCKS))]
        for g in range(4):
            jobs += [("kcT", l, g)] + ([("msS", l, g - 1)] if g else [])
        jobs += [("msS", l, 3), ("msR", l), ("msT", l), ("msO", l)]
        jobs += [("y", 3 * l + 1, t) for t in range(NT)]
        jobs += [("xT", 3 * l + 1, t) for t in range(NT)]
        jobs += [("rt", l)]
        jobs += [("moe" + s, l, i) for s, i in pipelined("H", "T", "Y", len(MOE_BLOCKS))]
        if l == 0:
            jobs += [("xT", 2, t) for t in range(NT)]
    return jobs


def decoder_step(nc, io, outs):
    (y_prompt, y_sample, swa_k_p, swa_v_p, ret_p, mla_p, mem_k_p, mem_v_p,
     swa_k_s, swa_v_s, ret_s, mla_s) = outs

    JOBS = psum_jobs()
    J = {key: n for n, key in enumerate(JOBS)}
    assert len(J) == len(JOBS)

    W = []

    def piece(name, src, shape, last):
        W.append((name, src, shape, last))

    for l in range(DEPTH):
        for w in ("k", "v"):
            piece(("m" + w, l), io["w_mem_" + w][l].rearrange("(k p) n -> p k n", p=P), (8, 256), ("mkv", l, 1))
    ein_last = [("qa", 1), ("qa", 3), ("va",), ("qr", 1), ("qr", 3), ("kr", 1), ("kr", 3),
                ("vr", 0, 1), ("vr", 1, 1), ("g", 0, 1), ("g", 1, 1)]
    for i, last in enumerate(ein_last):
        if i == 2:
            piece(("ka",), io["w_ka_twice"].rearrange("(k p) n -> p k n", p=P), (8, 256), ("ka", 1))
            piece(("va",), io["w_in_even"][0, :, 640:768].rearrange("(k p) n -> p k n", p=P), (8, 128), last)
            continue
        piece(("ein", i), io["w_in_even"][0, :, 256 * i:256 * i + 256].rearrange("(k p) n -> p k n", p=P), (8, 256), last)
    for l in range(DEPTH):
        if l == 0:
            for i in range(4):
                piece(("out", l, i), io["w_out_even"][0, 256 * i:256 * i + 256].rearrange("(k p) n -> p k n", p=P),
                      (2, 1024), ("y", 0, 4))
        else:
            piece(("uk",), io["w_uk"][0].rearrange("c h n -> c (h n)"), (512,), ("ukT",))
            for i in range(2):
                piece(("oin", i), io["w_in_odd"][0, 512 * i:512 * i + 512].rearrange("(k p) n -> p k n", p=P),
                      (4, 416), ("oin", 4))
            piece(("uq",), io["w_uq_split"].rearrange("(k p) n -> p k n", p=P), (2, 768), ("qrope", 4))
            piece(("uv",), io["w_uv"][0].rearrange("c h n -> c (h n)"), (512,), ("uv", 3))
            for i in range(2):
                piece(("out", l, i), io["w_out_odd"][0, 256 * i:256 * i + 256].rearrange("(k p) n -> p k n", p=P),
                      (2, 1024), ("y", 3, 4))
        piece(("mq", l), io["w_mem_q"][l].rearrange("(k p) n -> p k n", p=P), (8, 256), ("mq", l, 1))
        piece(("mo", l), io["w_mem_o"][l].rearrange("(k p) n -> p k n", p=P), (2, 1024), ("y", 3 * l + 1, 4))
        for e in range(NE):
            last = NT * e + NT - 1
            for i in range(2):
                piece(("wi", l, e, i), io["moe_w_in"][l, e, 512 * i:512 * i + 512].rearrange("(k p) n -> p k n", p=P),
                      (4, 512), ("moeH", l, last))
            piece(("wo", l, e), io["moe_w_out"][l, e].rearrange("(k p) n -> p k n", p=P), (2, 1024), ("moeY", l, last))
    WI = {w[0]: n for n, w in enumerate(W)}

    with ExitStack() as ctx:
        def sb(name, shape, dt=F32):
            return ctx.enter_context(nc.sbuf_tensor(name, shape, dt))

        def sem(name):
            return ctx.enter_context(nc.semaphore(name))

        PS = ctx.enter_context(nc.psum_tensor("PS", [P, 4, 1024], F32))

        ring = sb("ring", [P, SLOTS, PIECE])
        x = sb("x", [P, NT, D])
        xT = sb("xT", [P, KD, T])
        oT = xT
        ident = sb("ident", [P, P])
        cosf = sb("cosf", [P, T])
        sinf = sb("sinf", [P, T])
        rope_t = sb("rope_t", [P, NT, 64])
        band = sb("band", [P, 256])
        decay = sb("decay", [P, 8, P])
        qdec = sb("qdec", [P, 4, P])
        small = sb("small", [P, 64])
        lnb = sb("lnb", [P, 2, D])
        mkT = sb("mkT", [P, DEPTH, 2, 256])
        mv = sb("mv", [P, DEPTH, 2, 256])
        wr = sb("wr", [P, DEPTH, KD, 20])
        rb = sb("rb", [P, DEPTH, 20])
        ptab = sb("ptab", [1, 64], I32)
        pbuf = sb("pbuf", [P, 2, 1024])
        pT = sb("pT", [P, 2, 1024])
        rowmax = sb("rowmax", [P, 2, 4])
        negmax = sb("negmax", [P, 2, 4])
        rowsum = sb("rowsum", [P, 2, 4])
        sinke = sb("sinke", [P, 2, 4])
        sinkb = sb("sinkb", [P, 8])
        sinkr = sb("sinkr", [64, 1])
        st = sb("st", [P, 32])
        bns = sb("bns", [P, 2, 6])
        mv_t = sb("mv_t", [P, 2, 2])
        rstd = sb("rstd", [P, 2, 1])
        rms = sb("rms", [P, 2, 4])
        arena = sb("arena", [P, ARENA])

        at = [0]

        def part(*dims, at0=None):
            n = int(np.prod(dims))
            o = at[0] if at0 is None else at0
            if at0 is None:
                at[0] += n
                assert at[0] <= ARENA, at[0]
            v = arena[:, o:o + n]
            names = "abcde"[:len(dims)]
            if len(dims) > 1:
                v = v.rearrange("p (" + " ".join(names) + ") -> p " + " ".join(names),
                                **{c: d for c, d in zip(names, dims)})
            return v

        qaT = part(4, T)
        kaD = part(2, T)
        qrT = part(4, T)
        krT = part(4, T)
        v_tok = part(NT, 640)
        g_s = part(NT, 512)
        swap0 = at[0]
        swapb = part(2, T)
        retP = part(8, P, at0=swap0)
        vmk = part(8, P, at0=swap0)
        kd = part(512)
        qd = part(4, P)
        S = part(4, 64)
        o_t = part(2, 512)
        o_u = part(512)
        gng = lnb[:, :, 0:512]
        mk = part(2, 256, at0=at[0])
        Kw = part(8, P)
        Vw = part(8, P)
        ka_tok = part(P)
        ks_tok = part(512)
        sTs = part(64)
        sRs = part(P)
        pTs_sw = part(64)
        soT = part(4, 8)
        qas = part(4, 8)
        Ss = pT[:, :, :].rearrange("p a (b c) -> p (a b c)", b=2).rearrange("p (b j e) -> p b j e", b=8, j=4)
        memT = part(KD, 256, at0=0)
        at[0] = 0
        qmT = part(2, T)
        Kc = part(8, 2, 256)
        Vc = part(8, 2, 256)
        KcT = part(2, 2, 2, 256)
        sTm = part(2, 32)
        sRm = part(256)
        pTm = part(2, 32)
        at[0] = 0
        acc = part(NT, D)
        ex = part(2, 256)
        actb = part(2, 256)
        aTb = part(2, 2, P)
        L = part(NT, 20)
        rA = part(NT, 4)
        rB = part(NT, 4)
        rC = part(NT, 4)
        oh = part(NT, 4)
        oh1 = part(NT, 4)
        oh2 = part(NT, 4)
        el4 = part(NT, 4)
        prod = part(NT, 16)
        gates = part(NT, 16)
        rs = part(12, NT)
        at[0] = 0
        cqn = part(2, 256)
        kr4 = part(2, P)
        cqT = part(2, T)
        rows = part(NT, ROW_W)
        ckvT = part(T)
        krT4 = part(T)
        qn_at = at[0]
        qnT = part(4, T)
        q_lat = part(8, T)
        ctxT = q_lat
        qr_tok = part(2, 256)
        qr_at = at[0]
        qrT2 = part(2, T)
        qrS = part(4, 8, 8)
        qlS = part(8, 8)
        kvg = part(P)
        qg = part(2)
        ukT = part(4, P)
        scratch = part(384)
        tmpm = part(64)
        nat = part(64, P)
        natr = lnb[:, :, :].rearrange("p a n -> p (a n)")
        krp = part(16, P, at0=qn_at)
        sTp = part(8, 64, at0=0)
        srow = part(1032, at0=512)
        pTn = part(64, at0=1544)
        qr_rep = part(8, P, at0=768)
        pTp = part(8, 64, at0=qr_at)
        ckvp = pbuf

        names = ["x_loaded", "mem_loaded", "const_in", "ident_in", "router_in", "sink_in", "gn_in", "cache_in",
                 "state_in", "newk_in", "kc_in", "vc_in", "odd_in", "ptab_in", "pages_in", "ln_in", "stored",
                 "mk_stored", "var_ready", "rstd_ready", "x_ready", "ln_norm", "swapped", "rope_done", "negmax_ready", "probs_ready",
                 "vec_step", "act_step", "pool_step", "g_exp", "qd_ready", "vm_ready", "gated_ready",
                 "row_neg", "row_exp", "row_probs", "router_neg", "router_exp", "moe_exp",
                 "moe_done", "sq_done", "qrS_zero", "oin_ready", "qrtok_ready"]
        s = {n: sem(n) for n in names}
        pair_full = [sem(f"pair_full{i}") for i in range(4)]
        pair_free = [sem(f"pair_free{i}") for i in range(4)]
        slot_landed = [sem(f"slot_landed{i}") for i in range(SLOTS)]
        n_stored = [0]

        def pair(key):
            return PS[:, J[key] % 4, :]

        def full(eng, key):
            n = J[key]
            eng.wait_ge(pair_full[n % 4], n // 4 + 1)

        def free(ins, key):
            ins.then_inc(pair_free[J[key] % 4], 1)

        def taken(eng, key):
            n = J[key]
            eng.wait_ge(pair_free[n % 4], n // 4 + 1)

        def wview(name):
            n = WI[name]
            shape = W[n][2]
            v = ring[:, n % SLOTS, 0:int(np.prod(shape))]
            if len(shape) == 2:
                v = v.rearrange("p (a b) -> p a b", a=shape[0])
            return v

        def landed(eng, name):
            n = WI[name]
            eng.wait_ge(slot_landed[n % SLOTS], 16 * (n // SLOTS + 1))

        def bank_pos(h):
            return 2 * (h % 2) + h // 2

        ATT = [("swa", i, b) for i, b in enumerate(SWA_BLOCKS)]
        ATT += [("mem0", i, b) for i, b in enumerate(MEM_BLOCKS)]
        ATT += [("mla", i, b) for i, b in enumerate(MLA_BLOCKS)]
        ATT += [("mem1", i, b) for i, b in enumerate(MEM_BLOCKS)]
        A0 = {}
        for n, (k, i, b) in enumerate(ATT):
            A0.setdefault(k, n)
        BLOCKS = {"swa": SWA_BLOCKS, "mem0": MEM_BLOCKS, "mem1": MEM_BLOCKS, "mla": MLA_BLOCKS}

        def att_key(kind, step, i):
            return ("mem" + step, int(kind[3]), i) if kind.startswith("mem") else (kind + step, i)

        SCALE = {"swa": 0.125, "mem0": 0.125, "mem1": 0.125, "mla": 96.0 ** -0.5}

        block = ctx.enter_context(nc.Block())

        @block.sync
        def _(sp):
            def load(dst, src, signal):
                sp.dma_start(dst, src).then_inc(s[signal], 16)

            for t in range(NT):
                src = io["x_prompt"][0, t * P:t * P + P] if t < 4 else io["x_sample"].rearrange("b s d -> (b s) d")
                load(x[0:ROWS[t], t, :], src, "x_loaded")
            load(ident[:, :], io["c_ident"], "ident_in")
            load(arena[:, 2048:4096].rearrange("p (a b) -> p a b", a=2),
                 io["mem_prompt"][0].rearrange("(m p) d -> p m d", p=P), "mem_loaded")

            def load_piece(n):
                name, src, shape, last = W[n]
                if n >= SLOTS:
                    full(sp, W[n - SLOTS][3])
                sp.dma_start(wview(name), src).then_inc(slot_landed[n % SLOTS], 16)

            pages_before = WI[("uk",)]
            for n in range(len(W)):
                if n == pages_before:
                    sp.wait_ge(s["ptab_in"], 16)
                    sp.wait_ge(s["moe_done"], 1)
                    for b in range(DB):
                        for pg in range(NPAGE):
                            i = b * NPAGE + pg
                            r = sp.value_load(ptab[0:1, i:i + 1], min_val=0, max_val=79)
                            page = io["cache_mla"][0, bass.ds(r, 1)].rearrange("o p r -> p (o r)")
                            sp.dma_start(nat[:, i, :], page[:, 0:P]).then_inc(s["pages_in"], 16)
                            sp.dma_start(natr[:, 32 * i:32 * i + 32], page[:, P:ROW_W]).then_inc(s["pages_in"], 16)
                load_piece(n)

        @block.gpsimd
        def _(pool):
            step = [0]

            def load(dst, src, signal):
                pool.dma_start(dst, src).then_inc(s[signal], 16)

            def store(dst, src):
                pool.dma_start(dst, src).then_inc(s["stored"], 16)
                n_stored[0] += 1

            def load_ln(i):
                load(lnb[:, 0, :], io["ln_g"][i // 3, i % 3].partition_broadcast(P), "ln_in")
                load(lnb[:, 1, :], io["ln_b"][i // 3, i % 3].partition_broadcast(P), "ln_in")

            n_rstd = [0]

            def power(v):
                n_rstd[0] += 1
                pool.wait_ge(s["var_ready"], n_rstd[0])
                pool.tensor_tensor(v, v, small[0:v.shape[0], 36:36 + v.shape[1]], ALU.pow).then_inc(s["rstd_ready"], 1)

            def norm_gains(i):
                pool.wait_ge(s["ln_in"], 32 * (i + 1))
                power(rstd[0:ROWS[0], 0, 0:1])
                for t in range(NT):
                    if t + 1 < NT:
                        power(rstd[0:ROWS[t + 1], (t + 1) % 2, 0:1])
                    n = NT * i + t
                    r = ROWS[t]
                    pool.wait_ge(s["ln_norm"], n + 1)
                    pool.tensor_tensor(x[0:r, t, :], x[0:r, t, :], lnb[0:r, 0, :], ALU.mult).then_inc(s["pool_step"], 1)
                    step[0] += 1
                    pool.wait_ge(s["pool_step"], step[0])
                    pool.tensor_tensor(x[0:r, t, :], x[0:r, t, :], lnb[0:r, 1, :], ALU.add).then_inc(s["x_ready"], 1)

            load(cosf[:, :], io["c_cos"], "const_in")
            load(sinf[:, :], io["c_sin"], "const_in")
            load(band[:, :], io["c_band"], "const_in")
            load(decay[:, :, :], io["c_decay"], "const_in")
            load(qdec[:, :, :], io["c_qdec"], "const_in")
            load(small[:, :], io["c_small"], "const_in")
            load(rope_t[:, :, :], io["c_rope"], "const_in")
            load(sinkb[:, :], io["sink_by_bank"].partition_broadcast(P), "sink_in")
            load(sinkr[:, :], io["sink_rows"].rearrange("(r o) -> r o", o=1), "sink_in")
            for l in range(DEPTH):
                load(wr[:, l, :, 0:4], io["moe_w_group"][l].rearrange("(k p) n -> p k n", p=P), "router_in")
                load(wr[:, l, :, 4:20], io["moe_w_router"][l].rearrange("(k p) n -> p k n", p=P), "router_in")
                load(rb[:, l, 0:4], io["moe_b_group"][l].partition_broadcast(P), "router_in")
                load(rb[:, l, 4:20], io["moe_b_router"][l].partition_broadcast(P), "router_in")
            load(ptab[:, :], io["page_table"].rearrange("(o b) g -> o (b g)", o=1), "ptab_in")

            for l in range(DEPTH):
                for m in range(2):
                    taken(pool, ("mkv", l, m))
                    store(mem_k_p[l, 0, m * P:m * P + P].rearrange("s h d -> s (h d)"), mk[:, m, :])
                    store(mem_v_p[l, 0, m * P:m * P + P].rearrange("s h d -> s (h d)"), mv[:, l, m, :])
                pool.wait_ge(s["stored"], 16 * n_stored[0])
                pool.nop().then_inc(s["mk_stored"], 1)

            load(gng[:, 0, :], io["ret_gn_g"][0].partition_broadcast(P), "gn_in")
            load(gng[:, 1, :], io["ret_gn_b"][0].partition_broadcast(P), "gn_in")
            full(pool, ("mkT", 1))
            for dst, name in ((Kw, "cache_swa_k"), (Vw, "cache_swa_v")):
                load(dst[0:127, :, :], io[name][0, :, 1:128].rearrange("b s h d -> s b (h d)"), "cache_in")
            taken(pool, ("va",))
            taken(pool, ("kaTok",))
            for b in range(DB):
                load(Kw[127:128, b, :], sRs[b:b + 1, :], "newk_in")
                load(Vw[127:128, b, :], v_tok[b:b + 1, 4, 0:128], "newk_in")
            store(swa_k_p[0, 0].rearrange("s h d -> s (h d)"), ka_tok[:, :])
            store(swa_v_p[0, 0].rearrange("s h d -> s (h d)"), v_tok[:, 3, 0:128])
            pool.wait_ge(s["cache_in"], 32)
            pool.wait_ge(s["newk_in"], 16 * 16)
            for src, dst in ((Kw, swa_k_s), (Vw, swa_v_s)):
                store(dst[0].rearrange("b s h d -> s b (h d)"), src[:, :, :])
            full(pool, ("swO",))
            for par in range(2):
                for b in range(DB):
                    load(Ss[par * 64:par * 64 + 64, b, :, :],
                         io["state_ret"][0, b].rearrange("(j t) k e -> t k j e", t=2)[par], "state_in")
            pool.wait_ge(s["rope_done"], 14)
            pool.wait_ge(s["const_in"], 16 * 7)
            for n in range(1, 4):
                if n > 1:
                    full(pool, ("retO", n - 1))
                pool.tensor_tensor(qd, qrT[:, :, tile_cols(n)], qdec[:, :, :], ALU.mult).then_inc(s["qd_ready"], 1)
                power(st[:, 16:24])
            power(st[:, 16:24])
            full(pool, ("retO", 3))
            for j in range(4):
                if j:
                    full(pool, ("sU", j - 1))
                pool.tensor_tensor(vmk[0:8, :, :], v_tok[0:8, 4, 128 + j * P:256 + j * P].unsqueeze(1).to_broadcast([8, 8, P]),
                                   small[0:8, 24:32].unsqueeze(2).to_broadcast([8, 8, P]), ALU.mult).then_inc(s["vm_ready"], 1)
            power(st[0:8, 16:24])
            taken(pool, ("retU", 3))
            for par in range(2):
                store(ret_p[0, 0].rearrange("(j t) k e -> t k j e", t=2)[par], S[par * 64:par * 64 + 64, :, :])
            taken(pool, ("sU", 3))
            for par in range(2):
                for b in range(DB):
                    store(ret_s[0, b].rearrange("(j t) k e -> t k j e", t=2)[par], Ss[par * 64:par * 64 + 64, b, :, :])
            pool.wait_ge(s["gated_ready"], 5)
            load_ln(0)

            for l in range(DEPTH):
                if l == 1:
                    load(kvg[:, :], io["mla_kv_norm"][0].partition_broadcast(P), "odd_in")
                    pool.dma_start(qg[:, :], io["mla_q_norm"][0].rearrange("(k p) -> p k", p=P),
                                   allow_slow_non_contiguous=True).then_inc(s["odd_in"], 16)
                    for t in range(NT):
                        power(rms[0:ROWS[t], t % 2, 2:4])
                        pool.wait_ge(s["oin_ready"], t + 1)
                        dst = mla_p[0, 0, t * P:t * P + P] if t < 4 else mla_s[0].rearrange("b s r -> (b s) r")
                        store(dst, rows[0:ROWS[t], t, :])
                    full(pool, ("pkT", 1))
                    load_ln(3)
                pool.wait_ge(s["stored"], 16 * n_stored[0])
                norm_gains(3 * l)
                pool.wait_ge(s["x_ready"], NT * (3 * l + 1))
                load_ln(3 * l + 1)
                for b in range(DB):
                    for dst, name, sg in ((Kc, "cache_mem_k", "kc_in"), (Vc, "cache_mem_v", "vc_in")):
                        load(dst[:, b, :, :], io[name][l, b].rearrange("(c p) h d -> p c (h d)", p=P), sg)
                norm_gains(3 * l + 1)
                pool.wait_ge(s["x_ready"], NT * (3 * l + 2))
                load_ln(3 * l + 2)
                norm_gains(3 * l + 2)
                pool.wait_ge(s["x_ready"], NT * (3 * l + 3))
                if l == 0:
                    pool.nop().then_inc(s["moe_done"], 1)
            for t in range(NT):
                dst = y_prompt[0, t * P:t * P + P] if t < 4 else y_sample.rearrange("b s d -> (b s) d")
                store(dst, x[0:ROWS[t], t, :])
            pool.wait_ge(s["stored"], 16 * n_stored[0])

        @block.tensor
        def _(pe):
            def open_(key):
                n = J[key]
                if n >= 4:
                    pe.wait_ge(pair_free[n % 4], n // 4)
                return PS[:, n % 4, :]

            def close(mm, key):
                mm.then_inc(pair_full[J[key] % 4], 1)

            def transpose_x(i):
                for t in range(NT):
                    key = ("xT", i, t)
                    o = open_(key)
                    r = ROWS[t]
                    pe.wait_ge(s["x_loaded"], 16 * NT) if i < 0 else pe.wait_ge(s["x_ready"], NT * i + t + 1)
                    for k in range(KD):
                        mm = pe.transpose(o[:, k * r:k * r + r], x[0:r, t, k * P:k * P + P], ident[0:r, 0:r])
                    close(mm, key)

            def by_feature(key, lhs, rhs, nk, out_rows=slice(0, P), start=True, last=True):
                o = pair(key)
                for k in range(nk):
                    for h in range(2):
                        mm = pe.matmul(o[out_rows, 512 * h:512 * h + HALF], lhs(k), rhs(k)[:, HALF * h:HALF * h + HALF],
                                       start=(k == 0), stop=(k == nk - 1))
                return mm

            def attention(kind, score, apply):
                blocks = BLOCKS[kind]
                base = A0[kind]

                def step_s(i):
                    key = att_key(kind, "S", i)
                    o = open_(key)
                    close(score(i, o, blocks[i]), key)

                def step_t(i):
                    key = att_key(kind, "T", i)
                    o = open_(key)
                    g, w = blocks[i][2:]
                    pe.wait_ge(s["probs_ready"], base + i + 1)
                    b = pbuf[:, (base + i) % 2, :].rearrange("p (g w) -> p g w", g=g)
                    for c in range(w // P):
                        for h in range(g):
                            col = (c * g + h) * P
                            mm = pe.transpose(o[:, col:col + P], b[:, h, c * P:c * P + P], ident[:, :])
                    close(mm, key)

                def step_o(i):
                    key = att_key(kind, "O", i)
                    o = open_(key)
                    taken(pe, att_key(kind, "T", i))
                    g, w = blocks[i][2:]
                    v = pT[:, (base + i) % 2, :].rearrange("p (c g q) -> p c g q", g=g, q=P)
                    close(apply(i, o, blocks[i], v), key)

                steps = {"S": step_s, "T": step_t, "O": step_o}
                for st_, i in pipelined("S", "T", "O", len(blocks)):
                    steps[st_](i)

            pe.wait_ge(s["ident_in"], 16)
            transpose_x(-1)
            mem_tok = arena[:, 2048:4096].rearrange("p (a b) -> p a b", a=2)
            pe.wait_ge(s["mem_loaded"], 16)
            for m in range(2):
                key = ("memT", m)
                o = open_(key)
                for k in range(KD):
                    mm = pe.transpose(o[:, k * P:k * P + P], mem_tok[:, m, k * P:k * P + P], ident[:, :])
                close(mm, key)
            taken(pe, ("memT", 1))
            for l in range(DEPTH):
                for m in range(2):
                    key = ("mkv", l, m)
                    o = open_(key)
                    for c, w in enumerate("kv"):
                        landed(pe, ("m" + w, l))
                        for k in range(KD):
                            mm = pe.matmul(o[:, 512 * c:512 * c + 256], memT[:, k, m * P:m * P + P],
                                           wview(("m" + w, l))[:, k, :], start=(k == 0), stop=(k == KD - 1))
                    close(mm, key)
                key = ("mkT", l)
                o = open_(key)
                taken(pe, ("mkv", l, 1))
                for c in range(2):
                    for m in range(2):
                        mm = pe.transpose(o[:, c * 256 + m * P:c * 256 + m * P + P], mk[:, m, c * P:c * P + P], ident[:, :])
                close(mm, key)

            taken(pe, ("xT", -1, 4))
            xk = lambda k: xT[:, k, :]

            def chunk(key, name, lhs):
                open_(key)
                landed(pe, name)
                close(by_feature(key, lhs, xk, KD), key)

            def plain(name, j):
                w = wview(name)
                return lambda k: w[:, k, j * P:j * P + P]

            def tokens(key, name, tiles, cols):
                o = open_(key)
                landed(pe, name)
                w = wview(name)
                width = cols.stop - cols.start
                for n, t in enumerate(tiles):
                    for k in range(KD):
                        mm = pe.matmul(o[0:ROWS[t], n * width:n * width + width], xT[:, k, tile_cols(t)], w[:, k, cols],
                                       start=(k == 0), stop=(k == KD - 1))
                close(mm, key)

            def chunks(what, i, j):
                name = ("ein", i + j // 2)
                chunk((what, j), name, plain(name, j % 2))

            for j in range(4):
                chunks("qa", 0, j)
            for kv in range(2):
                chunk(("ka", kv), ("ka",), plain(("ka",), kv))
            tokens(("va",), ("va",), range(NT), slice(0, P))
            for what, i in (("qr", 3), ("kr", 5)):
                for j in range(4):
                    chunks(what, i, j)
            for c, what in enumerate(("vr", "g")):
                for i in range(2):
                    name = ("ein", 7 + 2 * c + i)
                    tokens((what, i, 0), name, range(4), slice(0, 256))
                    tokens((what, i, 1), name, range(4, 5), slice(0, 256))

            key = ("kaTok",)
            o = open_(key)
            pe.wait_ge(s["rope_done"], 6)
            for kv in range(2):
                pe.transpose(o[:, 64 * kv:64 * kv + 64], kaD[0:64, kv, 384:512], ident[0:64, 0:64])
                mm = pe.transpose(o[0:8, 128 + 64 * kv:192 + 64 * kv], kaD[0:64, kv, 512:520], ident[0:64, 0:64])
            close(mm, key)
            taken(pe, ("va",))

            def swa_score(i, o, blk):
                n, h0, g, w = blk
                k0 = max(n - 1, 0) * P
                o = o.rearrange("p (g w) -> p g w", g=g)
                for h in (0, 2, 1, 3):
                    b, c = 64 * (h % 2), (h0 + h) // 2
                    mm = pe.matmul(o[:, bank_pos(h), 0:w], qaT[b:b + 64, c, n * P:n * P + P],
                                   kaD[b:b + 64, h0 // 4, k0:k0 + w], start=True, stop=True)
                return mm

            def swa_apply(i, o, blk, v):
                n, h0, g, w = blk
                t0 = max(n - 1, 0)
                for b in range(2):
                    for c in range(w // P):
                        mm = pe.matmul(o[64 * b:64 * b + 64, 0:256], v_tok[:, t0 + c, 16 * h0:16 * h0 + 64],
                                       v[:, c, 2 * b:2 * b + 2, :], start=(c == 0), stop=(c == w // P - 1))
                return mm

            attention("swa", swa_score, swa_apply)

            pe.wait_ge(s["cache_in"], 32)
            pe.wait_ge(s["newk_in"], 16 * 16)
            key = ("kwT",)
            o = open_(key)
            for b in range(DB):
                mm = pe.transpose(o[:, b * P:b * P + P], Kw[:, b, :], ident[:, :])
            close(mm, key)
            key = ("swS",)
            o = open_(key)
            taken(pe, ("kwT",))
            for kv in range(2):
                for b in range(DB):
                    mm = pe.matmul(o[:, 512 * kv + 4 * b:512 * kv + 4 * b + 4], pbuf[64 * kv:64 * kv + 64, 0, b * P:b * P + P],
                                   qas[64 * kv:64 * kv + 64, :, b], start=True, stop=True)
            close(mm, key)
            n_rows = [0]

            def to_rows(key, src, count, chunks):
                o = open_(key)
                for c in range(chunks):
                    mm = pe.transpose(o[0:count, c * P:c * P + P], src[:, c, :], ident[:, :])
                close(mm, key)

            def from_rows(key, src, count, chunks, new=0):
                o = open_(key)
                n_rows[0] += 1
                pe.wait_ge(s["row_probs"], n_rows[0])
                for c in range(chunks):
                    mm = pe.transpose(o[:, c * count:c * count + count], src[0:count, c * P:c * P + P],
                                      ident[0:count, 0:count])
                if new:
                    mm = pe.transpose(o[0:new, 512:512 + count], src[0:count, chunks * P:chunks * P + new],
                                      ident[0:count, 0:count])
                close(mm, key)

            taken(pe, ("swS",))
            to_rows(("swR",), sTs.unsqueeze(1), 64, 1)
            from_rows(("swT",), sRs, 64, 1)
            key = ("swO",)
            o = open_(key)
            taken(pe, ("swT",))
            for kv in range(2):
                for b in range(DB):
                    for h in range(2):
                        c0 = 8 * b + 4 * kv + h
                        mm = pe.matmul(o[64 * h:64 * h + 64, 16 * kv + b:16 * kv + b + 9:8],
                                       Vw[:, b, 64 * kv:64 * kv + 64], pTs_sw[:, c0:c0 + 3:2], start=True, stop=True)
            close(mm, key)

            pe.wait_ge(s["rope_done"], 14)
            taken(pe, ("vr", 1, 1))

            def ret_gated(n):
                key = ("retG", n)
                o = open_(key)
                r = ROWS[n]
                pe.wait_ge(s["gated_ready"], n + 1)
                for j in range(4):
                    mm = pe.transpose(o[:, j * r:j * r + r], o_t[0:r, n % 2, j * P:j * P + P], ident[0:r, 0:r])
                close(mm, key)

            for n in range(4):
                cols = tile_cols(n)
                key = ("retS", n)
                o = open_(key)
                for h in (0, 2, 4, 6, 1, 3, 5, 7):
                    b, c = 64 * (h % 2), h // 2
                    k = 512 * (h % 2) + c * P
                    mm = pe.matmul(o[:, k:k + P], krT[b:b + 64, c, cols], qrT[b:b + 64, c, cols], start=True, stop=True)
                close(mm, key)
                key = ("retK", n)
                o = open_(key)
                for c in range(4):
                    mm = pe.transpose(o[:, c * P:c * P + P], krT[:, c, cols], ident[:, :])
                close(mm, key)
                key = ("retO", n)
                o = open_(key)
                taken(pe, ("retS", n))
                if n:
                    taken(pe, ("retU", n - 1))
                    pe.wait_ge(s["qd_ready"], n)
                for h in (0, 2, 4, 6, 1, 3, 5, 7):
                    b, c = 64 * (h % 2), h // 2
                    k = 512 * (h % 2) + 64 * c
                    mm = pe.matmul(o[:, k:k + 64], retP[:, 4 * (h % 2) + c, :], v_tok[:, n, 128 + 64 * h:192 + 64 * h],
                                   start=True, stop=(n == 0))
                    if n:
                        mm = pe.matmul(o[:, k:k + 64], qd[b:b + 64, c, :], S[b:b + 64, c, :], start=False, stop=True)
                close(mm, key)
                key = ("retU", n)
                o = open_(key)
                taken(pe, ("retK", n))
                for c in range(4):
                    mm = pe.matmul(o[:, c * P:c * P + P], kd[:, c * P:c * P + P], v_tok[:, n, 128 + c * P:256 + c * P],
                                   start=True, stop=True)
                close(mm, key)
                if n:
                    ret_gated(n - 1)

            key = ("skT",)
            o = open_(key)
            for c in range(4):
                mm = pe.transpose(o[0:8, c * P:c * P + P], krT[:, c, 512:520], ident[:, :])
            close(mm, key)
            ret_gated(3)
            taken(pe, ("skT",))
            for j in range(4):
                key = ("sU", j)
                o = open_(key)
                pe.wait_ge(s["vm_ready"], j + 1)
                for h in range(2):
                    mm = pe.matmul(o[:, 512 * h:512 * h + 512], ks_tok[0:8, j * P:j * P + P],
                                   vmk[0:8, 4 * h:4 * h + 4, :], start=True, stop=True)
                close(mm, key)
            key = ("sO",)
            o = open_(key)
            taken(pe, ("sU", 3))
            for b in range(DB):
                for h in range(8):
                    q, c = 64 * (h % 2), h // 2
                    mm = pe.matmul(o[q:q + 64, c * 8 + b:c * 8 + b + 1], Ss[q:q + 64, b, c, :],
                                   qrT[q:q + 64, c, 512 + b:513 + b], start=True, stop=True)
            close(mm, key)
            key = ("sOt",)
            o = open_(key)
            taken(pe, ("sO",))
            for c in range(4):
                mm = pe.transpose(o[0:8, c * P:c * P + P], soT[:, c, :], ident[:, :])
            close(mm, key)
            ret_gated(4)

            def out_proj(i, pieces, last):
                taken(pe, last)
                for t in range(NT):
                    key = ("y", i, t)
                    o = open_(key)
                    for h in range(2):
                        for n, name in enumerate(pieces):
                            landed(pe, name)
                            w = wview(name)
                            for k in range(2):
                                mm = pe.matmul(o[0:ROWS[t], 512 * h:512 * h + 512], oT[:, 2 * n + k, tile_cols(t)],
                                               w[:, k, 512 * h:512 * h + 512], start=(n == 0 and k == 0),
                                               stop=(n == len(pieces) - 1 and k == 1))
                    close(mm, key)

            def cross_attention(l):
                taken(pe, ("xT", 3 * l, 4))
                for j in range(2):
                    key = ("mq", l, j)
                    open_(key)
                    landed(pe, ("mq", l))
                    w = wview(("mq", l))
                    close(by_feature(key, lambda k: w[:, k, j * P:j * P + P], xk, KD), key)
                taken(pe, ("mq", l, 1))

                def score(i, o, blk):
                    n = blk[0]
                    for h in (0, 2, 1, 3):
                        b, c = 64 * (h % 2), h // 2
                        k = 256 * bank_pos(h)
                        mm = pe.matmul(o[:, k:k + 256], qmT[b:b + 64, c, n * P:n * P + P],
                                       mkT[b:b + 64, l, c, :], start=True, stop=True)
                    return mm

                def apply(i, o, blk, v):
                    for h in range(4):
                        for c in range(2):
                            mm = pe.matmul(o[64 * (h % 2):64 * (h % 2) + 64, (h // 2) * P:(h // 2) * P + P],
                                           mv[:, l, c, 64 * h:64 * h + 64], v[:, c, bank_pos(h), :], start=(c == 0), stop=(c == 1))
                    return mm

                attention(f"mem{l}", score, apply)

                def sample_scores(g):
                    key = ("msS", l, g)
                    o = open_(key)
                    taken(pe, ("kcT", l, g))
                    for bb in range(2):
                        for c in range(2):
                            for h in range(4):
                                q, hc = 64 * (h % 2), h // 2
                                col = 512 * (h % 2) + c * 4 + bb * 2 + hc
                                mm = pe.matmul(o[:, col:col + 1], KcT[q:q + 64, g % 2, bb, hc, c * P:c * P + P],
                                               qmT[q:q + 64, hc, 512 + 2 * g + bb:513 + 2 * g + bb], start=True, stop=True)
                    close(mm, key)

                pe.wait_ge(s["kc_in"], 16 * DB * (l + 1))
                for g in range(4):
                    key = ("kcT", l, g)
                    o = open_(key)
                    for bb in range(2):
                        for hc in range(2):
                            for c in range(2):
                                col = bb * 512 + hc * 256 + c * P
                                mm = pe.transpose(o[:, col:col + P], Kc[:, 2 * g + bb, c, hc * P:hc * P + P], ident[:, :])
                    close(mm, key)
                    if g:
                        sample_scores(g - 1)
                sample_scores(3)
                taken(pe, ("msS", l, 3))
                to_rows(("msR", l), sTm, 32, 2)
                from_rows(("msT", l), sRm, 32, 2)
                key = ("msO", l)
                o = open_(key)
                taken(pe, ("msT", l))
                pe.wait_ge(s["vc_in"], 16 * DB * (l + 1))
                for b in range(DB):
                    for h in range(4):
                        for c in range(2):
                            mm = pe.matmul(o[64 * (h % 2):64 * (h % 2) + 64, 8 * (h // 2) + b:8 * (h // 2) + b + 1],
                                           Vc[:, b, c, 64 * h:64 * h + 64], pTm[:, c, 4 * b + h:4 * b + h + 1],
                                           start=(c == 0), stop=(c == 1))
                close(mm, key)
                out_proj(3 * l + 1, [("mo", l)], ("msO", l))

            def experts(l):
                key = ("rt", l)
                o = open_(key)
                taken(pe, ("xT", 3 * l + 1, 4))
                pe.wait_ge(s["router_in"], 16 * 8)
                for t in range(NT):
                    for k in range(KD):
                        mm = pe.matmul(o[0:ROWS[t], t * 32:t * 32 + 20], xT[:, k, tile_cols(t)], wr[:, l, k, :],
                                       start=(k == 0), stop=(k == KD - 1))
                close(mm, key)
                base = l * len(MOE_BLOCKS)

                def step_h(i):
                    e, t = MOE_BLOCKS[i]
                    key = ("moeH", l, i)
                    o = open_(key)
                    for c in range(2):
                        landed(pe, ("wi", l, e, c))
                        w = wview(("wi", l, e, c))
                        for k in range(4):
                            mm = pe.matmul(o[0:ROWS[t], 0:512], xT[:, 4 * c + k, tile_cols(t)], w[:, k, :],
                                           start=(c == 0 and k == 0), stop=(c == 1 and k == 3))
                    close(mm, key)

                def step_t(i):
                    e, t = MOE_BLOCKS[i]
                    r = ROWS[t]
                    key = ("moeT", l, i)
                    o = open_(key)
                    taken(pe, ("moeH", l, i))
                    for c in range(2):
                        mm = pe.transpose(o[:, c * P:c * P + r], actb[0:r, i % 2, c * P:c * P + P], ident[0:r, 0:r])
                    close(mm, key)

                def step_y(i):
                    e, t = MOE_BLOCKS[i]
                    r = ROWS[t]
                    key = ("moeY", l, i)
                    o = open_(key)
                    landed(pe, ("wo", l, e))
                    w = wview(("wo", l, e))
                    taken(pe, ("moeT", l, i))
                    for h in range(2):
                        for c in range(2):
                            mm = pe.matmul(o[0:r, 512 * h:512 * h + 512], aTb[:, i % 2, c, 0:r], w[:, c, 512 * h:512 * h + 512],
                                           start=(c == 0), stop=(c == 1))
                    close(mm, key)

                steps = {"H": step_h, "T": step_t, "Y": step_y}
                for st_, i in pipelined("H", "T", "Y", len(MOE_BLOCKS)):
                    steps[st_](i)

            def latent_attention():
                taken(pe, ("xT", 2, 4))
                key = ("ukT",)
                o = open_(key)
                landed(pe, ("uk",))
                for c in range(4):
                    mm = pe.transpose(o[:, c * P:c * P + P], wview(("uk",))[:, c * P:c * P + P], ident[:, :])
                close(mm, key)

                def oin_back(t):
                    key = ("oinT", t)
                    o = open_(key)
                    r = ROWS[t]
                    pe.wait_ge(s["oin_ready"], t + 1)
                    for c, src in enumerate((cqn[0:r, t % 2, 0:P], cqn[0:r, t % 2, P:2 * P], rows[0:r, t, 0:P], kr4[0:r, t % 2, :])):
                        mm = pe.transpose(o[:, c * P:c * P + r], src, ident[0:r, 0:r])
                    close(mm, key)

                for t in range(NT):
                    key = ("oin", t)
                    o = open_(key)
                    for c in range(2):
                        landed(pe, ("oin", c))
                        for k in range(4):
                            mm = pe.matmul(o[0:ROWS[t], 0:416], xT[:, 4 * c + k, tile_cols(t)], wview(("oin", c))[:, k, :],
                                           start=(c == 0 and k == 0), stop=(c == 1 and k == 3))
                    close(mm, key)
                    if t:
                        oin_back(t - 1)
                oin_back(4)
                taken(pe, ("oinT", 4))
                landed(pe, ("uq",))
                uq = wview(("uq",))
                cqk = lambda k: cqT[:, k, :]
                for j in range(4):
                    key = ("qn", j)
                    open_(key)
                    close(by_feature(key, lambda k: uq[:, k, j * P:j * P + P], cqk, 2), key)

                def q_rope(t):
                    key = ("qrope", t)
                    o = open_(key)
                    for k in range(2):
                        mm = pe.matmul(o[0:ROWS[t], 0:256], cqT[:, k, tile_cols(t)], uq[:, k, 512:768],
                                       start=(k == 0), stop=(k == 1))
                    close(mm, key)

                def q_rope_back(t):
                    key = ("qrT", t)
                    o = open_(key)
                    pe.wait_ge(s["qrtok_ready"], t + 1)
                    if t < 4:
                        for c in range(2):
                            mm = pe.transpose(o[:, c * P:c * P + P], qr_tok[:, t % 2, c * P:c * P + P], ident[:, :])
                    else:
                        for h in range(8):
                            mm = pe.transpose(o[:, 8 * h:8 * h + 8], qr_rep[0:8, h, :], ident[0:8, 0:8])
                    close(mm, key)

                q_rope(0)
                taken(pe, ("ukT",))
                taken(pe, ("qn", 2))
                taken(pe, ("qn", 3))
                for h in range(8):
                    key = ("ql", h)
                    open_(key)
                    b, c = 64 * (h % 2), h // 2
                    close(by_feature(key, lambda k: ukT[b:b + 64, c, :], lambda k: qnT[b:b + 64, c, :], 1), key)
                for t in range(1, NT):
                    q_rope(t)
                    q_rope_back(t - 1)
                q_rope_back(4)
                taken(pe, ("qrT", 4))
                taken(pe, ("ql", 6))
                taken(pe, ("ql", 7))

                def score(i, o, blk):
                    n, h0, g, w = blk
                    o = o.rearrange("p (g w) -> p g w", g=g)
                    for h in range(h0, h0 + g):
                        b, c = 32 * (h % 4), h // 4
                        pe.matmul(o[:, h - h0, 0:w], q_lat[:, h, n * P:n * P + P], ckvT[:, 0:w], start=True, stop=False)
                        mm = pe.matmul(o[:, h - h0, 0:w], qrT2[b:b + 32, c, n * P:n * P + P], krT4[b:b + 32, 0:w],
                                       start=False, stop=True, **({"tile_position": (b, 0)} if b == 96 else {}))
                    return mm

                def apply(i, o, blk, v):
                    n, h0, g, w = blk
                    for c in range(n + 1):
                        mm = pe.matmul(o[:, 0:g * P], rows[:, c, 0:P], v[:, c, :, :], start=(c == 0), stop=(c == n))
                    return mm

                attention("mla", score, apply)

                pe.wait_ge(s["pages_in"], 16 * 128)
                for g in range(2):
                    key = ("pkT", g)
                    o = open_(key)
                    for c in range(8):
                        mm = pe.transpose(o[:, c * P:c * P + P], natr[:, (8 * g + c) * P:(8 * g + c + 1) * P], ident[:, :])
                    close(mm, key)

                def sample_scores(b):
                    key = ("pS", b)
                    o = open_(key)
                    taken(pe, ("pcT", b))
                    taken(pe, ("pkT", 1))
                    for pg in range(NPAGE):
                        pe.matmul(o[:, 8 * pg:8 * pg + 8], ckvp[:, b % 2, pg * P:pg * P + P], qlS[:, b, :],
                                  start=True, stop=False)
                        mm = pe.matmul(o[:, 8 * pg:8 * pg + 8], krp[:, 2 * b + pg // 4, :], qrS[:, pg % 4, b, :],
                                       start=False, stop=True)
                    close(mm, key)

                for b in range(DB):
                    key = ("pcT", b)
                    o = open_(key)
                    for pg in range(NPAGE):
                        mm = pe.transpose(o[:, pg * P:pg * P + P], nat[:, 8 * b + pg, 0:P], ident[:, :])
                    close(mm, key)
                    if b:
                        sample_scores(b - 1)
                sample_scores(7)
                taken(pe, ("pS", 7))
                to_rows(("pR",), sTp, 64, 8)
                key = ("pN",)
                o = open_(key)
                pe.matmul(o[0:64, 0:8], qlS.rearrange("p b h -> p (b h)"), ckvT[:, 512:520], start=True, stop=False)
                mm = pe.matmul(o[0:64, 0:8], qrS[0:32, 0, :, :].rearrange("p b h -> p (b h)"), krT4[0:32, 512:520], start=False, stop=True)
                close(mm, key)
                from_rows(("pT",), srow, 64, 8, new=8)
                key = ("pO",)
                o = open_(key)
                taken(pe, ("pT",))
                pe.matmul(o[:, 0:64], rows[0:8, 4, 0:P], pTn[0:8, :], start=True, stop=False, skip_group_check=True)
                for b in range(DB):
                    for pg in range(NPAGE):
                        mm = pe.matmul(o[:, 8 * b:8 * b + 8], nat[:, 8 * b + pg, 0:P], pTp[:, pg, 8 * b:8 * b + 8],
                                       start=False, stop=(b == DB - 1 and pg == NPAGE - 1), skip_group_check=True)
                close(mm, key)
                taken(pe, ("pO",))
                landed(pe, ("uv",))
                for j in range(4):
                    key = ("uv", j)
                    open_(key)
                    for q in range(2):
                        h = 2 * j + q
                        mm = by_feature(key, lambda k: wview(("uv",))[:, 64 * h:64 * h + 64], lambda k: ctxT[:, h, :], 1,
                                        out_rows=slice(64 * q, 64 * q + 64))
                    close(mm, key)

            out_proj(0, [("out", 0, i) for i in range(4)], ("retG", 4))
            transpose_x(0)
            cross_attention(0)
            transpose_x(1)
            experts(0)
            transpose_x(2)
            latent_attention()
            out_proj(3, [("out", 1, i) for i in range(2)], ("uv", 3))
            transpose_x(3)
            cross_attention(1)
            transpose_x(4)
            experts(1)

        CHUNKS = [(("qa", j), qaT[:, j, :]) for j in range(4)] + [(("ka", j), kaD[:, j, :]) for j in range(2)]
        CHUNKS += [(("qr", j), qrT[:, j, :]) for j in range(4)] + [(("kr", j), krT[:, j, :]) for j in range(4)]

        def halves(ap):
            if ap.shape[1] == 1024:
                return ap.rearrange("p (a b) -> p a b", a=2)[:, :, 0:HALF]
            return ap.rearrange("p (a b) -> p a b", a=2)

        def score_view(kind, i):
            g, w = BLOCKS[kind][i][2:]
            return pair(att_key(kind, "S", i)).rearrange("p (g w) -> p g w", g=g)[:, :, 0:w]

        def prob_view(kind, i):
            g, w = BLOCKS[kind][i][2:]
            return pbuf[:, (A0[kind] + i) % 2, :].rearrange("p (g w) -> p g w", g=g)[:, :, 0:w]

        def gate_views(i, m):
            o = pair(("g", i, m))
            if m == 0:
                return g_s[:, 0:4, 256 * i:256 * i + 256], o.rearrange("p (t n) -> p t n", t=4)
            return g_s[0:8, 4, 256 * i:256 * i + 256], o[0:8, 0:256]

        @block.scalar
        def _(act):
            def copy(dst, src):
                return act.activation(dst, src, ACT.Copy)

            def take(key, dst, src):
                full(act, key)
                free(copy(dst, src(pair(key)) if callable(src) else src), key)

            def take_xT(i):
                for t in range(NT):
                    r = ROWS[t]
                    take(("xT", i, t), xT[:, :, tile_cols(t)], lambda o: o[:, 0:KD * r].rearrange("p (k q) -> p k q", k=KD))

            take_xT(-1)
            for m in range(2):
                take(("memT", m), memT[:, :, m * P:m * P + P], lambda o: o.rearrange("p (k q) -> p k q", k=KD))
            for l in range(DEPTH):
                if l:
                    act.wait_ge(s["mk_stored"], 1)
                for m in range(2):
                    key = ("mkv", l, m)
                    full(act, key)
                    copy(mk[:, m, :], pair(key)[:, 0:256])
                    free(copy(mv[:, l, m, :], pair(key)[:, 512:768]), key)
                take(("mkT", l), mkT[:, l, :, :], lambda o: o[:, 0:512].rearrange("p (c q) -> p c q", c=2))

            def swap(i):
                key = CHUNKS[i][0]
                full(act, key)
                if i >= 2:
                    act.wait_ge(s["rope_done"], i - 1)
                for q in range(4):
                    a, b = 32 * q, 32 * (q ^ 1)
                    ins = copy(halves(swapb[a:a + 32, i % 2, :]), halves(pair(key)[b:b + 32, :]))
                ins.then_inc(s["swapped"], 1)

            for i in range(6):
                swap(i)
            key = ("va",)
            full(act, key)
            copy(v_tok[:, 0:4, 0:P], pair(key)[:, 0:512].rearrange("p (t n) -> p t n", t=4))
            free(copy(v_tok[0:8, 4, 0:P], pair(key)[0:8, 512:640]), key)
            for i in range(6, 14):
                swap(i)
            for i in range(2):
                take(("vr", i, 0), v_tok[:, 0:4, P + 256 * i:P + 256 * i + 256], lambda o: o.rearrange("p (t n) -> p t n", t=4))
                take(("vr", i, 1), v_tok[0:8, 4, P + 256 * i:P + 256 * i + 256], lambda o: o[0:8, 0:256])
            for i in range(2):
                for m in range(2):
                    key = ("g", i, m)
                    full(act, key)
                    g, o = gate_views(i, m)
                    act.activation(g, o, ACT.Exp, scale=-1.0).then_inc(s["g_exp"], 1)

            key = ("kaTok",)
            full(act, key)
            copy(ka_tok[:, :], pair(key)[:, 0:P])
            free(copy(sRs[0:8, :], pair(key)[0:8, P:2 * P]), key)

            def attention(kind):
                base = A0[kind]
                blocks = BLOCKS[kind]

                def exps(i):
                    n = base + i
                    g = blocks[i][2]
                    act.wait_ge(s["negmax_ready"], n + 1)
                    if kind == "swa":
                        act.activation(sinke[:, n % 2, :], sinke[:, n % 2, :], ACT.Exp)
                    for h in range(g):
                        ins = act.activation(prob_view(kind, i)[:, h, :], score_view(kind, i)[:, h, :], ACT.Exp,
                                             bias=negmax[:, n % 2, h:h + 1], scale=SCALE[kind],
                                             accum_out=rowsum[:, n % 2, h:h + 1])
                    free(ins, att_key(kind, "S", i))

                def outputs(i):
                    n, h0, g, w = blocks[i]
                    cols = g * w
                    take(att_key(kind, "T", i), pT[:, (base + i) % 2, 0:cols], lambda o: o[:, 0:cols])
                    if kind == "mla":
                        take(att_key(kind, "O", i), ctxT[:, h0:h0 + g, tile_cols(n)],
                             lambda o: o[:, 0:g * P].rearrange("p (g q) -> p g q", g=g))
                    else:
                        take(att_key(kind, "O", i), oT[:, h0 // 2:h0 // 2 + 2, tile_cols(n)],
                             lambda o: o[:, 0:256].rearrange("p (c q) -> p c q", c=2))

                exps(0)
                for i in range(len(blocks)):
                    if i + 1 < len(blocks):
                        exps(i + 1)
                    outputs(i)

            n_rows = [0]

            def row_exps(dst, count, w, scale, sink):
                n_rows[0] += 1
                act.wait_ge(s["row_neg"], n_rows[0])
                if sink:
                    act.activation(st[0:count, 27:28], st[0:count, 27:28], ACT.Exp)
                act.activation(dst[0:count, 0:w], dst[0:count, 0:w], ACT.Exp, bias=st[0:count, 26:27], scale=scale,
                               accum_out=st[0:count, 28:29]).then_inc(s["row_exp"], 1)

            attention("swa")
            for kv in range(2):
                for h in range(2):
                    copy(qas[64 * kv:64 * kv + 64, h::2, :], qaT[64 * h:64 * h + 64, 2 * kv:2 * kv + 2, 512:520])
            take(("kwT",), pbuf[:, 0, :], lambda o: o)
            take(("swS",), sTs.rearrange("p (b k h) -> p k b h", b=8, k=2),
                 lambda o: o.rearrange("p (k n) -> p k n", k=2)[:, :, 0:32].rearrange("p k (b h) -> p k b h", b=8))
            row_exps(sRs, 64, P, 0.125, True)
            take(("swT",), pTs_sw, lambda o: o[:, 0:64])
            take(("swO",), oT[:, 0:4, 512:520], lambda o: o[:, 0:32].rearrange("p (c b) -> p c b", c=4))

            def take_gated(n):
                r = ROWS[n]
                take(("retG", n), oT[:, 4:8, tile_cols(n)], lambda o: o[:, 0:4 * r].rearrange("p (c q) -> p c q", c=4))

            for n in range(3):
                take_gated(n)
            full(act, ("skT",))
            free(act.activation(ks_tok[0:8, :], pair(("skT",))[0:8, 0:512], ACT.Copy, scale=0.125), ("skT",))
            take_gated(3)
            take(("sO",), soT, lambda o: o[:, 0:32].rearrange("p (c b) -> p c b", c=4))
            take_gated(4)

            def cross_attention(l):
                for j in range(2):
                    take(("mq", l, j), halves(qmT[:, j, :]), halves)
                attention(f"mem{l}")

                def take_scores(g):
                    key = ("msS", l, g)
                    full(act, key)
                    for q in range(2):
                        dst = sTm[:, :, 8 * g:8 * g + 8].rearrange("p c (b x q) -> p q c b x", b=2, q=2)[:, q]
                        ins = copy(dst, pair(key)[:, 512 * q:512 * q + 8].rearrange("p (c b x) -> p c b x", c=2, b=2))
                    free(ins, key)

                for g in range(4):
                    take(("kcT", l, g), KcT[:, g % 2, :, :, :], lambda o: o.rearrange("p (a b c) -> p a b c", a=2, b=2))
                    if g:
                        take_scores(g - 1)
                take_scores(3)
                row_exps(sRm, 32, 256, 0.125, False)
                take(("msT", l), pTm, lambda o: o[:, 0:64].rearrange("p (c r) -> p c r", c=2))
                take(("msO", l), oT[:, 0:2, 512:520], lambda o: o[:, 0:16].rearrange("p (c b) -> p c b", c=2))

            def experts(l):
                base = l * len(MOE_BLOCKS)
                for n in range(2):
                    act.wait_ge(s["router_neg"], 2 * l + n + 1)
                    v = (rA, rs[:, 5:6, :])[n]
                    act.activation(v, v, ACT.Exp).then_inc(s["router_exp"], 1)

                def exps(i):
                    e, t = MOE_BLOCKS[i]
                    key = ("moeH", l, i)
                    full(act, key)
                    if i >= 2:
                        taken(act, ("moeH", l, i - 2))
                    act.activation(ex[0:ROWS[t], i % 2, :], pair(key)[0:ROWS[t], 0:DE], ACT.Exp, scale=-1.0
                                   ).then_inc(s["moe_exp"], 1)

                exps(0)
                for i, (e, t) in enumerate(MOE_BLOCKS):
                    if i + 1 < len(MOE_BLOCKS):
                        exps(i + 1)
                    if i >= 2:
                        full(act, ("moeY", l, i - 2))
                    r = ROWS[t]
                    take(("moeT", l, i), aTb[:, i % 2, :, 0:r], lambda o: o[:, 0:256].rearrange("p (c q) -> p c q", c=2)[:, :, 0:r])

            def latent_attention():
                take(("ukT",), ukT, lambda o: o[:, 0:512].rearrange("p (c q) -> p c q", c=4))
                act.wait_ge(s["odd_in"], 32)

                def back(t):
                    key = ("oinT", t)
                    full(act, key)
                    o = pair(key)
                    r = ROWS[t]
                    for c in range(2):
                        act.activation(cqT[:, c, tile_cols(t)], o[:, c * P:c * P + r], ACT.Copy, scale=qg[:, c:c + 1])
                    copy(ckvT[:, tile_cols(t)], o[:, 2 * P:2 * P + r])
                    free(copy(krT4[:, tile_cols(t)], o[:, 3 * P:3 * P + r]), key)

                for t in range(NT):
                    key = ("oin", t)
                    r = ROWS[t]
                    full(act, key)
                    if t:
                        act.wait_ge(s["sq_done"], t)
                    act.activation(scratch[0:r, 0:256], pair(key)[0:r, 0:256], ACT.Square, accum_out=rms[0:r, t % 2, 0:1])
                    act.activation(scratch[0:r, 256:384], pair(key)[0:r, 256:384], ACT.Square,
                                   accum_out=rms[0:r, t % 2, 1:2]).then_inc(s["sq_done"], 1)
                    if t:
                        back(t - 1)
                back(4)
                for j in (1, 3):
                    take(("qn", j), halves(qnT[:, j, :]), halves)
                for h in (1, 3, 5, 7):
                    take(("ql", h), halves(q_lat[:, h, :]), halves)
                for t in range(4):
                    take(("qrT", t), qrT2[:, :, tile_cols(t)], lambda o: o[:, 0:256].rearrange("p (c q) -> p c q", c=2))
                taken(act, ("ql", 6))
                taken(act, ("ql", 7))
                copy(qlS, q_lat[:, :, 512:520].rearrange("p h b -> p b h"))
                full(act, ("qrT", 4))
                act.wait_ge(s["qrS_zero"], 1)
                for q in range(4):
                    ins = copy(qrS[32 * q:32 * q + 32, q, :, :], pair(("qrT", 4))[32 * q:32 * q + 32, 0:64].rearrange("p (h b) -> p b h", h=8))
                free(ins, ("qrT", 4))
                attention("mla")
                for g in range(2):
                    take(("pkT", g), krp[:, 8 * g:8 * g + 8, :], lambda o: o.rearrange("p (c q) -> p c q", c=8))

                def take_scores(b):
                    take(("pS", b), sTp[:, :, 8 * b:8 * b + 8], lambda o: o[:, 0:64].rearrange("p (g h) -> p g h", g=8))

                for b in range(DB):
                    if b % 2:
                        take(("pcT", b), ckvp[:, b % 2, :], lambda o: o)
                    if b:
                        take_scores(b - 1)
                take_scores(7)
                row_exps(srow, 64, 1032, SCALE["mla"], False)
                full(act, ("pT",))
                copy(pTn[0:8, :], pair(("pT",))[0:8, 512:576])
                take(("pT",), pTp, lambda o: o[:, 0:512].rearrange("p (g r) -> p g r", g=8))
                take(("pO",), ctxT[:, :, 512:520].rearrange("p h b -> p b h"), lambda o: o[:, 0:64].rearrange("p (b h) -> p b h", b=8))
                for j in range(4):
                    take(("uv", j), halves(oT[:, j, :]), halves)

            take_xT(0)
            cross_attention(0)
            take_xT(1)
            experts(0)
            take_xT(2)
            latent_attention()
            take_xT(3)
            cross_attention(1)
            take_xT(4)
            experts(1)

        @block.vector
        def _(dve):
            steps = [0]

            def link(ins):
                ins.then_inc(s["vec_step"], 1)
                steps[0] += 1
                dve.wait_ge(s["vec_step"], steps[0])

            dve.wait_ge(s["const_in"], 16 * 7)
            for i, (key, dst) in enumerate(CHUNKS):
                if i == 6:
                    pass
                full(dve, key)
                dve.wait_ge(s["swapped"], i + 1)
                d = halves(dst)
                free(dve.tensor_tensor(d, halves(pair(key)), halves(cosf[:, :]), ALU.mult), key)
                link(dve.tensor_tensor(swapb[:, i % 2, :], swapb[:, i % 2, :], sinf[:, :], ALU.mult))
                dve.tensor_tensor(dst, dst, swapb[:, i % 2, :], ALU.add).then_inc(s["rope_done"], 1)
            for i in range(2):
                for m in range(2):
                    g, o = gate_views(i, m)
                    dve.wait_ge(s["g_exp"], 2 * i + m + 1)
                    link(dve.tensor_scalar(g, g, 1.0, None, ALU.add))
                    link(dve.reciprocal(g, g))
                    free(dve.tensor_tensor(g, o, g, ALU.mult), ("g", i, m))

            def attention(kind):
                base = A0[kind]
                blocks = BLOCKS[kind]

                def maxima(i):
                    n = base + i
                    m = n % 2
                    t, h0, g, w = blocks[i]
                    full(dve, att_key(kind, "S", i))
                    v = score_view(kind, i)
                    if kind == "swa":
                        link(dve.tensor_tensor(v, v, band[:, 256 - w:256].unsqueeze(1).to_broadcast([P, g, w]), ALU.add))
                    if kind == "mla":
                        d = v[:, :, w - P:w]
                        link(dve.tensor_tensor(d, d, band[:, P:256].unsqueeze(1).to_broadcast([P, g, P]), ALU.add))
                    link(dve.tensor_reduce(rowmax[:, m, 0:g], v, AX.X, ALU.max))
                    if kind == "swa":
                        sk = sinkb[:, h0:h0 + g]
                        link(dve.scalar_tensor_tensor(rowmax[:, m, 0:g], rowmax[:, m, 0:g], SCALE[kind], sk, ALU.mult, ALU.max))
                        dve.tensor_scalar(negmax[:, m, 0:g], rowmax[:, m, 0:g], -1.0, None, ALU.mult)
                        dve.tensor_tensor(sinke[:, m, 0:g], sk, rowmax[:, m, 0:g], ALU.subtract).then_inc(s["negmax_ready"], 1)
                    else:
                        dve.tensor_scalar(negmax[:, m, 0:g], rowmax[:, m, 0:g], -SCALE[kind], None, ALU.mult
                                          ).then_inc(s["negmax_ready"], 1)

                def scale(i):
                    m = (base + i) % 2
                    g = blocks[i][2]
                    taken(dve, att_key(kind, "S", i))
                    rsum = rowsum[:, m, 0:g]
                    if kind == "swa":
                        link(dve.tensor_tensor(rsum, rsum, sinke[:, m, 0:g], ALU.add))
                    link(dve.reciprocal(rsum, rsum))
                    for h in range(g):
                        v = prob_view(kind, i)[:, h, :]
                        ins = dve.tensor_scalar(v, v, rowsum[:, m, h:h + 1], None, ALU.mult)
                    ins.then_inc(s["probs_ready"], 1)

                maxima(0)
                for i in range(len(blocks)):
                    if i + 1 < len(blocks):
                        maxima(i + 1)
                    scale(i)

            n_rows = [0]

            def row_softmax(key, dst, count, w, scale, sink, more=None):
                full(dve, key)
                v = dst[0:count, 0:w]
                w0 = min(w, 1024)
                free(dve.tensor_copy(dst[0:count, 0:w0], pair(key)[0:count, 0:w0]), key)
                if more:
                    full(dve, more)
                    free(dve.tensor_tensor(dst[0:count, w0:w], pair(more)[0:count, 0:w - w0], small[0:count, 16:24], ALU.add), more)
                    taken(dve, more)
                taken(dve, key)
                c = lambda i: st[0:count, i:i + 1]
                link(dve.tensor_reduce(c(24), v, AX.X, ALU.max))
                if sink:
                    link(dve.scalar_tensor_tensor(c(25), c(24), scale, sinkr[:, :], ALU.mult, ALU.max))
                    dve.tensor_scalar(c(26), c(25), -1.0, None, ALU.mult)
                    dve.tensor_tensor(c(27), sinkr[:, :], c(25), ALU.subtract).then_inc(s["row_neg"], 1)
                else:
                    dve.tensor_scalar(c(26), c(24), -scale, None, ALU.mult).then_inc(s["row_neg"], 1)
                n_rows[0] += 1
                dve.wait_ge(s["row_exp"], n_rows[0])
                if sink:
                    link(dve.tensor_tensor(c(28), c(28), c(27), ALU.add))
                link(dve.reciprocal(c(29), c(28)))
                dve.tensor_scalar(v, v, c(29), None, ALU.mult).then_inc(s["row_probs"], 1)

            dve.wait_ge(s["sink_in"], 32)
            attention("swa")
            row_softmax(("swR",), sRs, 64, P, 0.125, True)

            n_rstd = [0]

            def variance(ins):
                ins.then_inc(s["var_ready"], 1)
                n_rstd[0] += 1
                return n_rstd[0]

            def decayed_scores(n):
                full(dve, ("retS", n))
                free(dve.tensor_tensor(retP, pair(("retS", n)).rearrange("p (h q) -> p h q", h=8), decay[:, :, :], ALU.mult), ("retS", n))

            def decayed_keys(n):
                full(dve, ("retK", n))
                free(dve.tensor_tensor(kd.rearrange("p (h e) -> p h e", h=8), pair(("retK", n))[:, 0:512].rearrange("p (h e) -> p h e", h=8),
                                       small[:, 0:8].unsqueeze(2).to_broadcast([P, 8, 64]), ALU.mult), ("retK", n))

            def new_state(n):
                key = ("retU", n)
                full(dve, key)
                u = pair(key)[:, 0:512].rearrange("p (j e) -> p j e", j=4)
                if n == 0:
                    dve.tensor_copy(S[0:64, :, :], u[0:64, :, 0:64])
                    free(dve.tensor_copy(S[64:P, :, :], u[64:P, :, 64:P]), key)
                    return
                taken(dve, ("retU", n - 1))
                link(dve.tensor_tensor(S, S, small[:, 8:12].unsqueeze(2).to_broadcast([P, 4, 64]), ALU.mult))
                dve.tensor_tensor(S[0:64, :, :], u[0:64, :, 0:64], S[0:64, :, :], ALU.add)
                free(dve.tensor_tensor(S[64:P, :, :], u[64:P, :, 64:P], S[64:P, :, :], ALU.add), key)

            def gated(n):
                key = ("retO", n) if n < 4 else ("sOt",)
                r = ROWS[n]
                full(dve, key)
                if n >= 2:
                    full(dve, ("retG", n - 2))
                flat = o_t[0:r, n % 2, :]
                heads = flat.rearrange("p (h e) -> p h e", h=8)
                by_bank = flat.rearrange("p (c q e) -> p q c e", c=4, q=2)
                sqr = o_u[0:r, :].rearrange("p (h e) -> p h e", h=8)
                if n < 4:
                    o = pair(key)[0:r, :].rearrange("p (q n) -> p q n", q=2)[:, :, 0:256].rearrange("p q (c e) -> p q c e", c=4)
                else:
                    o = pair(key)[0:r, 0:512].rearrange("p (c q e) -> p q c e", c=4, q=2)
                mean, var = st[0:r, 8:16], st[0:r, 16:24]
                wide = lambda a: a.unsqueeze(2).to_broadcast([r, 8, 64])
                mean_b = mean.rearrange("p (c q) -> p q c", q=2)
                link(dve.tensor_reduce(mean_b, o, AX.X, ALU.add))
                link(dve.tensor_scalar(mean, mean, 1.0 / 64, None, ALU.mult))
                free(dve.tensor_tensor(by_bank, o, mean_b.unsqueeze(3).to_broadcast([r, 2, 4, 64]), ALU.subtract), key)
                taken(dve, key)
                link(dve.tensor_tensor(sqr, heads, heads, ALU.mult))
                link(dve.tensor_reduce(var, sqr, AX.X, ALU.add))
                dve.wait_ge(s["rstd_ready"], variance(dve.tensor_scalar(var, var, 1.0 / 64, EPS, ALU.mult, ALU.add)))
                link(dve.tensor_tensor(heads, heads, wide(var), ALU.mult))
                link(dve.tensor_tensor(flat, flat, gng[0:r, 0, :], ALU.mult))
                link(dve.tensor_tensor(flat, flat, gng[0:r, 1, :], ALU.add))
                dve.tensor_tensor(flat, flat, g_s[0:r, n, :], ALU.mult).then_inc(s["gated_ready"], 1)

            dve.wait_ge(s["gn_in"], 32)
            taken(dve, ("g", 1, 1))
            for n in range(4):
                decayed_scores(n)
                if n:
                    gated(n - 1)
                decayed_keys(n)
                new_state(n)
            gated(3)
            dve.wait_ge(s["state_in"], 16 * 16)
            for j in range(4):
                key = ("sU", j)
                full(dve, key)
                u = pair(key).rearrange("p (b e) -> p b e", b=DB)
                for q in (0, 64):
                    ins = dve.scalar_tensor_tensor(Ss[q:q + 64, :, j, :], Ss[q:q + 64, :, j, :], small[q:q + 64, 12 + j:13 + j],
                                                   u[q:q + 64, :, q:q + 64], ALU.mult, ALU.add)
                free(ins, key)
            gated(4)

            def norm(i):
                def stats(t):
                    r = ROWS[t]
                    xt = x[0:r, t, :]
                    if i:
                        dve.wait_ge(s["x_ready"], NT * (i - 1) + t + 1)
                    else:
                        dve.wait_ge(s["x_loaded"], 16 * NT)
                    if i % 3 < 2:
                        key = ("y", i, t)
                        full(dve, key)
                        free(dve.scalar_tensor_tensor(xt, xt, ALPHA, pair(key)[0:r, :], ALU.mult, ALU.add), key)
                        taken(dve, key)
                    else:
                        taken(dve, ("moeY", i // 3, len(MOE_BLOCKS) - NT + t))
                        link(dve.scalar_tensor_tensor(xt, xt, ALPHA, acc[0:r, t, :], ALU.mult, ALU.add))
                    dve.bn_stats(bns[0:r, 0, :], xt[:, 0:512])
                    link(dve.bn_stats(bns[0:r, 1, :], xt[:, 512:1024]))
                    link(dve.bn_aggr(mv_t[0:r, t % 2, :], bns[0:r, :, :]))
                    return variance(dve.tensor_scalar(rstd[0:r, t % 2, 0:1], mv_t[0:r, t % 2, 1:2], EPS, None, ALU.add))

                def normalise(t, n):
                    r = ROWS[t]
                    xt = x[0:r, t, :]
                    dve.wait_ge(s["rstd_ready"], n)
                    dve.tensor_scalar(xt, xt, mv_t[0:r, t % 2, 0:1], rstd[0:r, t % 2, 0:1], ALU.subtract, ALU.mult
                                      ).then_inc(s["ln_norm"], 1)

                n = stats(0)
                for t in range(NT):
                    more = stats(t + 1) if t + 1 < NT else None
                    normalise(t, n)
                    n = more

            def first_max(out, m, v, tmp):
                mb = m.unsqueeze(2).to_broadcast([P, NT, 4])
                io4 = small[:, 32:36].unsqueeze(1).to_broadcast([P, NT, 4])
                link(dve.tensor_tensor(tmp, v, mb, ALU.is_equal))
                link(dve.tensor_tensor(tmp, tmp, io4, ALU.mult))
                link(dve.tensor_reduce(rs[:, 11, :], tmp, AX.X, ALU.min))
                link(dve.tensor_tensor(out, rs[:, 11, :].unsqueeze(2).to_broadcast([P, NT, 4]), io4, ALU.is_equal))

            def router(l):
                key = ("rt", l)
                link(dve.memset(L, 0.0))
                full(dve, key)
                o = pair(key)[:, 0:NT * 32].rearrange("p (t n) -> p t n", t=NT)
                dve.tensor_tensor(L[:, 0:4, :], o[:, 0:4, 0:20], rb[:, l, :].unsqueeze(1).to_broadcast([P, 4, 20]), ALU.add)
                free(dve.tensor_tensor(L[0:8, 4, :], o[0:8, 4, 0:20], rb[0:8, l, :], ALU.add), key)
                taken(dve, key)
                gl = L[:, :, 0:4]
                wide = lambda i: rs[:, i, :].unsqueeze(2).to_broadcast([P, NT, 4])
                link(dve.tensor_reduce(rs[:, 0, :], gl, AX.X, ALU.max))
                first_max(oh, rs[:, 0, :], gl, rB)
                dve.tensor_tensor(rA, gl, wide(0), ALU.subtract).then_inc(s["router_neg"], 1)
                pr = prod.rearrange("p t (g e) -> p t g e", g=4)
                link(dve.tensor_tensor(pr, L[:, :, 4:20].rearrange("p t (g e) -> p t g e", g=4),
                                       oh.unsqueeze(3).to_broadcast([P, NT, 4, 4]), ALU.mult))
                link(dve.tensor_reduce(el4, prod.rearrange("p t (g e) -> p t e g", g=4), AX.X, ALU.add))
                link(dve.tensor_reduce(rs[:, 1, :], el4, AX.X, ALU.max))
                first_max(oh1, rs[:, 1, :], el4, rB)
                link(dve.scalar_tensor_tensor(el4, oh1, NEG, el4, ALU.mult, ALU.add))
                link(dve.tensor_reduce(rs[:, 2, :], el4, AX.X, ALU.max))
                first_max(oh2, rs[:, 2, :], el4, rB)
                dve.tensor_tensor(rs[:, 5, :], rs[:, 2, :], rs[:, 1, :], ALU.subtract).then_inc(s["router_neg"], 1)
                dve.wait_ge(s["router_exp"], 2 * l + 2)
                link(dve.tensor_reduce(rs[:, 6, :], rA, AX.X, ALU.add))
                link(dve.scalar_tensor_tensor(rs[:, 7, :], rs[:, 5, :], 1.0, rs[:, 6, :], ALU.add, ALU.mult))
                link(dve.reciprocal(rs[:, 8, :], rs[:, 7, :]))
                link(dve.tensor_tensor(rs[:, 9, :], rs[:, 8, :], rs[:, 5, :], ALU.mult))
                link(dve.tensor_tensor(rB, oh1, wide(8), ALU.mult))
                link(dve.tensor_tensor(rC, oh2, wide(9), ALU.mult))
                link(dve.tensor_tensor(rB, rB, rC, ALU.add))
                link(dve.tensor_tensor(gates.rearrange("p t (g e) -> p t g e", g=4), oh.unsqueeze(3).to_broadcast([P, NT, 4, 4]),
                                       rB.unsqueeze(2).to_broadcast([P, NT, 4, 4]), ALU.mult))

            def experts(l):
                router(l)
                base = l * len(MOE_BLOCKS)

                def swiglu(i):
                    e, t = MOE_BLOCKS[i]
                    r = ROWS[t]
                    key = ("moeH", l, i)
                    o = pair(key)
                    sg = ex[0:r, i % 2, :]
                    dve.wait_ge(s["moe_exp"], base + i + 1)
                    link(dve.tensor_scalar(sg, sg, 1.0, None, ALU.add))
                    link(dve.reciprocal(sg, sg))
                    link(dve.tensor_tensor(sg, o[0:r, 0:DE], sg, ALU.mult))
                    if i >= 2:
                        full(dve, ("moeT", l, i - 2))
                    free(dve.tensor_tensor(actb[0:r, i % 2, :], o[0:r, DE:2 * DE], sg, ALU.mult), key)

                swiglu(0)
                for i, (e, t) in enumerate(MOE_BLOCKS):
                    if i + 1 < len(MOE_BLOCKS):
                        swiglu(i + 1)
                    r = ROWS[t]
                    key = ("moeY", l, i)
                    full(dve, key)
                    gate = gates[0:r, t, e:e + 1]
                    if e == 0:
                        free(dve.tensor_scalar(acc[0:r, t, :], pair(key)[0:r, :], gate, None, ALU.mult), key)
                    else:
                        taken(dve, ("moeY", l, i - NT))
                        free(dve.scalar_tensor_tensor(acc[0:r, t, :], pair(key)[0:r, :], gate, acc[0:r, t, :], ALU.mult, ALU.add), key)

            def latent_attention():
                dve.wait_ge(s["odd_in"], 32)
                dve.memset(qrS, 0.0).then_inc(s["qrS_zero"], 1)
                for t in range(NT):
                    key = ("oin", t)
                    r = ROWS[t]
                    o = pair(key)
                    m = rms[0:r, t % 2, :]
                    tab = rope_t[0:r, t, :]
                    kr = rows[0:r, t, P:ROW_W]
                    tm = tmpm[0:r, 0:32]
                    dve.wait_ge(s["sq_done"], t + 1)
                    dve.tensor_scalar(m[:, 2:3], m[:, 0:1], 1.0 / 256, EPS, ALU.mult, ALU.add)
                    dve.wait_ge(s["rstd_ready"], variance(dve.tensor_scalar(m[:, 3:4], m[:, 1:2], 1.0 / 128, EPS, ALU.mult, ALU.add)))
                    dve.tensor_scalar(cqn[0:r, t % 2, :], o[0:r, 0:256], m[:, 2:3], None, ALU.mult)
                    dve.scalar_tensor_tensor(rows[0:r, t, 0:P], o[0:r, 256:384], m[:, 3:4], kvg[0:r, :], ALU.mult, ALU.mult)
                    dve.tensor_tensor(kr, o[0:r, 384:416], tab[:, 0:32], ALU.mult)
                    dve.tensor_tensor(tm[:, 0:16], o[0:r, 400:416], tab[:, 32:48], ALU.mult)
                    free(dve.tensor_tensor(tm[:, 16:32], o[0:r, 384:400], tab[:, 48:64], ALU.mult), key)
                    taken(dve, key)
                    link(dve.tensor_tensor(kr, kr, tm, ALU.add))
                    dve.tensor_copy(kr4[0:r, t % 2, :].rearrange("p (a b) -> p a b", a=4),
                                    kr.unsqueeze(1).to_broadcast([r, 4, 32])).then_inc(s["oin_ready"], 1)

                def rotate(t):
                    key = ("qrope", t)
                    r = ROWS[t]
                    full(dve, key)
                    if t:
                        dve.wait_ge(s["qrtok_ready"], t)
                    o = pair(key)[0:r, 0:256].rearrange("p (h e) -> p h e", h=8)
                    tab = rope_t[0:r, t, :].unsqueeze(1)
                    q = qr_tok[0:r, t % 2, :].rearrange("p (h e) -> p h e", h=8)
                    u = scratch[0:r, 0:256].rearrange("p (h e) -> p h e", h=8)
                    dve.tensor_tensor(q, o, tab[:, :, 0:32].to_broadcast([r, 8, 32]), ALU.mult)
                    dve.tensor_tensor(u[:, :, 0:16], o[:, :, 16:32], tab[:, :, 32:48].to_broadcast([r, 8, 16]), ALU.mult)
                    free(dve.tensor_tensor(u[:, :, 16:32], o[:, :, 0:16], tab[:, :, 48:64].to_broadcast([r, 8, 16]), ALU.mult), key)
                    taken(dve, key)
                    if t < 4:
                        dve.tensor_tensor(q, q, u, ALU.add).then_inc(s["qrtok_ready"], 1)
                    else:
                        link(dve.tensor_tensor(q, q, u, ALU.add))
                        dve.tensor_copy(qr_rep[0:8, :, :].rearrange("p h (a e) -> p h a e", a=4),
                                        q.unsqueeze(2).to_broadcast([8, 8, 4, 32])).then_inc(s["qrtok_ready"], 1)

                def take(key, dst, src):
                    full(dve, key)
                    free(dve.tensor_copy(dst, src), key)

                for j in (0, 2):
                    take(("qn", j), halves(qnT[:, j, :]), halves(pair(("qn", j))))
                rotate(0)
                for h in (0, 2, 4, 6):
                    take(("ql", h), halves(q_lat[:, h, :]), halves(pair(("ql", h))))
                for t in range(1, NT):
                    rotate(t)
                attention("mla")
                for b in (0, 2, 4, 6):
                    take(("pcT", b), ckvp[:, b % 2, :], pair(("pcT", b)))
                row_softmax(("pR",), srow, 64, 1032, SCALE["mla"], False, more=("pN",))

            norm(0)
            attention("mem0")
            row_softmax(("msR", 0), sRm, 32, 256, 0.125, False)
            norm(1)
            dve.wait_ge(s["router_in"], 16 * 8)
            experts(0)
            norm(2)
            latent_attention()
            norm(3)
            attention("mem1")
            row_softmax(("msR", 1), sRm, 32, 256, 0.125, False)
            norm(4)
            experts(1)
            norm(5)


_INS = ["x_prompt", "x_sample", "mem_prompt", "cache_swa_k", "cache_swa_v", "state_ret", "cache_mla", "page_table",
        "cache_mem_k", "cache_mem_v", "w_in_even", "swa_sink", "ret_gn_g", "ret_gn_b", "w_out_even", "w_in_odd",
        "mla_q_norm", "mla_kv_norm", "w_uq", "w_uk", "w_uv", "w_out_odd", "w_mem_q", "w_mem_k", "w_mem_v", "w_mem_o",
        "moe_w_group", "moe_b_group", "moe_w_router", "moe_b_router", "moe_w_in", "moe_w_out", "ln_g", "ln_b"]
_OUTS = [(1, 512, 1024), (8, 1, 1024), (1, 1, 128, 2, 64), (1, 1, 128, 2, 64), (1, 1, 8, 64, 64), (1, 1, 512, 160),
         (2, 1, 256, 4, 64), (2, 1, 256, 4, 64), (1, 8, 128, 2, 64), (1, 8, 128, 2, 64), (1, 8, 8, 64, 64), (1, 8, 1, 160)]


def kernel(**inputs):
    import numpy as _np
    import concourse.bacc as _bacc
    from concourse import mybir as _mybir
    from concourse.bass_utils import run_bass_kernel_spmd as _run

    nc = _bacc.Bacc("TRN2", target_bir_lowering=False, num_devices=1)
    arrays, io = {}, {}
    given = {name: _np.ascontiguousarray(inputs[name]) for name in _INS}
    w_in, w_uq = given.pop("w_in_even"), given.pop("w_uq")
    given["w_in_even"] = w_in
    given["w_ka_twice"] = _np.ascontiguousarray(w_in[0][:, 512:640].reshape(1024, 2, 1, 64).repeat(2, 2).reshape(1024, 256))
    sink = given.pop("swa_sink")[0]
    given["sink_by_bank"] = _np.ascontiguousarray(sink[[0, 2, 1, 3, 4, 6, 5, 7]])
    given["sink_rows"] = _np.tile(sink, 8)
    per_head = w_uq[0].reshape(256, 8, 96)
    given["w_uq_split"] = _np.concatenate([per_head[:, :, :64].reshape(256, 512), per_head[:, :, 64:].reshape(256, 256)], 1)
    given.update({name: _np.ascontiguousarray(a) for name, a in shape_constants().items()})
    for name, a in given.items():
        arrays[f"in_{name}_dram"] = a
        io[name] = nc.dram_tensor(f"in_{name}_dram", a.shape, _mybir.dt.from_np(a.dtype), kind="ExternalInput").ap()
    outs = [nc.dram_tensor(f"out_{i}_dram", shape, _mybir.dt.float32, kind="ExternalOutput").ap()
            for i, shape in enumerate(_OUTS)]
    decoder_step(nc, io, outs)
    r = _run(nc, [arrays], core_ids=[0])
    return tuple(r.results[0][f"out_{i}_dram"] for i in range(len(_OUTS)))
```

```python
from contextlib import ExitStack

import numpy as np

import concourse.bass as bass
from concourse import mybir

F32 = mybir.dt.float32
I32 = mybir.dt.int32
U32 = mybir.dt.uint32
ALU = mybir.AluOpType
ACT = mybir.ActivationFunctionType
AX = mybir.AxisListType

P = 128
D = 1024
KD = D // P
SEQ = 512
DB = 8
T = SEQ + DB
HALF = T // 2
NT = 5
ROWS = [128, 128, 128, 128, 8]
PAST = 1024
DEPTH = 2
ALPHA = (2 * DEPTH) ** 0.25
EPS = 1e-5
NEG = -1e30
NE = 16
DE = 256
NPAGE = 8
ROW_W = 160
SLOTS = 5
ARENA = 21500
PIECE = 2048
EXTRA_SLOTS = 4
CAP = 96
SPILL = 2 * T // (CAP + 1)
NB = NE + SPILL
STEPS = (T - 1) // CAP
EIN_W = 2816


def tile_cols(t):
    return slice(t * P, t * P + ROWS[t])


def shape_constants():
    f = np.float32
    pos = np.concatenate([np.arange(SEQ), np.full(DB, PAST)]).astype(f)
    inv64 = (f(10000.0) ** (-np.arange(0, 64, 2, dtype=f) / f(64))).astype(f)
    ang = (pos[None, :] * inv64[:, None]).astype(f)
    cos, sin = np.cos(ang).astype(f), np.sin(ang).astype(f)
    cos_f = np.tile(cos, (4, 1))
    sin_f = np.concatenate([-sin, sin, -sin, sin], 0)
    inv32 = (f(10000.0) ** (-np.arange(0, 32, 2, dtype=f) / f(32))).astype(f)
    ang2 = (pos[:, None] * inv32[None, :]).astype(f)
    c2, s2 = np.cos(ang2).astype(f), np.sin(ang2).astype(f)
    tab = np.zeros((NT * P, 64), f)
    tab[:T] = np.concatenate([c2, c2, -s2, s2], 1)
    rope_t = tab.reshape(NT, P, 64).transpose(1, 0, 2)
    q = np.arange(P)[:, None]
    s = np.arange(2 * P)[None, :]
    band = np.where((q + P - s >= 0) & (q + P - s < P), 0.0, NEG).astype(f)
    h = np.arange(8, dtype=f)
    lg = np.log1p(-np.exp2(f(-5.0) - h)).astype(f)
    by_bank = [0, 2, 4, 6, 1, 3, 5, 7]
    i = np.arange(P, dtype=f)
    diff = i[None, :] - i[:, None]
    decay = np.where(diff[:, None, :] >= 0,
                     np.exp(np.maximum(diff, 0)[:, None, :] * lg[None, :, None]), 0.0) * 0.125
    hp = (2 * np.arange(4)[None, :] + (np.arange(P) // 64)[:, None])
    qdec = np.exp((i[None, None, :] + 1) * lg[hp][:, :, None])
    kdec = np.exp((P - 1 - i)[:, None] * lg[None, :]) * 0.125
    sdec = np.exp(P * lg[hp])
    sdec1 = np.exp(lg[hp])
    bh = np.arange(64) // 8
    newmask = np.where(bh[:, None] == np.arange(8)[None, :], 0.0, NEG)
    vmask = np.eye(8)
    iota4 = np.tile(np.arange(4) - 8.0, (P, 1))
    small = np.zeros((P, 96), f)
    small[:, 0:8] = kdec
    small[:, 8:12] = sdec
    small[:, 12:16] = sdec1
    small[:64, 16:24] = newmask
    small[:8, 24:32] = vmask
    small[:, 32:36] = iota4
    small[:, 36:44] = -0.5
    small[:, 44:60] = np.arange(16)
    small[:, 60:60 + STEPS] = CAP * np.arange(1, STEPS + 1)
    route = np.zeros((P, 4, P), f)
    route[:, 0] = i[:, None] < i[None, :]
    route[:, 1] = 1.0
    before = np.arange(NE)[None, :] < np.arange(NE)[:, None]
    route[:, 2:4] = before.reshape(1, 2, P)
    tokens = np.arange(P, dtype=np.int32)[:, None] + P * np.arange(NT, dtype=np.int32)[None, :]
    return {
        "c_ident": np.eye(P, dtype=f),
        "c_cos": cos_f.astype(f), "c_sin": sin_f.astype(f),
        "c_rope": np.ascontiguousarray(rope_t, f),
        "c_band": band,
        "c_decay": np.ascontiguousarray(decay.astype(f)[:, by_bank]), "c_qdec": qdec.astype(f), "c_small": small,
        "c_route": route, "c_tokens": tokens.astype(np.uint32), "c_no_tokens": np.zeros((CAP, NB), np.uint32), "c_no_row": np.zeros((1, 1, D), f),
    }


SWA_BLOCKS = [(n, 4 * kv, 4, 128 if n == 0 else 256) for n in range(4) for kv in range(2)]
MEM_BLOCKS = [(n, 0, 4, 256) for n in range(4)]
MLA_BLOCKS = [(n, h, 2, 128 * (n + 1)) for n in range(4) for h in range(0, 8, 2)]


def pipelined(first, second, third, n):
    out = [(first, 0)] + ([(first, 1)] if n > 1 else [])
    for i in range(n):
        out.append((second, i))
        if i + 2 < n:
            out.append((first, i + 2))
        out.append((third, i))
    return out


def expert_order():
    out = [("X", 0), ("X", 1), ("H", 0)]
    for e in range(NE):
        out += [("X", e + 2)] if e + 2 < NE else []
        out += [("H", e + 1)] if e + 1 < NE else []
        out += [("Y", e)]
    return out


def psum_jobs():
    jobs = []
    jobs += [("xT", -1, t) for t in range(NT)]
    jobs += [("memT", m) for m in range(2)]
    for l in range(DEPTH):
        jobs += [("mkv", l, m) for m in range(2)] + [("mkT", l)]
    jobs += [("qa", j) for j in range(4)] + [("ka", 0), ("ka", 1), ("va",)]
    jobs += [("qr", j) for j in range(4)] + [("kr", j) for j in range(4)]
    jobs += [(w, i, m) for w in ("vr", "g") for i in range(2) for m in range(2)]
    jobs += [("kaTok",)]
    jobs += [("swa" + s, i) for s, i in pipelined("S", "T", "O", len(SWA_BLOCKS))]
    jobs += [("kwT",), ("swS",), ("swR",), ("swT",), ("swO",)]
    for n in range(4):
        jobs += [("retS", n), ("retK", n), ("retO", n), ("retU", n)]
        if n:
            jobs += [("retG", n - 1)]
    jobs += [("skT",), ("retG", 3)] + [("sU", j) for j in range(4)] + [("sO",), ("sOt",), ("retG", 4)]
    for l in range(DEPTH):
        if l == 1:
            jobs += [("ukT",)]
            for t in range(NT):
                jobs += [("oin", t)] + ([("oinT", t - 1)] if t else [])
            jobs += [("oinT", 4)]
            jobs += [("qn", j) for j in range(4)]
            jobs += [("qrope", 0)]
            jobs += [("ql", h) for h in range(8)]
            for t in range(NT):
                jobs += ([("qrope", t)] if t else []) + ([("qrT", t - 1)] if t else [])
            jobs += [("qrT", 4)]
            jobs += [("mla" + s, i) for s, i in pipelined("S", "T", "O", len(MLA_BLOCKS))]
            jobs += [("pkT", 0), ("pkT", 1)]
            for b in range(DB):
                jobs += [("pcT", b)] + ([("pS", b - 1)] if b else [])
            jobs += [("pS", DB - 1), ("pR",), ("pN",), ("pT",), ("pO",)]
            jobs += [("uv", j) for j in range(4)]
        jobs += [("y", 3 * l, t) for t in range(NT)]
        jobs += [("xT", 3 * l, t) for t in range(NT)]
        jobs += [("mq", l, j) for j in range(2)]
        jobs += [("mem" + s, l, i) for s, i in pipelined("S", "T", "O", len(MEM_BLOCKS))]
        for g in range(4):
            jobs += [("kcT", l, g)] + ([("msS", l, g - 1)] if g else [])
        jobs += [("msS", l, 3), ("msR", l), ("msT", l), ("msO", l)]
        jobs += [("y", 3 * l + 1, t) for t in range(NT)]
        jobs += [("xT", 3 * l + 1, t) for t in range(NT)]
        jobs += [("rt", l), ("rank", l)]
        jobs += [("moe" + s, l, e) for s, e in expert_order()]
        if l == 0:
            jobs += [("xT", 2, t) for t in range(NT)]
    return jobs


def decoder_step(nc, io, outs):
    (y_prompt, y_sample, swa_k_p, swa_v_p, ret_p, mla_p, mem_k_p, mem_v_p,
     swa_k_s, swa_v_s, ret_s, mla_s) = outs

    JOBS = psum_jobs()
    J = {key: n for n, key in enumerate(JOBS)}
    assert len(J) == len(JOBS)

    W = []

    def piece(name, src, shape, last):
        W.append((name, src, shape, last))

    for l in range(DEPTH):
        for w in ("k", "v"):
            piece(("m" + w, l), io["w_mem_" + w][l].rearrange("(k p) n -> p k n", p=P), (8, 256), ("mkv", l, 1))
    ein_last = [("qa", 1), ("qa", 3), ("va",), ("qr", 1), ("qr", 3), ("kr", 1), ("kr", 3),
                ("vr", 0, 1), ("vr", 1, 1), ("g", 0, 1), ("g", 1, 1)]
    for i, last in enumerate(ein_last):
        if i == 2:
            piece(("ka",), io["w_ka_twice"].rearrange("(k p) n -> p k n", p=P), (8, 256), ("ka", 1))
            piece(("va",), io["w_in_even"][0, :, 640:768].rearrange("(k p) n -> p k n", p=P), (8, 128), last)
            continue
        piece(("ein", i), io["w_in_even"][0, :, 256 * i:256 * i + 256].rearrange("(k p) n -> p k n", p=P), (8, 256), last)
    for l in range(DEPTH):
        if l == 0:
            for i in range(4):
                piece(("out", l, i), io["w_out_even"][0, 256 * i:256 * i + 256].rearrange("(k p) n -> p k n", p=P),
                      (2, 1024), ("y", 0, 4))
        else:
            piece(("uk",), io["w_uk"][0].rearrange("c h n -> c (h n)"), (512,), ("ukT",))
            for i in range(2):
                piece(("oin", i), io["w_in_odd"][0, 512 * i:512 * i + 512].rearrange("(k p) n -> p k n", p=P),
                      (4, 416), ("oin", 4))
            piece(("uq",), io["w_uq_split"].rearrange("(k p) n -> p k n", p=P), (2, 768), ("qrope", 4))
            piece(("uv",), io["w_uv"][0].rearrange("c h n -> c (h n)"), (512,), ("uv", 3))
            for i in range(2):
                piece(("out", l, i), io["w_out_odd"][0, 256 * i:256 * i + 256].rearrange("(k p) n -> p k n", p=P),
                      (2, 1024), ("y", 3, 4))
        piece(("mq", l), io["w_mem_q"][l].rearrange("(k p) n -> p k n", p=P), (8, 256), ("mq", l, 1))
        piece(("mo", l), io["w_mem_o"][l].rearrange("(k p) n -> p k n", p=P), (2, 1024), ("y", 3 * l + 1, 4))
        for e in range(NE):
            for i in range(2):
                piece(("wi", l, e, i), io["moe_w_in"][l, e, 512 * i:512 * i + 512].rearrange("(k p) n -> p k n", p=P),
                      (4, 512), ("moeH", l, e))
            piece(("wo", l, e), io["moe_w_out"][l, e].rearrange("(k p) n -> p k n", p=P), (2, 1024), ("moeY", l, e))
    WI = {w[0]: n for n, w in enumerate(W)}
    PLACE, held = [], {}
    for n, (name, src, shape, last) in enumerate(W):
        slots = range(SLOTS + EXTRA_SLOTS if name[0] in ("wi", "wo") else SLOTS)
        slot = min(slots, key=lambda q: J[W[held[q][-1]][3]] if q in held else -1)
        before = held.setdefault(slot, [])
        PLACE.append((slot, len(before), before[-1] if before else None))
        before.append(n)

    x_rows = nc.dram_tensor("x_rows", (T, D), F32, kind="Internal").ap()
    slot_tokens = nc.dram_tensor("slot_tokens", (CAP * NB, 1), U32, kind="Internal").ap()
    y_rows = nc.dram_tensor("y_rows", (CAP * NB, D), F32, kind="Internal").ap()

    with ExitStack() as ctx:
        def sb(name, shape, dt=F32):
            return ctx.enter_context(nc.sbuf_tensor(name, shape, dt))

        def sem(name):
            return ctx.enter_context(nc.semaphore(name))

        PS = ctx.enter_context(nc.psum_tensor("PS", [P, 4, 1024], F32))

        ring = sb("ring", [P, SLOTS, PIECE])
        x = sb("x", [P, NT, D])
        xT = sb("xT", [P, KD, T])
        oT = xT
        ident = sb("ident", [P, P])
        cosf = sb("cosf", [P, T])
        sinf = sb("sinf", [P, T])
        rope_t = sb("rope_t", [P, NT, 64])
        band = sb("band", [P, 256])
        decay = sb("decay", [P, 8, P])
        qdec = sb("qdec", [P, 4, P])
        small = sb("small", [P, 96])
        route = qdec
        tokens = sb("tokens", [P, NT], U32)
        places = sb("places", [P, 2, NT], U32)
        block_tokens = sb("block_tokens", [CAP, NB], U32)
        spill = sb("spill", [1, 1 + SPILL], I32)
        lnb = sb("lnb", [P, 2, D])
        mkT = sb("mkT", [P, DEPTH, 2, 256])
        mv = sb("mv", [P, DEPTH, 2, 256])
        wr = sb("wr", [P, DEPTH, KD, 20])
        rb = sb("rb", [P, DEPTH, 20])
        ptab = sb("ptab", [1, 64], I32)
        pbuf = sb("pbuf", [P, 2, 1024])
        pT = sb("pT", [P, 2, 1024])
        rowmax = sb("rowmax", [P, 2, 4])
        negmax = sb("negmax", [P, 2, 4])
        rowsum = sb("rowsum", [P, 2, 4])
        sinke = sb("sinke", [P, 2, 4])
        sinkb = sb("sinkb", [P, 8])
        sinkr = sb("sinkr", [64, 1])
        st = sb("st", [P, 32])
        bns = sb("bns", [P, 2, 6])
        mv_t = sb("mv_t", [P, 2, 2])
        rstd = sb("rstd", [P, 2, 1])
        rms = sb("rms", [P, 2, 4])
        arena = sb("arena", [P, ARENA])

        at = [0]

        def part(*dims, at0=None):
            n = int(np.prod(dims))
            o = at[0] if at0 is None else at0
            if at0 is None:
                at[0] += n
                assert at[0] <= ARENA, at[0]
            v = arena[:, o:o + n]
            names = "abcde"[:len(dims)]
            if len(dims) > 1:
                v = v.rearrange("p (" + " ".join(names) + ") -> p " + " ".join(names),
                                **{c: d for c, d in zip(names, dims)})
            return v

        qaT = part(4, T)
        kaD = part(2, T)
        qrT = part(4, T)
        krT = part(4, T)
        v_tok = part(NT, 640)
        g_s = part(NT, 512)
        swap0 = at[0]
        swapb = part(2, T)
        retP = part(8, P, at0=swap0)
        vmk = part(8, P, at0=swap0)
        kd = part(512)
        qd = part(4, P)
        S = part(4, 64)
        o_t = part(2, 512)
        o_u = part(512)
        gng = lnb[:, :, 0:512]
        mk = part(2, 256, at0=at[0])
        Kw = part(8, P)
        Vw = part(8, P)
        ka_tok = part(P)
        ks_tok = part(512)
        sTs = part(64)
        sRs = part(P)
        pTs_sw = part(64)
        soT = part(4, 8)
        qas = part(4, 8)
        Ss = pT[:, :, :].rearrange("p a (b c) -> p (a b c)", b=2).rearrange("p (b j e) -> p b j e", b=8, j=4)
        memT = part(KD, 256, at0=0)
        at[0] = 0
        qmT = part(2, T)
        Kc = part(8, 2, 256)
        Vc = part(8, 2, 256)
        KcT = part(2, 2, 2, 256)
        sTm = part(2, 32)
        sRm = part(256)
        pTm = part(2, 32)
        at[0] = 0
        xs = part(3, D)
        xsT = part(2, KD, CAP)
        ex = part(2, 2, CAP)
        actT = part(2, 2, CAP)
        ybuf = part(2, D)
        L = part(NT, 20)
        rA = part(NT, 4)
        rB = part(NT, 4)
        oh = part(NT, 4)
        oh1 = part(NT, 4)
        oh2 = part(NT, 4)
        el4 = part(NT, 4)
        prod = part(NT, 16)
        rs = part(12, NT)
        picks = part(2, NT, NE)
        picked = part(NT, NE)
        sel = part(2, NT, NE)
        more = part(NE, STEPS)
        pre = part(NE, NE)
        pl = part(6, 2, NT)
        per_e = part(3, NE)
        sp_f = part(1 + SPILL)
        assert at[0] <= ARENA - EXTRA_SLOTS * PIECE
        y_of = (pbuf, pT)
        at[0] = 0
        cqn = part(2, 256)
        kr4 = part(2, P)
        cqT = part(2, T)
        rows = part(NT, ROW_W)
        ckvT = part(T)
        krT4 = part(T)
        qn_at = at[0]
        qnT = part(4, T)
        q_lat = part(8, T)
        ctxT = q_lat
        qr_tok = part(2, 256)
        qr_at = at[0]
        qrT2 = part(2, T)
        qrS = part(4, 8, 8)
        qlS = part(8, 8)
        kvg = part(P)
        qg = part(2)
        ukT = part(4, P)
        scratch = part(384)
        tmpm = part(64)
        nat = part(64, P)
        natr = lnb[:, :, :].rearrange("p a n -> p (a n)")
        krp = part(16, P, at0=qn_at)
        sTp = part(8, 64, at0=0)
        srow = part(1032, at0=512)
        pTn = part(64, at0=1544)
        qr_rep = part(8, P, at0=768)
        pTp = part(8, 64, at0=qr_at)
        ckvp = pbuf

        names = ["x_loaded", "mem_loaded", "const_in", "ident_in", "router_in", "sink_in", "gn_in", "cache_in",
                 "state_in", "newk_in", "kc_in", "vc_in", "odd_in", "ptab_in", "pages_in", "ln_in", "stored",
                 "mk_stored", "var_ready", "rstd_ready", "x_ready", "ln_norm", "swapped", "rope_done", "negmax_ready", "probs_ready",
                 "vec_step", "act_step", "pool_step", "g_exp", "qd_ready", "vm_ready", "gated_ready",
                 "row_neg", "row_exp", "row_probs", "router_neg", "router_exp", "moe_exp",
                 "moe_done", "picks_ready", "places_ready", "route_in", "tokens_in", "table_out", "scattered",
                 "block_tokens_in", "x_out", "y_scaled", "combined", "sq_done", "qrS_zero", "oin_ready", "qrtok_ready"]
        s = {n: sem(n) for n in names}
        pair_full = [sem(f"pair_full{i}") for i in range(4)]
        pair_free = [sem(f"pair_free{i}") for i in range(4)]
        slot_landed = [sem(f"slot_landed{i}") for i in range(SLOTS + EXTRA_SLOTS)]
        xs_in = [sem(f"xs_in{i}") for i in range(3)]
        y_out = [sem(f"y_out{i}") for i in range(2)]
        y_in = [sem(f"y_in{i}") for i in range(2)]
        spill_s = [{n: sem(f"spill{l}_{n}") for n in ("weights_in", "xs_in", "pe", "act", "dve", "y_out")} for l in range(DEPTH)]
        n_stored = [0]

        def pair(key):
            return PS[:, J[key] % 4, :]

        def full(eng, key):
            n = J[key]
            eng.wait_ge(pair_full[n % 4], n // 4 + 1)

        def free(ins, key):
            ins.then_inc(pair_free[J[key] % 4], 1)

        def taken(eng, key):
            n = J[key]
            eng.wait_ge(pair_free[n % 4], n // 4 + 1)

        def wview(name):
            n = WI[name]
            shape, slot = W[n][2], PLACE[n][0]
            size = int(np.prod(shape))
            at_ = ARENA - (SLOTS + EXTRA_SLOTS - slot) * PIECE
            v = ring[:, slot, 0:size] if slot < SLOTS else arena[:, at_:at_ + size]
            if len(shape) == 2:
                v = v.rearrange("p (a b) -> p a b", a=shape[0])
            return v

        def landed(eng, name):
            n = WI[name]
            eng.wait_ge(slot_landed[PLACE[n][0]], 16 * (PLACE[n][1] + 1))

        def uses(n, bufs, l, i):
            return l * len(range(i % bufs, n, bufs)) + i // bufs + 1

        def spilled(eng, l):
            eng.wait_ge(s["places_ready"], l + 1)
            count = eng.value_load(spill[0:1, 0:1], min_val=0, max_val=SPILL)
            return eng.If(count > 0)

        def bank_pos(h):
            return 2 * (h % 2) + h // 2

        ATT = [("swa", i, b) for i, b in enumerate(SWA_BLOCKS)]
        ATT += [("mem0", i, b) for i, b in enumerate(MEM_BLOCKS)]
        ATT += [("mla", i, b) for i, b in enumerate(MLA_BLOCKS)]
        ATT += [("mem1", i, b) for i, b in enumerate(MEM_BLOCKS)]
        A0 = {}
        for n, (k, i, b) in enumerate(ATT):
            A0.setdefault(k, n)
        BLOCKS = {"swa": SWA_BLOCKS, "mem0": MEM_BLOCKS, "mem1": MEM_BLOCKS, "mla": MLA_BLOCKS}

        def att_key(kind, step, i):
            return ("mem" + step, int(kind[3]), i) if kind.startswith("mem") else (kind + step, i)

        SCALE = {"swa": 0.125, "mem0": 0.125, "mem1": 0.125, "mla": 96.0 ** -0.5}

        block = ctx.enter_context(nc.Block())

        @block.sync
        def _(sp):
            def load(dst, src, signal):
                sp.dma_start(dst, src).then_inc(s[signal], 16)

            for t in range(NT):
                src = io["x_prompt"][0, t * P:t * P + P] if t < 4 else io["x_sample"].rearrange("b s d -> (b s) d")
                load(x[0:ROWS[t], t, :], src, "x_loaded")
            load(ident[:, :], io["c_ident"], "ident_in")
            load(arena[:, 2048:4096].rearrange("p (a b) -> p a b", a=2),
                 io["mem_prompt"][0].rearrange("(m p) d -> p m d", p=P), "mem_loaded")

            def load_piece(n):
                name, src, shape, last = W[n]
                slot, use, before = PLACE[n]
                if before is not None:
                    full(sp, W[before][3])
                if slot >= SLOTS:
                    sp.wait_ge(s["x_ready"], NT * 3 * name[1] + 1)
                sp.dma_start(wview(name), src).then_inc(slot_landed[slot], 16)

            def spilled_weights(l, n):
                sem_ = spill_s[l]
                with spilled(sp, l):
                    for slot in range(3):
                        full(sp, W[max(m for m in range(n) if PLACE[m][0] == slot)][3])
                    for j in range(SPILL):
                        if j:
                            sp.wait_ge(sem_["pe"], 3 * j)
                        e = sp.value_load(spill[0:1, 1 + j:2 + j], min_val=0, max_val=NE - 1)
                        sp.dma_start(ring[:, 0:2, :].rearrange("p a (k n) -> p (a k) n", n=512),
                                     io["moe_w_in"][l, bass.ds(e, 1)].rearrange("o (k p) n -> p (o k) n", p=P)
                                     ).then_inc(sem_["weights_in"], 16)
                        sp.dma_start(ring[:, 2, :].rearrange("p (k n) -> p k n", k=2),
                                     io["moe_w_out"][l, bass.ds(e, 1)].rearrange("o (k p) n -> p (o k) n", p=P)
                                     ).then_inc(sem_["weights_in"], 16)
                    sp.wait_ge(sem_["pe"], 3 * SPILL)

            pages_before = WI[("uk",)]
            for n in range(len(W)):
                if n == pages_before:
                    spilled_weights(0, n)
                    sp.wait_ge(s["ptab_in"], 16)
                    sp.wait_ge(s["moe_done"], 1)
                    for b in range(DB):
                        for pg in range(NPAGE):
                            i = b * NPAGE + pg
                            r = sp.value_load(ptab[0:1, i:i + 1], min_val=0, max_val=79)
                            page = io["cache_mla"][0, bass.ds(r, 1)].rearrange("o p r -> p (o r)")
                            sp.dma_start(nat[:, i, :], page[:, 0:P]).then_inc(s["pages_in"], 16)
                            sp.dma_start(natr[:, 32 * i:32 * i + 32], page[:, P:ROW_W]).then_inc(s["pages_in"], 16)
                load_piece(n)
            spilled_weights(1, len(W))

        @block.gpsimd
        def _(pool):
            step = [0]

            def load(dst, src, signal):
                pool.dma_start(dst, src).then_inc(s[signal], 16)

            def store(dst, src):
                pool.dma_start(dst, src).then_inc(s["stored"], 16)
                n_stored[0] += 1

            def load_ln(i):
                load(lnb[:, 0, :], io["ln_g"][i // 3, i % 3].partition_broadcast(P), "ln_in")
                load(lnb[:, 1, :], io["ln_b"][i // 3, i % 3].partition_broadcast(P), "ln_in")

            n_rstd = [0]

            def power(v):
                n_rstd[0] += 1
                pool.wait_ge(s["var_ready"], n_rstd[0])
                pool.tensor_tensor(v, v, small[0:v.shape[0], 36:36 + v.shape[1]], ALU.pow).then_inc(s["rstd_ready"], 1)

            def norm_gains(i):
                if i % 3 == 2:
                    for t in range(2):
                        outputs_in(i // 3, t)
                pool.wait_ge(s["ln_in"], 32 * (i + 1))
                power(rstd[0:ROWS[0], 0, 0:1])
                for t in range(NT):
                    if t + 1 < NT:
                        power(rstd[0:ROWS[t + 1], (t + 1) % 2, 0:1])
                    if i % 3 == 2 and t + 2 < NT:
                        outputs_in(i // 3, t + 2)
                    n = NT * i + t
                    r = ROWS[t]
                    pool.wait_ge(s["ln_norm"], n + 1)
                    pool.tensor_tensor(x[0:r, t, :], x[0:r, t, :], lnb[0:r, 0, :], ALU.mult).then_inc(s["pool_step"], 1)
                    step[0] += 1
                    pool.wait_ge(s["pool_step"], step[0])
                    pool.tensor_tensor(x[0:r, t, :], x[0:r, t, :], lnb[0:r, 1, :], ALU.add).then_inc(s["x_ready"], 1)

            def outputs_in(l, t):
                if t >= 2:
                    pool.wait_ge(s["combined"], NT * l + t - 1)
                r = ROWS[t]
                for c in range(2):
                    pool.indirect_dma_start(y_of[c][0:r, t % 2, :], None, y_rows[:, :],
                                            bass.IndirectOffsetOnAxis(ap=places[0:r, c, t:t + 1], axis=0)).then_inc(y_in[t % 2], 16)

            def dispatch(l):
                for t in range(NT):
                    pool.dma_start(x_rows[t * P:t * P + ROWS[t], :], x[0:ROWS[t], t, :]).then_inc(s["x_out"], 16)
                pool.wait_ge(s["tokens_in"], 16)
                pool.wait_ge(s["table_out"], 32)
                pool.wait_ge(s["places_ready"], l + 1)
                for t in range(NT):
                    r = ROWS[t]
                    for c in range(2):
                        pool.indirect_dma_start(slot_tokens[:, :], bass.IndirectOffsetOnAxis(ap=places[0:r, c, t:t + 1], axis=0),
                                                tokens[0:r, t:t + 1], None).then_inc(s["scattered"], 16)
                pool.wait_ge(s["scattered"], 16 * 2 * NT * (l + 1))
                load(block_tokens[:, :], slot_tokens.rearrange("(s b) o -> s (b o)", b=NB), "block_tokens_in")
                pool.wait_ge(s["block_tokens_in"], 16 * (l + 1))
                pool.wait_ge(s["x_out"], 16 * NT * (l + 1))

                def rows_in(buf, b, signal):
                    pool.indirect_dma_start(xs[0:CAP, buf, :], None, x_rows[:, :],
                                            bass.IndirectOffsetOnAxis(ap=block_tokens[:, b:b + 1], axis=0)).then_inc(signal, 16)

                for e in range(NE):
                    if e >= 3:
                        full(pool, ("moeX", l, e - 3))
                    rows_in(e % 3, e, xs_in[e % 3])
                sem_ = spill_s[l]
                with spilled(pool, l):
                    full(pool, ("moeX", l, NE - 1))
                    for j in range(SPILL):
                        if j:
                            pool.wait_ge(sem_["pe"], 3 * j)
                        rows_in(0, NE + j, sem_["xs_in"])
                    pool.wait_ge(sem_["y_out"], 16 * SPILL)
                for i in range(2):
                    pool.wait_ge(y_out[i], 16 * NE // 2 * (l + 1))

            load(cosf[:, :], io["c_cos"], "const_in")
            load(sinf[:, :], io["c_sin"], "const_in")
            load(band[:, :], io["c_band"], "const_in")
            load(decay[:, :, :], io["c_decay"], "const_in")
            load(qdec[:, :, :], io["c_qdec"], "const_in")
            load(small[:, :], io["c_small"], "const_in")
            load(rope_t[:, :, :], io["c_rope"], "const_in")
            load(sinkb[:, :], io["sink_by_bank"].partition_broadcast(P), "sink_in")
            load(sinkr[:, :], io["sink_rows"].rearrange("(r o) -> r o", o=1), "sink_in")
            for l in range(DEPTH):
                load(wr[:, l, :, 0:4], io["moe_w_group"][l].rearrange("(k p) n -> p k n", p=P), "router_in")
                load(wr[:, l, :, 4:20], io["moe_w_router"][l].rearrange("(k p) n -> p k n", p=P), "router_in")
                load(rb[:, l, 0:4], io["moe_b_group"][l].partition_broadcast(P), "router_in")
                load(rb[:, l, 4:20], io["moe_b_router"][l].partition_broadcast(P), "router_in")
            load(tokens[:, :], io["c_tokens"], "tokens_in")
            pool.dma_start(slot_tokens.rearrange("(s b) o -> s (b o)", b=NB), io["c_no_tokens"]).then_inc(s["table_out"], 16)
            pool.dma_start(y_rows.rearrange("(s b) d -> s b d", b=NB)[:, NE:, :], io["c_no_row"].to_broadcast([CAP, SPILL, D])
                           ).then_inc(s["table_out"], 16)
            load(ptab[:, :], io["page_table"].rearrange("(o b) g -> o (b g)", o=1), "ptab_in")

            for l in range(DEPTH):
                for m in range(2):
                    taken(pool, ("mkv", l, m))
                    store(mem_k_p[l, 0, m * P:m * P + P].rearrange("s h d -> s (h d)"), mk[:, m, :])
                    store(mem_v_p[l, 0, m * P:m * P + P].rearrange("s h d -> s (h d)"), mv[:, l, m, :])
                pool.wait_ge(s["stored"], 16 * n_stored[0])
                pool.nop().then_inc(s["mk_stored"], 1)

            load(gng[:, 0, :], io["ret_gn_g"][0].partition_broadcast(P), "gn_in")
            load(gng[:, 1, :], io["ret_gn_b"][0].partition_broadcast(P), "gn_in")
            full(pool, ("mkT", 1))
            for dst, name in ((Kw, "cache_swa_k"), (Vw, "cache_swa_v")):
                load(dst[0:127, :, :], io[name][0, :, 1:128].rearrange("b s h d -> s b (h d)"), "cache_in")
            taken(pool, ("va",))
            taken(pool, ("kaTok",))
            for b in range(DB):
                load(Kw[127:128, b, :], sRs[b:b + 1, :], "newk_in")
                load(Vw[127:128, b, :], v_tok[b:b + 1, 4, 0:128], "newk_in")
            store(swa_k_p[0, 0].rearrange("s h d -> s (h d)"), ka_tok[:, :])
            store(swa_v_p[0, 0].rearrange("s h d -> s (h d)"), v_tok[:, 3, 0:128])
            pool.wait_ge(s["cache_in"], 32)
            pool.wait_ge(s["newk_in"], 16 * 16)
            for src, dst in ((Kw, swa_k_s), (Vw, swa_v_s)):
                store(dst[0].rearrange("b s h d -> s b (h d)"), src[:, :, :])
            full(pool, ("swO",))
            for par in range(2):
                for b in range(DB):
                    load(Ss[par * 64:par * 64 + 64, b, :, :],
                         io["state_ret"][0, b].rearrange("(j t) k e -> t k j e", t=2)[par], "state_in")
            pool.wait_ge(s["rope_done"], 14)
            pool.wait_ge(s["const_in"], 16 * 7)
            for n in range(1, 4):
                if n > 1:
                    full(pool, ("retO", n - 1))
                pool.tensor_tensor(qd, qrT[:, :, tile_cols(n)], qdec[:, :, :], ALU.mult).then_inc(s["qd_ready"], 1)
                power(st[:, 16:24])
            power(st[:, 16:24])
            pool.wait_ge(s["qd_ready"], 3)
            load(route[:, :, :], io["c_route"], "route_in")
            full(pool, ("retO", 3))
            for j in range(4):
                if j:
                    full(pool, ("sU", j - 1))
                pool.tensor_tensor(vmk[0:8, :, :], v_tok[0:8, 4, 128 + j * P:256 + j * P].unsqueeze(1).to_broadcast([8, 8, P]),
                                   small[0:8, 24:32].unsqueeze(2).to_broadcast([8, 8, P]), ALU.mult).then_inc(s["vm_ready"], 1)
            power(st[0:8, 16:24])
            taken(pool, ("retU", 3))
            for par in range(2):
                store(ret_p[0, 0].rearrange("(j t) k e -> t k j e", t=2)[par], S[par * 64:par * 64 + 64, :, :])
            taken(pool, ("sU", 3))
            for par in range(2):
                for b in range(DB):
                    store(ret_s[0, b].rearrange("(j t) k e -> t k j e", t=2)[par], Ss[par * 64:par * 64 + 64, b, :, :])
            pool.wait_ge(s["gated_ready"], 5)
            load_ln(0)

            for l in range(DEPTH):
                if l == 1:
                    load(kvg[:, :], io["mla_kv_norm"][0].partition_broadcast(P), "odd_in")
                    pool.dma_start(qg[:, :], io["mla_q_norm"][0].rearrange("(k p) -> p k", p=P),
                                   allow_slow_non_contiguous=True).then_inc(s["odd_in"], 16)
                    for t in range(NT):
                        power(rms[0:ROWS[t], t % 2, 2:4])
                        pool.wait_ge(s["oin_ready"], t + 1)
                        dst = mla_p[0, 0, t * P:t * P + P] if t < 4 else mla_s[0].rearrange("b s r -> (b s) r")
                        store(dst, rows[0:ROWS[t], t, :])
                    full(pool, ("pkT", 1))
                    load_ln(3)
                pool.wait_ge(s["stored"], 16 * n_stored[0])
                norm_gains(3 * l)
                pool.wait_ge(s["x_ready"], NT * (3 * l + 1))
                load_ln(3 * l + 1)
                for b in range(DB):
                    for dst, name, sg in ((Kc, "cache_mem_k", "kc_in"), (Vc, "cache_mem_v", "vc_in")):
                        load(dst[:, b, :, :], io[name][l, b].rearrange("(c p) h d -> p c (h d)", p=P), sg)
                norm_gains(3 * l + 1)
                pool.wait_ge(s["x_ready"], NT * (3 * l + 2))
                load_ln(3 * l + 2)
                dispatch(l)
                norm_gains(3 * l + 2)
                pool.wait_ge(s["x_ready"], NT * (3 * l + 3))
                if l == 0:
                    pool.nop().then_inc(s["moe_done"], 1)
            for t in range(NT):
                dst = y_prompt[0, t * P:t * P + P] if t < 4 else y_sample.rearrange("b s d -> (b s) d")
                store(dst, x[0:ROWS[t], t, :])
            pool.wait_ge(s["stored"], 16 * n_stored[0])

        @block.tensor
        def _(pe):
            def open_(key):
                n = J[key]
                if n >= 4:
                    pe.wait_ge(pair_free[n % 4], n // 4)
                return PS[:, n % 4, :]

            def close(mm, key):
                mm.then_inc(pair_full[J[key] % 4], 1)

            def transpose_x(i):
                for t in range(NT):
                    key = ("xT", i, t)
                    o = open_(key)
                    r = ROWS[t]
                    pe.wait_ge(s["x_loaded"], 16 * NT) if i < 0 else pe.wait_ge(s["x_ready"], NT * i + t + 1)
                    for k in range(KD):
                        mm = pe.transpose(o[:, k * r:k * r + r], x[0:r, t, k * P:k * P + P], ident[0:r, 0:r])
                    close(mm, key)

            def by_feature(key, lhs, rhs, nk, out_rows=slice(0, P), start=True, last=True):
                o = pair(key)
                for k in range(nk):
                    for h in range(2):
                        mm = pe.matmul(o[out_rows, 512 * h:512 * h + HALF], lhs(k), rhs(k)[:, HALF * h:HALF * h + HALF],
                                       start=(k == 0), stop=(k == nk - 1))
                return mm

            def attention(kind, score, apply):
                blocks = BLOCKS[kind]
                base = A0[kind]

                def step_s(i):
                    key = att_key(kind, "S", i)
                    o = open_(key)
                    close(score(i, o, blocks[i]), key)

                def step_t(i):
                    key = att_key(kind, "T", i)
                    o = open_(key)
                    g, w = blocks[i][2:]
                    pe.wait_ge(s["probs_ready"], base + i + 1)
                    b = pbuf[:, (base + i) % 2, :].rearrange("p (g w) -> p g w", g=g)
                    for c in range(w // P):
                        for h in range(g):
                            col = (c * g + h) * P
                            mm = pe.transpose(o[:, col:col + P], b[:, h, c * P:c * P + P], ident[:, :])
                    close(mm, key)

                def step_o(i):
                    key = att_key(kind, "O", i)
                    o = open_(key)
                    taken(pe, att_key(kind, "T", i))
                    g, w = blocks[i][2:]
                    v = pT[:, (base + i) % 2, :].rearrange("p (c g q) -> p c g q", g=g, q=P)
                    close(apply(i, o, blocks[i], v), key)

                steps = {"S": step_s, "T": step_t, "O": step_o}
                for st_, i in pipelined("S", "T", "O", len(blocks)):
                    steps[st_](i)

            pe.wait_ge(s["ident_in"], 16)
            transpose_x(-1)
            mem_tok = arena[:, 2048:4096].rearrange("p (a b) -> p a b", a=2)
            pe.wait_ge(s["mem_loaded"], 16)
            for m in range(2):
                key = ("memT", m)
                o = open_(key)
                for k in range(KD):
                    mm = pe.transpose(o[:, k * P:k * P + P], mem_tok[:, m, k * P:k * P + P], ident[:, :])
                close(mm, key)
            taken(pe, ("memT", 1))
            for l in range(DEPTH):
                for m in range(2):
                    key = ("mkv", l, m)
                    o = open_(key)
                    for c, w in enumerate("kv"):
                        landed(pe, ("m" + w, l))
                        for k in range(KD):
                            mm = pe.matmul(o[:, 512 * c:512 * c + 256], memT[:, k, m * P:m * P + P],
                                           wview(("m" + w, l))[:, k, :], start=(k == 0), stop=(k == KD - 1))
                    close(mm, key)
                key = ("mkT", l)
                o = open_(key)
                taken(pe, ("mkv", l, 1))
                for c in range(2):
                    for m in range(2):
                        mm = pe.transpose(o[:, c * 256 + m * P:c * 256 + m * P + P], mk[:, m, c * P:c * P + P], ident[:, :])
                close(mm, key)

            taken(pe, ("xT", -1, 4))
            xk = lambda k: xT[:, k, :]

            def chunk(key, name, lhs):
                open_(key)
                landed(pe, name)
                close(by_feature(key, lhs, xk, KD), key)

            def plain(name, j):
                w = wview(name)
                return lambda k: w[:, k, j * P:j * P + P]

            def tokens(key, name, tiles, cols):
                o = open_(key)
                landed(pe, name)
                w = wview(name)
                width = cols.stop - cols.start
                for n, t in enumerate(tiles):
                    for k in range(KD):
                        mm = pe.matmul(o[0:ROWS[t], n * width:n * width + width], xT[:, k, tile_cols(t)], w[:, k, cols],
                                       start=(k == 0), stop=(k == KD - 1))
                close(mm, key)

            def chunks(what, i, j):
                name = ("ein", i + j // 2)
                chunk((what, j), name, plain(name, j % 2))

            for j in range(4):
                chunks("qa", 0, j)
            for kv in range(2):
                chunk(("ka", kv), ("ka",), plain(("ka",), kv))
            tokens(("va",), ("va",), range(NT), slice(0, P))
            for what, i in (("qr", 3), ("kr", 5)):
                for j in range(4):
                    chunks(what, i, j)
            for c, what in enumerate(("vr", "g")):
                for i in range(2):
                    name = ("ein", 7 + 2 * c + i)
                    tokens((what, i, 0), name, range(4), slice(0, 256))
                    tokens((what, i, 1), name, range(4, 5), slice(0, 256))

            key = ("kaTok",)
            o = open_(key)
            pe.wait_ge(s["rope_done"], 6)
            for kv in range(2):
                pe.transpose(o[:, 64 * kv:64 * kv + 64], kaD[0:64, kv, 384:512], ident[0:64, 0:64])
                mm = pe.transpose(o[0:8, 128 + 64 * kv:192 + 64 * kv], kaD[0:64, kv, 512:520], ident[0:64, 0:64])
            close(mm, key)
            taken(pe, ("va",))

            def swa_score(i, o, blk):
                n, h0, g, w = blk
                k0 = max(n - 1, 0) * P
                o = o.rearrange("p (g w) -> p g w", g=g)
                for h in (0, 2, 1, 3):
                    b, c = 64 * (h % 2), (h0 + h) // 2
                    mm = pe.matmul(o[:, bank_pos(h), 0:w], qaT[b:b + 64, c, n * P:n * P + P],
                                   kaD[b:b + 64, h0 // 4, k0:k0 + w], start=True, stop=True)
                return mm

            def swa_apply(i, o, blk, v):
                n, h0, g, w = blk
                t0 = max(n - 1, 0)
                for b in range(2):
                    for c in range(w // P):
                        mm = pe.matmul(o[64 * b:64 * b + 64, 0:256], v_tok[:, t0 + c, 16 * h0:16 * h0 + 64],
                                       v[:, c, 2 * b:2 * b + 2, :], start=(c == 0), stop=(c == w // P - 1))
                return mm

            attention("swa", swa_score, swa_apply)

            pe.wait_ge(s["cache_in"], 32)
            pe.wait_ge(s["newk_in"], 16 * 16)
            key = ("kwT",)
            o = open_(key)
            for b in range(DB):
                mm = pe.transpose(o[:, b * P:b * P + P], Kw[:, b, :], ident[:, :])
            close(mm, key)
            key = ("swS",)
            o = open_(key)
            taken(pe, ("kwT",))
            for kv in range(2):
                for b in range(DB):
                    mm = pe.matmul(o[:, 512 * kv + 4 * b:512 * kv + 4 * b + 4], pbuf[64 * kv:64 * kv + 64, 0, b * P:b * P + P],
                                   qas[64 * kv:64 * kv + 64, :, b], start=True, stop=True)
            close(mm, key)
            n_rows = [0]

            def to_rows(key, src, count, chunks):
                o = open_(key)
                for c in range(chunks):
                    mm = pe.transpose(o[0:count, c * P:c * P + P], src[:, c, :], ident[:, :])
                close(mm, key)

            def from_rows(key, src, count, chunks, new=0):
                o = open_(key)
                n_rows[0] += 1
                pe.wait_ge(s["row_probs"], n_rows[0])
                for c in range(chunks):
                    mm = pe.transpose(o[:, c * count:c * count + count], src[0:count, c * P:c * P + P],
                                      ident[0:count, 0:count])
                if new:
                    mm = pe.transpose(o[0:new, 512:512 + count], src[0:count, chunks * P:chunks * P + new],
                                      ident[0:count, 0:count])
                close(mm, key)

            taken(pe, ("swS",))
            to_rows(("swR",), sTs.unsqueeze(1), 64, 1)
            from_rows(("swT",), sRs, 64, 1)
            key = ("swO",)
            o = open_(key)
            taken(pe, ("swT",))
            for kv in range(2):
                for b in range(DB):
                    for h in range(2):
                        c0 = 8 * b + 4 * kv + h
                        mm = pe.matmul(o[64 * h:64 * h + 64, 16 * kv + b:16 * kv + b + 9:8],
                                       Vw[:, b, 64 * kv:64 * kv + 64], pTs_sw[:, c0:c0 + 3:2], start=True, stop=True)
            close(mm, key)

            pe.wait_ge(s["rope_done"], 14)
            taken(pe, ("vr", 1, 1))

            def ret_gated(n):
                key = ("retG", n)
                o = open_(key)
                r = ROWS[n]
                pe.wait_ge(s["gated_ready"], n + 1)
                for j in range(4):
                    mm = pe.transpose(o[:, j * r:j * r + r], o_t[0:r, n % 2, j * P:j * P + P], ident[0:r, 0:r])
                close(mm, key)

            for n in range(4):
                cols = tile_cols(n)
                key = ("retS", n)
                o = open_(key)
                for h in (0, 2, 4, 6, 1, 3, 5, 7):
                    b, c = 64 * (h % 2), h // 2
                    k = 512 * (h % 2) + c * P
                    mm = pe.matmul(o[:, k:k + P], krT[b:b + 64, c, cols], qrT[b:b + 64, c, cols], start=True, stop=True)
                close(mm, key)
                key = ("retK", n)
                o = open_(key)
                for c in range(4):
                    mm = pe.transpose(o[:, c * P:c * P + P], krT[:, c, cols], ident[:, :])
                close(mm, key)
                key = ("retO", n)
                o = open_(key)
                taken(pe, ("retS", n))
                if n:
                    taken(pe, ("retU", n - 1))
                    pe.wait_ge(s["qd_ready"], n)
                for h in (0, 2, 4, 6, 1, 3, 5, 7):
                    b, c = 64 * (h % 2), h // 2
                    k = 512 * (h % 2) + 64 * c
                    mm = pe.matmul(o[:, k:k + 64], retP[:, 4 * (h % 2) + c, :], v_tok[:, n, 128 + 64 * h:192 + 64 * h],
                                   start=True, stop=(n == 0))
                    if n:
                        mm = pe.matmul(o[:, k:k + 64], qd[b:b + 64, c, :], S[b:b + 64, c, :], start=False, stop=True)
                close(mm, key)
                key = ("retU", n)
                o = open_(key)
                taken(pe, ("retK", n))
                for c in range(4):
                    mm = pe.matmul(o[:, c * P:c * P + P], kd[:, c * P:c * P + P], v_tok[:, n, 128 + c * P:256 + c * P],
                                   start=True, stop=True)
                close(mm, key)
                if n:
                    ret_gated(n - 1)

            key = ("skT",)
            o = open_(key)
            for c in range(4):
                mm = pe.transpose(o[0:8, c * P:c * P + P], krT[:, c, 512:520], ident[:, :])
            close(mm, key)
            ret_gated(3)
            taken(pe, ("skT",))
            for j in range(4):
                key = ("sU", j)
                o = open_(key)
                pe.wait_ge(s["vm_ready"], j + 1)
                for h in range(2):
                    mm = pe.matmul(o[:, 512 * h:512 * h + 512], ks_tok[0:8, j * P:j * P + P],
                                   vmk[0:8, 4 * h:4 * h + 4, :], start=True, stop=True)
                close(mm, key)
            key = ("sO",)
            o = open_(key)
            taken(pe, ("sU", 3))
            for b in range(DB):
                for h in range(8):
                    q, c = 64 * (h % 2), h // 2
                    mm = pe.matmul(o[q:q + 64, c * 8 + b:c * 8 + b + 1], Ss[q:q + 64, b, c, :],
                                   qrT[q:q + 64, c, 512 + b:513 + b], start=True, stop=True)
            close(mm, key)
            key = ("sOt",)
            o = open_(key)
            taken(pe, ("sO",))
            for c in range(4):
                mm = pe.transpose(o[0:8, c * P:c * P + P], soT[:, c, :], ident[:, :])
            close(mm, key)
            ret_gated(4)

            def out_proj(i, pieces, last):
                taken(pe, last)
                for t in range(NT):
                    key = ("y", i, t)
                    o = open_(key)
                    for h in range(2):
                        for n, name in enumerate(pieces):
                            landed(pe, name)
                            w = wview(name)
                            for k in range(2):
                                mm = pe.matmul(o[0:ROWS[t], 512 * h:512 * h + 512], oT[:, 2 * n + k, tile_cols(t)],
                                               w[:, k, 512 * h:512 * h + 512], start=(n == 0 and k == 0),
                                               stop=(n == len(pieces) - 1 and k == 1))
                    close(mm, key)

            def cross_attention(l):
                taken(pe, ("xT", 3 * l, 4))
                for j in range(2):
                    key = ("mq", l, j)
                    open_(key)
                    landed(pe, ("mq", l))
                    w = wview(("mq", l))
                    close(by_feature(key, lambda k: w[:, k, j * P:j * P + P], xk, KD), key)
                taken(pe, ("mq", l, 1))

                def score(i, o, blk):
                    n = blk[0]
                    for h in (0, 2, 1, 3):
                        b, c = 64 * (h % 2), h // 2
                        k = 256 * bank_pos(h)
                        mm = pe.matmul(o[:, k:k + 256], qmT[b:b + 64, c, n * P:n * P + P],
                                       mkT[b:b + 64, l, c, :], start=True, stop=True)
                    return mm

                def apply(i, o, blk, v):
                    for h in range(4):
                        for c in range(2):
                            mm = pe.matmul(o[64 * (h % 2):64 * (h % 2) + 64, (h // 2) * P:(h // 2) * P + P],
                                           mv[:, l, c, 64 * h:64 * h + 64], v[:, c, bank_pos(h), :], start=(c == 0), stop=(c == 1))
                    return mm

                attention(f"mem{l}", score, apply)

                def sample_scores(g):
                    key = ("msS", l, g)
                    o = open_(key)
                    taken(pe, ("kcT", l, g))
                    for bb in range(2):
                        for c in range(2):
                            for h in range(4):
                                q, hc = 64 * (h % 2), h // 2
                                col = 512 * (h % 2) + c * 4 + bb * 2 + hc
                                mm = pe.matmul(o[:, col:col + 1], KcT[q:q + 64, g % 2, bb, hc, c * P:c * P + P],
                                               qmT[q:q + 64, hc, 512 + 2 * g + bb:513 + 2 * g + bb], start=True, stop=True)
                    close(mm, key)

                pe.wait_ge(s["kc_in"], 16 * DB * (l + 1))
                for g in range(4):
                    key = ("kcT", l, g)
                    o = open_(key)
                    for bb in range(2):
                        for hc in range(2):
                            for c in range(2):
                                col = bb * 512 + hc * 256 + c * P
                                mm = pe.transpose(o[:, col:col + P], Kc[:, 2 * g + bb, c, hc * P:hc * P + P], ident[:, :])
                    close(mm, key)
                    if g:
                        sample_scores(g - 1)
                sample_scores(3)
                taken(pe, ("msS", l, 3))
                to_rows(("msR", l), sTm, 32, 2)
                from_rows(("msT", l), sRm, 32, 2)
                key = ("msO", l)
                o = open_(key)
                taken(pe, ("msT", l))
                pe.wait_ge(s["vc_in"], 16 * DB * (l + 1))
                for b in range(DB):
                    for h in range(4):
                        for c in range(2):
                            mm = pe.matmul(o[64 * (h % 2):64 * (h % 2) + 64, 8 * (h // 2) + b:8 * (h // 2) + b + 1],
                                           Vc[:, b, c, 64 * h:64 * h + 64], pTm[:, c, 4 * b + h:4 * b + h + 1],
                                           start=(c == 0), stop=(c == 1))
                close(mm, key)
                out_proj(3 * l + 1, [("mo", l)], ("msO", l))

            def experts(l):
                key = ("rt", l)
                o = open_(key)
                taken(pe, ("xT", 3 * l + 1, 4))
                pe.wait_ge(s["router_in"], 16 * 8)
                for t in range(NT):
                    for k in range(KD):
                        mm = pe.matmul(o[0:ROWS[t], t * 32:t * 32 + 20], xT[:, k, tile_cols(t)], wr[:, l, k, :],
                                       start=(k == 0), stop=(k == KD - 1))
                close(mm, key)
                key = ("rank", l)
                o = open_(key)
                pe.wait_ge(s["route_in"], 16)
                pe.wait_ge(s["picks_ready"], l + 1)
                for t in range(NT + 1):
                    for u in range(min(t + 1, NT)):
                        r = ROWS[u]
                        mm = pe.matmul(o[:, 16 * t:16 * t + 16], route[0:r, 0 if u == t else 1, :], picked[0:r, u, :],
                                       start=(u == 0), stop=(u == min(t, NT - 1)))
                close(mm, key)

                def rows_to_features(o, src):
                    for k in range(KD):
                        col = 512 * (k // 4) + CAP * (k % 4)
                        mm = pe.transpose(o[:, col:col + CAP], src[0:CAP, k * P:k * P + P], ident[0:CAP, 0:CAP])
                    return mm

                def hidden(o, w, xT_):
                    for c in range(4):
                        col = 512 * (c // 2) + CAP * (c % 2)
                        for k in range(KD):
                            mm = pe.matmul(o[:, col:col + CAP], w(k)[:, c * P:c * P + P], xT_[:, k, :], start=(k == 0), stop=(k == KD - 1))
                    return mm

                def output(o, w, a):
                    for h in range(2):
                        for c in range(2):
                            mm = pe.matmul(o[0:CAP, 512 * h:512 * h + 512], a[:, c, :], w[:, c, 512 * h:512 * h + 512],
                                           start=(c == 0), stop=(c == 1))
                    return mm

                def step_x(e):
                    key = ("moeX", l, e)
                    o = open_(key)
                    pe.wait_ge(xs_in[e % 3], 16 * uses(NE, 3, l, e))
                    close(rows_to_features(o, xs[:, e % 3, :]), key)

                def step_h(e):
                    key = ("moeH", l, e)
                    o = open_(key)
                    taken(pe, ("moeX", l, e))
                    for c in range(2):
                        landed(pe, ("wi", l, e, c))
                    w = [wview(("wi", l, e, c)) for c in range(2)]
                    close(hidden(o, lambda k: w[k // 4][:, k % 4, :], xsT[:, e % 2, :, :]), key)

                def step_y(e):
                    key = ("moeY", l, e)
                    o = open_(key)
                    landed(pe, ("wo", l, e))
                    taken(pe, ("moeH", l, e))
                    close(output(o, wview(("wo", l, e)), actT[:, e % 2, :, :]), key)

                steps = {"X": step_x, "H": step_h, "Y": step_y}
                for st_, e in expert_order():
                    steps[st_](e)

                sem_ = spill_s[l]
                with spilled(pe, l):
                    for e in range(NE - 3, NE):
                        taken(pe, ("moeY", l, e))
                    taken(pe, ("moeH", l, NE - 1))
                    win = ring[:, 0:2, :].rearrange("p a (k n) -> p (a k) n", n=512)
                    for j in range(SPILL):
                        pe.wait_ge(sem_["xs_in"], 16 * (j + 1))
                        rows_to_features(PS[:, 0, :], xs[:, 0, :]).then_inc(sem_["pe"], 1)
                        pe.wait_ge(sem_["act"], 3 * j + 1)
                        pe.wait_ge(sem_["weights_in"], 32 * (j + 1))
                        hidden(PS[:, 1, :], lambda k: win[:, k, :], xsT[:, 0, :, :]).then_inc(sem_["pe"], 1)
                        pe.wait_ge(sem_["dve"], 4 * (j + 1))
                        if j:
                            pe.wait_ge(sem_["act"], 3 * j)
                        output(PS[:, 2, :], ring[:, 2, :].rearrange("p (k n) -> p k n", k=2), actT[:, 0, :, :]).then_inc(sem_["pe"], 1)

            def latent_attention():
                taken(pe, ("xT", 2, 4))
                key = ("ukT",)
                o = open_(key)
                landed(pe, ("uk",))
                for c in range(4):
                    mm = pe.transpose(o[:, c * P:c * P + P], wview(("uk",))[:, c * P:c * P + P], ident[:, :])
                close(mm, key)

                def oin_back(t):
                    key = ("oinT", t)
                    o = open_(key)
                    r = ROWS[t]
                    pe.wait_ge(s["oin_ready"], t + 1)
                    for c, src in enumerate((cqn[0:r, t % 2, 0:P], cqn[0:r, t % 2, P:2 * P], rows[0:r, t, 0:P], kr4[0:r, t % 2, :])):
                        mm = pe.transpose(o[:, c * P:c * P + r], src, ident[0:r, 0:r])
                    close(mm, key)

                for t in range(NT):
                    key = ("oin", t)
                    o = open_(key)
                    for c in range(2):
                        landed(pe, ("oin", c))
                        for k in range(4):
                            mm = pe.matmul(o[0:ROWS[t], 0:416], xT[:, 4 * c + k, tile_cols(t)], wview(("oin", c))[:, k, :],
                                           start=(c == 0 and k == 0), stop=(c == 1 and k == 3))
                    close(mm, key)
                    if t:
                        oin_back(t - 1)
                oin_back(4)
                taken(pe, ("oinT", 4))
                landed(pe, ("uq",))
                uq = wview(("uq",))
                cqk = lambda k: cqT[:, k, :]
                for j in range(4):
                    key = ("qn", j)
                    open_(key)
                    close(by_feature(key, lambda k: uq[:, k, j * P:j * P + P], cqk, 2), key)

                def q_rope(t):
                    key = ("qrope", t)
                    o = open_(key)
                    for k in range(2):
                        mm = pe.matmul(o[0:ROWS[t], 0:256], cqT[:, k, tile_cols(t)], uq[:, k, 512:768],
                                       start=(k == 0), stop=(k == 1))
                    close(mm, key)

                def q_rope_back(t):
                    key = ("qrT", t)
                    o = open_(key)
                    pe.wait_ge(s["qrtok_ready"], t + 1)
                    if t < 4:
                        for c in range(2):
                            mm = pe.transpose(o[:, c * P:c * P + P], qr_tok[:, t % 2, c * P:c * P + P], ident[:, :])
                    else:
                        for h in range(8):
                            mm = pe.transpose(o[:, 8 * h:8 * h + 8], qr_rep[0:8, h, :], ident[0:8, 0:8])
                    close(mm, key)

                q_rope(0)
                taken(pe, ("ukT",))
                taken(pe, ("qn", 2))
                taken(pe, ("qn", 3))
                for h in range(8):
                    key = ("ql", h)
                    open_(key)
                    b, c = 64 * (h % 2), h // 2
                    close(by_feature(key, lambda k: ukT[b:b + 64, c, :], lambda k: qnT[b:b + 64, c, :], 1), key)
                for t in range(1, NT):
                    q_rope(t)
                    q_rope_back(t - 1)
                q_rope_back(4)
                taken(pe, ("qrT", 4))
                taken(pe, ("ql", 6))
                taken(pe, ("ql", 7))

                def score(i, o, blk):
                    n, h0, g, w = blk
                    o = o.rearrange("p (g w) -> p g w", g=g)
                    for h in range(h0, h0 + g):
                        b, c = 32 * (h % 4), h // 4
                        pe.matmul(o[:, h - h0, 0:w], q_lat[:, h, n * P:n * P + P], ckvT[:, 0:w], start=True, stop=False)
                        mm = pe.matmul(o[:, h - h0, 0:w], qrT2[b:b + 32, c, n * P:n * P + P], krT4[b:b + 32, 0:w],
                                       start=False, stop=True, **({"tile_position": (b, 0)} if b == 96 else {}))
                    return mm

                def apply(i, o, blk, v):
                    n, h0, g, w = blk
                    for c in range(n + 1):
                        mm = pe.matmul(o[:, 0:g * P], rows[:, c, 0:P], v[:, c, :, :], start=(c == 0), stop=(c == n))
                    return mm

                attention("mla", score, apply)

                pe.wait_ge(s["pages_in"], 16 * 128)
                for g in range(2):
                    key = ("pkT", g)
                    o = open_(key)
                    for c in range(8):
                        mm = pe.transpose(o[:, c * P:c * P + P], natr[:, (8 * g + c) * P:(8 * g + c + 1) * P], ident[:, :])
                    close(mm, key)

                def sample_scores(b):
                    key = ("pS", b)
                    o = open_(key)
                    taken(pe, ("pcT", b))
                    taken(pe, ("pkT", 1))
                    for pg in range(NPAGE):
                        pe.matmul(o[:, 8 * pg:8 * pg + 8], ckvp[:, b % 2, pg * P:pg * P + P], qlS[:, b, :],
                                  start=True, stop=False)
                        mm = pe.matmul(o[:, 8 * pg:8 * pg + 8], krp[:, 2 * b + pg // 4, :], qrS[:, pg % 4, b, :],
                                       start=False, stop=True)
                    close(mm, key)

                for b in range(DB):
                    key = ("pcT", b)
                    o = open_(key)
                    for pg in range(NPAGE):
                        mm = pe.transpose(o[:, pg * P:pg * P + P], nat[:, 8 * b + pg, 0:P], ident[:, :])
                    close(mm, key)
                    if b:
                        sample_scores(b - 1)
                sample_scores(7)
                taken(pe, ("pS", 7))
                to_rows(("pR",), sTp, 64, 8)
                key = ("pN",)
                o = open_(key)
                pe.matmul(o[0:64, 0:8], qlS.rearrange("p b h -> p (b h)"), ckvT[:, 512:520], start=True, stop=False)
                mm = pe.matmul(o[0:64, 0:8], qrS[0:32, 0, :, :].rearrange("p b h -> p (b h)"), krT4[0:32, 512:520], start=False, stop=True)
                close(mm, key)
                from_rows(("pT",), srow, 64, 8, new=8)
                key = ("pO",)
                o = open_(key)
                taken(pe, ("pT",))
                pe.matmul(o[:, 0:64], rows[0:8, 4, 0:P], pTn[0:8, :], start=True, stop=False, skip_group_check=True)
                for b in range(DB):
                    for pg in range(NPAGE):
                        mm = pe.matmul(o[:, 8 * b:8 * b + 8], nat[:, 8 * b + pg, 0:P], pTp[:, pg, 8 * b:8 * b + 8],
                                       start=False, stop=(b == DB - 1 and pg == NPAGE - 1), skip_group_check=True)
                close(mm, key)
                taken(pe, ("pO",))
                landed(pe, ("uv",))
                for j in range(4):
                    key = ("uv", j)
                    open_(key)
                    for q in range(2):
                        h = 2 * j + q
                        mm = by_feature(key, lambda k: wview(("uv",))[:, 64 * h:64 * h + 64], lambda k: ctxT[:, h, :], 1,
                                        out_rows=slice(64 * q, 64 * q + 64))
                    close(mm, key)

            out_proj(0, [("out", 0, i) for i in range(4)], ("retG", 4))
            transpose_x(0)
            cross_attention(0)
            transpose_x(1)
            experts(0)
            transpose_x(2)
            latent_attention()
            out_proj(3, [("out", 1, i) for i in range(2)], ("uv", 3))
            transpose_x(3)
            cross_attention(1)
            transpose_x(4)
            experts(1)

        CHUNKS = [(("qa", j), qaT[:, j, :]) for j in range(4)] + [(("ka", j), kaD[:, j, :]) for j in range(2)]
        CHUNKS += [(("qr", j), qrT[:, j, :]) for j in range(4)] + [(("kr", j), krT[:, j, :]) for j in range(4)]

        def halves(ap):
            if ap.shape[1] == 1024:
                return ap.rearrange("p (a b) -> p a b", a=2)[:, :, 0:HALF]
            return ap.rearrange("p (a b) -> p a b", a=2)

        def score_view(kind, i):
            g, w = BLOCKS[kind][i][2:]
            return pair(att_key(kind, "S", i)).rearrange("p (g w) -> p g w", g=g)[:, :, 0:w]

        def prob_view(kind, i):
            g, w = BLOCKS[kind][i][2:]
            return pbuf[:, (A0[kind] + i) % 2, :].rearrange("p (g w) -> p g w", g=g)[:, :, 0:w]

        def gate_views(i, m):
            o = pair(("g", i, m))
            if m == 0:
                return g_s[:, 0:4, 256 * i:256 * i + 256], o.rearrange("p (t n) -> p t n", t=4)
            return g_s[0:8, 4, 256 * i:256 * i + 256], o[0:8, 0:256]

        @block.scalar
        def _(act):
            def copy(dst, src):
                return act.activation(dst, src, ACT.Copy)

            def take(key, dst, src):
                full(act, key)
                free(copy(dst, src(pair(key)) if callable(src) else src), key)

            def take_xT(i):
                for t in range(NT):
                    r = ROWS[t]
                    take(("xT", i, t), xT[:, :, tile_cols(t)], lambda o: o[:, 0:KD * r].rearrange("p (k q) -> p k q", k=KD))

            take_xT(-1)
            for m in range(2):
                take(("memT", m), memT[:, :, m * P:m * P + P], lambda o: o.rearrange("p (k q) -> p k q", k=KD))
            for l in range(DEPTH):
                if l:
                    act.wait_ge(s["mk_stored"], 1)
                for m in range(2):
                    key = ("mkv", l, m)
                    full(act, key)
                    copy(mk[:, m, :], pair(key)[:, 0:256])
                    free(copy(mv[:, l, m, :], pair(key)[:, 512:768]), key)
                take(("mkT", l), mkT[:, l, :, :], lambda o: o[:, 0:512].rearrange("p (c q) -> p c q", c=2))

            def swap(i):
                key = CHUNKS[i][0]
                full(act, key)
                if i >= 2:
                    act.wait_ge(s["rope_done"], i - 1)
                for q in range(4):
                    a, b = 32 * q, 32 * (q ^ 1)
                    ins = copy(halves(swapb[a:a + 32, i % 2, :]), halves(pair(key)[b:b + 32, :]))
                ins.then_inc(s["swapped"], 1)

            for i in range(6):
                swap(i)
            key = ("va",)
            full(act, key)
            copy(v_tok[:, 0:4, 0:P], pair(key)[:, 0:512].rearrange("p (t n) -> p t n", t=4))
            free(copy(v_tok[0:8, 4, 0:P], pair(key)[0:8, 512:640]), key)
            for i in range(6, 14):
                swap(i)
            for i in range(2):
                take(("vr", i, 0), v_tok[:, 0:4, P + 256 * i:P + 256 * i + 256], lambda o: o.rearrange("p (t n) -> p t n", t=4))
                take(("vr", i, 1), v_tok[0:8, 4, P + 256 * i:P + 256 * i + 256], lambda o: o[0:8, 0:256])
            for i in range(2):
                for m in range(2):
                    key = ("g", i, m)
                    full(act, key)
                    g, o = gate_views(i, m)
                    act.activation(g, o, ACT.Exp, scale=-1.0).then_inc(s["g_exp"], 1)

            key = ("kaTok",)
            full(act, key)
            copy(ka_tok[:, :], pair(key)[:, 0:P])
            free(copy(sRs[0:8, :], pair(key)[0:8, P:2 * P]), key)

            def attention(kind):
                base = A0[kind]
                blocks = BLOCKS[kind]

                def exps(i):
                    n = base + i
                    g = blocks[i][2]
                    act.wait_ge(s["negmax_ready"], n + 1)
                    if kind == "swa":
                        act.activation(sinke[:, n % 2, :], sinke[:, n % 2, :], ACT.Exp)
                    for h in range(g):
                        ins = act.activation(prob_view(kind, i)[:, h, :], score_view(kind, i)[:, h, :], ACT.Exp,
                                             bias=negmax[:, n % 2, h:h + 1], scale=SCALE[kind],
                                             accum_out=rowsum[:, n % 2, h:h + 1])
                    free(ins, att_key(kind, "S", i))

                def outputs(i):
                    n, h0, g, w = blocks[i]
                    cols = g * w
                    take(att_key(kind, "T", i), pT[:, (base + i) % 2, 0:cols], lambda o: o[:, 0:cols])
                    if kind == "mla":
                        take(att_key(kind, "O", i), ctxT[:, h0:h0 + g, tile_cols(n)],
                             lambda o: o[:, 0:g * P].rearrange("p (g q) -> p g q", g=g))
                    else:
                        take(att_key(kind, "O", i), oT[:, h0 // 2:h0 // 2 + 2, tile_cols(n)],
                             lambda o: o[:, 0:256].rearrange("p (c q) -> p c q", c=2))

                exps(0)
                for i in range(len(blocks)):
                    if i + 1 < len(blocks):
                        exps(i + 1)
                    outputs(i)

            n_rows = [0]

            def row_exps(dst, count, w, scale, sink):
                n_rows[0] += 1
                act.wait_ge(s["row_neg"], n_rows[0])
                if sink:
                    act.activation(st[0:count, 27:28], st[0:count, 27:28], ACT.Exp)
                act.activation(dst[0:count, 0:w], dst[0:count, 0:w], ACT.Exp, bias=st[0:count, 26:27], scale=scale,
                               accum_out=st[0:count, 28:29]).then_inc(s["row_exp"], 1)

            attention("swa")
            for kv in range(2):
                for h in range(2):
                    copy(qas[64 * kv:64 * kv + 64, h::2, :], qaT[64 * h:64 * h + 64, 2 * kv:2 * kv + 2, 512:520])
            take(("kwT",), pbuf[:, 0, :], lambda o: o)
            take(("swS",), sTs.rearrange("p (b k h) -> p k b h", b=8, k=2),
                 lambda o: o.rearrange("p (k n) -> p k n", k=2)[:, :, 0:32].rearrange("p k (b h) -> p k b h", b=8))
            row_exps(sRs, 64, P, 0.125, True)
            take(("swT",), pTs_sw, lambda o: o[:, 0:64])
            take(("swO",), oT[:, 0:4, 512:520], lambda o: o[:, 0:32].rearrange("p (c b) -> p c b", c=4))

            def take_gated(n):
                r = ROWS[n]
                take(("retG", n), oT[:, 4:8, tile_cols(n)], lambda o: o[:, 0:4 * r].rearrange("p (c q) -> p c q", c=4))

            for n in range(3):
                take_gated(n)
            full(act, ("skT",))
            free(act.activation(ks_tok[0:8, :], pair(("skT",))[0:8, 0:512], ACT.Copy, scale=0.125), ("skT",))
            take_gated(3)
            take(("sO",), soT, lambda o: o[:, 0:32].rearrange("p (c b) -> p c b", c=4))
            take_gated(4)

            def cross_attention(l):
                for j in range(2):
                    take(("mq", l, j), halves(qmT[:, j, :]), halves)
                attention(f"mem{l}")

                def take_scores(g):
                    key = ("msS", l, g)
                    full(act, key)
                    for q in range(2):
                        dst = sTm[:, :, 8 * g:8 * g + 8].rearrange("p c (b x q) -> p q c b x", b=2, q=2)[:, q]
                        ins = copy(dst, pair(key)[:, 512 * q:512 * q + 8].rearrange("p (c b x) -> p c b x", c=2, b=2))
                    free(ins, key)

                for g in range(4):
                    take(("kcT", l, g), KcT[:, g % 2, :, :, :], lambda o: o.rearrange("p (a b c) -> p a b c", a=2, b=2))
                    if g:
                        take_scores(g - 1)
                take_scores(3)
                row_exps(sRm, 32, 256, 0.125, False)
                take(("msT", l), pTm, lambda o: o[:, 0:64].rearrange("p (c r) -> p c r", c=2))
                take(("msO", l), oT[:, 0:2, 512:520], lambda o: o[:, 0:16].rearrange("p (c b) -> p c b", c=2))

            def experts(l):
                for n in range(2):
                    act.wait_ge(s["router_neg"], 2 * l + n + 1)
                    v = (rA, rs[:, 5:6, :])[n]
                    act.activation(v, v, ACT.Exp).then_inc(s["router_exp"], 1)

                def features(o):
                    return o.rearrange("p (a n) -> p a n", a=2)[:, :, 0:4 * CAP].rearrange("p a (k q) -> p a k q", k=4)

                def xsT_of(i):
                    return xsT[:, i, :, :].rearrange("p (a k) q -> p a k q", a=2)

                def step_x(e):
                    if e >= 2:
                        full(act, ("moeH", l, e - 2))
                    take(("moeX", l, e), xsT_of(e % 2), features)

                def step_h(e):
                    key = ("moeH", l, e)
                    full(act, key)
                    if e >= 2:
                        taken(act, ("moeH", l, e - 2))
                    act.activation(ex[:, e % 2, :, :], pair(key)[:, 0:2 * CAP].rearrange("p (c q) -> p c q", c=2), ACT.Exp, scale=-1.0
                                   ).then_inc(s["moe_exp"], 1)

                def step_y(e):
                    key = ("moeY", l, e)
                    if e >= 2:
                        act.wait_ge(y_out[e % 2], 16 * uses(NE, 2, l, e - 2))
                    take(key, ybuf[0:CAP, e % 2, :], lambda o: o[0:CAP, :])
                    taken(act, key)
                    act.dma_start(y_rows.rearrange("(s b) d -> s b d", b=NB)[:, e, :], ybuf[0:CAP, e % 2, :]).then_inc(y_out[e % 2], 16)

                steps = {"X": step_x, "H": step_h, "Y": step_y}
                for st_, e in expert_order():
                    steps[st_](e)

                sem_ = spill_s[l]
                with spilled(act, l):
                    act.wait_ge(y_out[0], 16 * uses(NE, 2, l, NE - 2))
                    for j in range(SPILL):
                        act.wait_ge(sem_["pe"], 3 * j + 1)
                        copy(xsT_of(0), features(PS[:, 0, :])).then_inc(sem_["act"], 1)
                        act.wait_ge(sem_["pe"], 3 * j + 2)
                        act.activation(ex[:, 0, :, :], PS[:, 1, 0:2 * CAP].rearrange("p (c q) -> p c q", c=2), ACT.Exp, scale=-1.0
                                       ).then_inc(sem_["act"], 1)
                        act.wait_ge(sem_["pe"], 3 * j + 3)
                        if j:
                            act.wait_ge(sem_["y_out"], 16 * j)
                        copy(ybuf[0:CAP, 0, :], PS[0:CAP, 2, :]).then_inc(sem_["act"], 1)
                        act.wait_ge(sem_["act"], 3 * j + 3)
                        act.dma_start(y_rows.rearrange("(s b) d -> s b d", b=NB)[:, NE + j, :], ybuf[0:CAP, 0, :]
                                      ).then_inc(sem_["y_out"], 16)

                for t in range(NT):
                    r = ROWS[t]
                    act.wait_ge(y_in[t % 2], 32 * uses(NT, 2, l, t))
                    v = y_of[0][0:r, t % 2, :]
                    act.activation(v, v, ACT.Copy, scale=rs[0:r, 8, t:t + 1]).then_inc(s["y_scaled"], 1)

            def latent_attention():
                take(("ukT",), ukT, lambda o: o[:, 0:512].rearrange("p (c q) -> p c q", c=4))
                act.wait_ge(s["odd_in"], 32)

                def back(t):
                    key = ("oinT", t)
                    full(act, key)
                    o = pair(key)
                    r = ROWS[t]
                    for c in range(2):
                        act.activation(cqT[:, c, tile_cols(t)], o[:, c * P:c * P + r], ACT.Copy, scale=qg[:, c:c + 1])
                    copy(ckvT[:, tile_cols(t)], o[:, 2 * P:2 * P + r])
                    free(copy(krT4[:, tile_cols(t)], o[:, 3 * P:3 * P + r]), key)

                for t in range(NT):
                    key = ("oin", t)
                    r = ROWS[t]
                    full(act, key)
                    if t:
                        act.wait_ge(s["sq_done"], t)
                    act.activation(scratch[0:r, 0:256], pair(key)[0:r, 0:256], ACT.Square, accum_out=rms[0:r, t % 2, 0:1])
                    act.activation(scratch[0:r, 256:384], pair(key)[0:r, 256:384], ACT.Square,
                                   accum_out=rms[0:r, t % 2, 1:2]).then_inc(s["sq_done"], 1)
                    if t:
                        back(t - 1)
                back(4)
                for j in (1, 3):
                    take(("qn", j), halves(qnT[:, j, :]), halves)
                for h in (1, 3, 5, 7):
                    take(("ql", h), halves(q_lat[:, h, :]), halves)
                for t in range(4):
                    take(("qrT", t), qrT2[:, :, tile_cols(t)], lambda o: o[:, 0:256].rearrange("p (c q) -> p c q", c=2))
                taken(act, ("ql", 6))
                taken(act, ("ql", 7))
                copy(qlS, q_lat[:, :, 512:520].rearrange("p h b -> p b h"))
                full(act, ("qrT", 4))
                act.wait_ge(s["qrS_zero"], 1)
                for q in range(4):
                    ins = copy(qrS[32 * q:32 * q + 32, q, :, :], pair(("qrT", 4))[32 * q:32 * q + 32, 0:64].rearrange("p (h b) -> p b h", h=8))
                free(ins, ("qrT", 4))
                attention("mla")
                for g in range(2):
                    take(("pkT", g), krp[:, 8 * g:8 * g + 8, :], lambda o: o.rearrange("p (c q) -> p c q", c=8))

                def take_scores(b):
                    take(("pS", b), sTp[:, :, 8 * b:8 * b + 8], lambda o: o[:, 0:64].rearrange("p (g h) -> p g h", g=8))

                for b in range(DB):
                    if b % 2:
                        take(("pcT", b), ckvp[:, b % 2, :], lambda o: o)
                    if b:
                        take_scores(b - 1)
                take_scores(7)
                row_exps(srow, 64, 1032, SCALE["mla"], False)
                full(act, ("pT",))
                copy(pTn[0:8, :], pair(("pT",))[0:8, 512:576])
                take(("pT",), pTp, lambda o: o[:, 0:512].rearrange("p (g r) -> p g r", g=8))
                take(("pO",), ctxT[:, :, 512:520].rearrange("p h b -> p b h"), lambda o: o[:, 0:64].rearrange("p (b h) -> p b h", b=8))
                for j in range(4):
                    take(("uv", j), halves(oT[:, j, :]), halves)

            take_xT(0)
            cross_attention(0)
            take_xT(1)
            experts(0)
            take_xT(2)
            latent_attention()
            take_xT(3)
            cross_attention(1)
            take_xT(4)
            experts(1)

        @block.vector
        def _(dve):
            steps = [0]

            def link(ins):
                ins.then_inc(s["vec_step"], 1)
                steps[0] += 1
                dve.wait_ge(s["vec_step"], steps[0])

            dve.wait_ge(s["const_in"], 16 * 7)
            for i, (key, dst) in enumerate(CHUNKS):
                if i == 6:
                    pass
                full(dve, key)
                dve.wait_ge(s["swapped"], i + 1)
                d = halves(dst)
                free(dve.tensor_tensor(d, halves(pair(key)), halves(cosf[:, :]), ALU.mult), key)
                link(dve.tensor_tensor(swapb[:, i % 2, :], swapb[:, i % 2, :], sinf[:, :], ALU.mult))
                dve.tensor_tensor(dst, dst, swapb[:, i % 2, :], ALU.add).then_inc(s["rope_done"], 1)
            for i in range(2):
                for m in range(2):
                    g, o = gate_views(i, m)
                    dve.wait_ge(s["g_exp"], 2 * i + m + 1)
                    link(dve.tensor_scalar(g, g, 1.0, None, ALU.add))
                    link(dve.reciprocal(g, g))
                    free(dve.tensor_tensor(g, o, g, ALU.mult), ("g", i, m))

            def attention(kind):
                base = A0[kind]
                blocks = BLOCKS[kind]

                def maxima(i):
                    n = base + i
                    m = n % 2
                    t, h0, g, w = blocks[i]
                    full(dve, att_key(kind, "S", i))
                    v = score_view(kind, i)
                    if kind == "swa":
                        link(dve.tensor_tensor(v, v, band[:, 256 - w:256].unsqueeze(1).to_broadcast([P, g, w]), ALU.add))
                    if kind == "mla":
                        d = v[:, :, w - P:w]
                        link(dve.tensor_tensor(d, d, band[:, P:256].unsqueeze(1).to_broadcast([P, g, P]), ALU.add))
                    link(dve.tensor_reduce(rowmax[:, m, 0:g], v, AX.X, ALU.max))
                    if kind == "swa":
                        sk = sinkb[:, h0:h0 + g]
                        link(dve.scalar_tensor_tensor(rowmax[:, m, 0:g], rowmax[:, m, 0:g], SCALE[kind], sk, ALU.mult, ALU.max))
                        dve.tensor_scalar(negmax[:, m, 0:g], rowmax[:, m, 0:g], -1.0, None, ALU.mult)
                        dve.tensor_tensor(sinke[:, m, 0:g], sk, rowmax[:, m, 0:g], ALU.subtract).then_inc(s["negmax_ready"], 1)
                    else:
                        dve.tensor_scalar(negmax[:, m, 0:g], rowmax[:, m, 0:g], -SCALE[kind], None, ALU.mult
                                          ).then_inc(s["negmax_ready"], 1)

                def scale(i):
                    m = (base + i) % 2
                    g = blocks[i][2]
                    taken(dve, att_key(kind, "S", i))
                    rsum = rowsum[:, m, 0:g]
                    if kind == "swa":
                        link(dve.tensor_tensor(rsum, rsum, sinke[:, m, 0:g], ALU.add))
                    link(dve.reciprocal(rsum, rsum))
                    for h in range(g):
                        v = prob_view(kind, i)[:, h, :]
                        ins = dve.tensor_scalar(v, v, rowsum[:, m, h:h + 1], None, ALU.mult)
                    ins.then_inc(s["probs_ready"], 1)

                maxima(0)
                for i in range(len(blocks)):
                    if i + 1 < len(blocks):
                        maxima(i + 1)
                    scale(i)

            n_rows = [0]

            def row_softmax(key, dst, count, w, scale, sink, more=None):
                full(dve, key)
                v = dst[0:count, 0:w]
                w0 = min(w, 1024)
                free(dve.tensor_copy(dst[0:count, 0:w0], pair(key)[0:count, 0:w0]), key)
                if more:
                    full(dve, more)
                    free(dve.tensor_tensor(dst[0:count, w0:w], pair(more)[0:count, 0:w - w0], small[0:count, 16:24], ALU.add), more)
                    taken(dve, more)
                taken(dve, key)
                c = lambda i: st[0:count, i:i + 1]
                link(dve.tensor_reduce(c(24), v, AX.X, ALU.max))
                if sink:
                    link(dve.scalar_tensor_tensor(c(25), c(24), scale, sinkr[:, :], ALU.mult, ALU.max))
                    dve.tensor_scalar(c(26), c(25), -1.0, None, ALU.mult)
                    dve.tensor_tensor(c(27), sinkr[:, :], c(25), ALU.subtract).then_inc(s["row_neg"], 1)
                else:
                    dve.tensor_scalar(c(26), c(24), -scale, None, ALU.mult).then_inc(s["row_neg"], 1)
                n_rows[0] += 1
                dve.wait_ge(s["row_exp"], n_rows[0])
                if sink:
                    link(dve.tensor_tensor(c(28), c(28), c(27), ALU.add))
                link(dve.reciprocal(c(29), c(28)))
                dve.tensor_scalar(v, v, c(29), None, ALU.mult).then_inc(s["row_probs"], 1)

            dve.wait_ge(s["sink_in"], 32)
            attention("swa")
            row_softmax(("swR",), sRs, 64, P, 0.125, True)

            n_rstd = [0]

            def variance(ins):
                ins.then_inc(s["var_ready"], 1)
                n_rstd[0] += 1
                return n_rstd[0]

            def decayed_scores(n):
                full(dve, ("retS", n))
                free(dve.tensor_tensor(retP, pair(("retS", n)).rearrange("p (h q) -> p h q", h=8), decay[:, :, :], ALU.mult), ("retS", n))

            def decayed_keys(n):
                full(dve, ("retK", n))
                free(dve.tensor_tensor(kd.rearrange("p (h e) -> p h e", h=8), pair(("retK", n))[:, 0:512].rearrange("p (h e) -> p h e", h=8),
                                       small[:, 0:8].unsqueeze(2).to_broadcast([P, 8, 64]), ALU.mult), ("retK", n))

            def new_state(n):
                key = ("retU", n)
                full(dve, key)
                u = pair(key)[:, 0:512].rearrange("p (j e) -> p j e", j=4)
                if n == 0:
                    dve.tensor_copy(S[0:64, :, :], u[0:64, :, 0:64])
                    free(dve.tensor_copy(S[64:P, :, :], u[64:P, :, 64:P]), key)
                    return
                taken(dve, ("retU", n - 1))
                link(dve.tensor_tensor(S, S, small[:, 8:12].unsqueeze(2).to_broadcast([P, 4, 64]), ALU.mult))
                dve.tensor_tensor(S[0:64, :, :], u[0:64, :, 0:64], S[0:64, :, :], ALU.add)
                free(dve.tensor_tensor(S[64:P, :, :], u[64:P, :, 64:P], S[64:P, :, :], ALU.add), key)

            def gated(n):
                key = ("retO", n) if n < 4 else ("sOt",)
                r = ROWS[n]
                full(dve, key)
                if n >= 2:
                    full(dve, ("retG", n - 2))
                flat = o_t[0:r, n % 2, :]
                heads = flat.rearrange("p (h e) -> p h e", h=8)
                by_bank = flat.rearrange("p (c q e) -> p q c e", c=4, q=2)
                sqr = o_u[0:r, :].rearrange("p (h e) -> p h e", h=8)
                if n < 4:
                    o = pair(key)[0:r, :].rearrange("p (q n) -> p q n", q=2)[:, :, 0:256].rearrange("p q (c e) -> p q c e", c=4)
                else:
                    o = pair(key)[0:r, 0:512].rearrange("p (c q e) -> p q c e", c=4, q=2)
                mean, var = st[0:r, 8:16], st[0:r, 16:24]
                wide = lambda a: a.unsqueeze(2).to_broadcast([r, 8, 64])
                mean_b = mean.rearrange("p (c q) -> p q c", q=2)
                link(dve.tensor_reduce(mean_b, o, AX.X, ALU.add))
                link(dve.tensor_scalar(mean, mean, 1.0 / 64, None, ALU.mult))
                free(dve.tensor_tensor(by_bank, o, mean_b.unsqueeze(3).to_broadcast([r, 2, 4, 64]), ALU.subtract), key)
                taken(dve, key)
                link(dve.tensor_tensor(sqr, heads, heads, ALU.mult))
                link(dve.tensor_reduce(var, sqr, AX.X, ALU.add))
                dve.wait_ge(s["rstd_ready"], variance(dve.tensor_scalar(var, var, 1.0 / 64, EPS, ALU.mult, ALU.add)))
                link(dve.tensor_tensor(heads, heads, wide(var), ALU.mult))
                link(dve.tensor_tensor(flat, flat, gng[0:r, 0, :], ALU.mult))
                link(dve.tensor_tensor(flat, flat, gng[0:r, 1, :], ALU.add))
                dve.tensor_tensor(flat, flat, g_s[0:r, n, :], ALU.mult).then_inc(s["gated_ready"], 1)

            dve.wait_ge(s["gn_in"], 32)
            taken(dve, ("g", 1, 1))
            for n in range(4):
                decayed_scores(n)
                if n:
                    gated(n - 1)
                decayed_keys(n)
                new_state(n)
            gated(3)
            dve.wait_ge(s["state_in"], 16 * 16)
            for j in range(4):
                key = ("sU", j)
                full(dve, key)
                u = pair(key).rearrange("p (b e) -> p b e", b=DB)
                for q in (0, 64):
                    ins = dve.scalar_tensor_tensor(Ss[q:q + 64, :, j, :], Ss[q:q + 64, :, j, :], small[q:q + 64, 12 + j:13 + j],
                                                   u[q:q + 64, :, q:q + 64], ALU.mult, ALU.add)
                free(ins, key)
            gated(4)

            def norm(i):
                def stats(t):
                    r = ROWS[t]
                    xt = x[0:r, t, :]
                    if i:
                        dve.wait_ge(s["x_ready"], NT * (i - 1) + t + 1)
                    else:
                        dve.wait_ge(s["x_loaded"], 16 * NT)
                    if i % 3 < 2:
                        key = ("y", i, t)
                        full(dve, key)
                        free(dve.scalar_tensor_tensor(xt, xt, ALPHA, pair(key)[0:r, :], ALU.mult, ALU.add), key)
                        taken(dve, key)
                    else:
                        n = NT * (i // 3) + t + 1
                        dve.wait_ge(s["y_scaled"], n)
                        y1, y2 = (y_of[c][0:r, t % 2, :] for c in range(2))
                        link(dve.scalar_tensor_tensor(y1, y2, rs[0:r, 9, t:t + 1], y1, ALU.mult, ALU.add))
                        dve.scalar_tensor_tensor(xt, xt, ALPHA, y1, ALU.mult, ALU.add).then_inc(s["combined"], 1)
                        dve.wait_ge(s["combined"], n)
                    dve.bn_stats(bns[0:r, 0, :], xt[:, 0:512])
                    link(dve.bn_stats(bns[0:r, 1, :], xt[:, 512:1024]))
                    link(dve.bn_aggr(mv_t[0:r, t % 2, :], bns[0:r, :, :]))
                    return variance(dve.tensor_scalar(rstd[0:r, t % 2, 0:1], mv_t[0:r, t % 2, 1:2], EPS, None, ALU.add))

                def normalise(t, n):
                    r = ROWS[t]
                    xt = x[0:r, t, :]
                    dve.wait_ge(s["rstd_ready"], n)
                    dve.tensor_scalar(xt, xt, mv_t[0:r, t % 2, 0:1], rstd[0:r, t % 2, 0:1], ALU.subtract, ALU.mult
                                      ).then_inc(s["ln_norm"], 1)

                n = stats(0)
                for t in range(NT):
                    more = stats(t + 1) if t + 1 < NT else None
                    normalise(t, n)
                    n = more

            def first_max(out, m, v, tmp):
                mb = m.unsqueeze(2).to_broadcast([P, NT, 4])
                io4 = small[:, 32:36].unsqueeze(1).to_broadcast([P, NT, 4])
                link(dve.tensor_tensor(tmp, v, mb, ALU.is_equal))
                link(dve.tensor_tensor(tmp, tmp, io4, ALU.mult))
                link(dve.tensor_reduce(rs[:, 11, :], tmp, AX.X, ALU.min))
                link(dve.tensor_tensor(out, rs[:, 11, :].unsqueeze(2).to_broadcast([P, NT, 4]), io4, ALU.is_equal))

            def router(l):
                key = ("rt", l)
                link(dve.memset(L, 0.0))
                full(dve, key)
                o = pair(key)[:, 0:NT * 32].rearrange("p (t n) -> p t n", t=NT)
                dve.tensor_tensor(L[:, 0:4, :], o[:, 0:4, 0:20], rb[:, l, :].unsqueeze(1).to_broadcast([P, 4, 20]), ALU.add)
                free(dve.tensor_tensor(L[0:8, 4, :], o[0:8, 4, 0:20], rb[0:8, l, :], ALU.add), key)
                taken(dve, key)
                gl = L[:, :, 0:4]
                wide = lambda i: rs[:, i, :].unsqueeze(2).to_broadcast([P, NT, 4])
                link(dve.tensor_reduce(rs[:, 0, :], gl, AX.X, ALU.max))
                first_max(oh, rs[:, 0, :], gl, rB)
                dve.tensor_tensor(rA, gl, wide(0), ALU.subtract).then_inc(s["router_neg"], 1)
                pr = prod.rearrange("p t (g e) -> p t g e", g=4)
                link(dve.tensor_tensor(pr, L[:, :, 4:20].rearrange("p t (g e) -> p t g e", g=4),
                                       oh.unsqueeze(3).to_broadcast([P, NT, 4, 4]), ALU.mult))
                link(dve.tensor_reduce(el4, prod.rearrange("p t (g e) -> p t e g", g=4), AX.X, ALU.add))
                link(dve.tensor_reduce(rs[:, 1, :], el4, AX.X, ALU.max))
                first_max(oh1, rs[:, 1, :], el4, rB)
                link(dve.scalar_tensor_tensor(el4, oh1, NEG, el4, ALU.mult, ALU.add))
                link(dve.tensor_reduce(rs[:, 2, :], el4, AX.X, ALU.max))
                first_max(oh2, rs[:, 2, :], el4, rB)
                dve.tensor_tensor(rs[:, 5, :], rs[:, 2, :], rs[:, 1, :], ALU.subtract).then_inc(s["router_neg"], 1)
                for c, o_c in enumerate((oh1, oh2)):
                    link(dve.tensor_tensor(picks[:, c].rearrange("p t (g e) -> p t g e", g=4), oh.unsqueeze(3).to_broadcast([P, NT, 4, 4]),
                                           o_c.unsqueeze(2).to_broadcast([P, NT, 4, 4]), ALU.mult))
                dve.tensor_tensor(picked, picks[:, 0], picks[:, 1], ALU.add).then_inc(s["picks_ready"], 1)
                dve.wait_ge(s["router_exp"], 2 * l + 2)
                link(dve.tensor_reduce(rs[:, 6, :], rA, AX.X, ALU.add))
                link(dve.scalar_tensor_tensor(rs[:, 7, :], rs[:, 5, :], 1.0, rs[:, 6, :], ALU.add, ALU.mult))
                link(dve.reciprocal(rs[:, 8, :], rs[:, 7, :]))
                link(dve.tensor_tensor(rs[:, 9, :], rs[:, 8, :], rs[:, 5, :], ALU.mult))
                key = ("rank", l)
                full(dve, key)
                o = pair(key)
                iota, steps_ = small[:, 44:44 + NE], small[:, 60:60 + STEPS]
                spills, spills_before, spills_to = (per_e[:, i, :] for i in range(3))
                link(dve.tensor_tensor(more, o[:, 16 * NT:16 * NT + NE].unsqueeze(2).to_broadcast([P, NE, STEPS]),
                                       steps_.unsqueeze(1).to_broadcast([P, NE, STEPS]), ALU.is_gt))
                link(dve.tensor_reduce(spills, more, AX.X, ALU.add))
                link(dve.tensor_tensor(pre, spills.unsqueeze(1).to_broadcast([P, NE, NE]),
                                       route[:, 2:4, :].rearrange("p a (b c) -> p (a b) c", c=NE), ALU.mult))
                link(dve.tensor_reduce(spills_before, pre, AX.X, ALU.add))
                link(dve.tensor_tensor(spills_to, spills_before, spills, ALU.add))
                rank, expert, before, step, blk, place = (pl[:, i] for i in range(6))
                sel_of = lambda v: v.unsqueeze(1).to_broadcast([P, 2 * NT, NE])
                picks_f, sel_f = (v.rearrange("p c t e -> p (c t) e") for v in (picks, sel))
                flat = lambda v: v.rearrange("p c t -> p (c t)")
                for c in range(2):
                    ins = dve.tensor_tensor(sel[:, c], picks[:, c], o[:, 0:16 * NT].rearrange("p (t e) -> p t e", t=NT), ALU.mult)
                free(ins, key)
                taken(dve, key)
                link(dve.tensor_reduce(flat(rank), sel_f, AX.X, ALU.add))
                link(dve.tensor_tensor(sel_f, picks_f, sel_of(iota), ALU.mult))
                link(dve.tensor_reduce(flat(expert), sel_f, AX.X, ALU.add))
                link(dve.tensor_tensor(sel_f, picks_f, sel_of(spills_before), ALU.mult))
                link(dve.tensor_reduce(flat(before), sel_f, AX.X, ALU.add))
                m = more.rearrange("p e s -> p (e s)")[:, 0:2 * NT * STEPS].rearrange("p (n s) -> p n s", s=STEPS)
                link(dve.tensor_tensor(m, flat(rank).unsqueeze(2).to_broadcast([P, 2 * NT, STEPS]),
                                       steps_.unsqueeze(1).to_broadcast([P, 2 * NT, STEPS]), ALU.is_ge))
                link(dve.tensor_reduce(flat(step), m, AX.X, ALU.add))
                link(dve.tensor_tensor(blk, before, step, ALU.add))
                link(dve.scalar_tensor_tensor(blk, blk, float(NE - 1), expert, ALU.add, ALU.subtract))
                link(dve.tensor_scalar(before, step, 1.0, None, ALU.min))
                link(dve.tensor_tensor(blk, blk, before, ALU.mult))
                link(dve.tensor_tensor(blk, blk, expert, ALU.add))
                link(dve.scalar_tensor_tensor(place, step, -float(CAP), rank, ALU.mult, ALU.add))
                link(dve.scalar_tensor_tensor(places[:, :, :], place, float(NB), blk, ALU.mult, ALU.add))
                sel1 = pre.rearrange("p a b -> p (a b)")[0:1, 0:SPILL * NE].rearrange("p (j e) -> p j e", e=NE)
                link(dve.tensor_tensor(sel1, spills_to[0:1, :].unsqueeze(1).to_broadcast([1, SPILL, NE]),
                                       small[0:1, 44:44 + SPILL].unsqueeze(2).to_broadcast([1, SPILL, NE]), ALU.is_le))
                link(dve.tensor_copy(sp_f[0:1, 0:1], spills_to[0:1, NE - 1:NE]))
                link(dve.tensor_reduce(sp_f[0:1, 1:], sel1, AX.X, ALU.add))
                dve.tensor_scalar(spill[:, :], sp_f[0:1, :], float(NE - 1), None, ALU.min).then_inc(s["places_ready"], 1)

            def experts(l):
                router(l)

                def gated_units(o, sg, dst, link=link):
                    a, b = (o[:, 512 * i:512 * i + 2 * CAP].rearrange("p (c q) -> p c q", c=2) for i in range(2))
                    link(dve.tensor_scalar(sg, sg, 1.0, None, ALU.add))
                    link(dve.reciprocal(sg, sg))
                    link(dve.tensor_tensor(sg, a, sg, ALU.mult))
                    return dve.tensor_tensor(dst, b, sg, ALU.mult)

                for e in range(NE):
                    key = ("moeH", l, e)
                    dve.wait_ge(s["moe_exp"], NE * l + e + 1)
                    if e >= 2:
                        full(dve, ("moeY", l, e - 2))
                    free(gated_units(pair(key), ex[:, e % 2, :, :], actT[:, e % 2, :, :]), key)
                sem_ = spill_s[l]

                def link_spilled(ins):
                    ins.then_inc(sem_["dve"], 1)
                    steps_s[0] += 1
                    dve.wait_ge(sem_["dve"], steps_s[0])

                with spilled(dve, l):
                    steps_s = [0]
                    full(dve, ("moeY", l, NE - 1))
                    for j in range(SPILL):
                        dve.wait_ge(sem_["act"], 3 * j + 2)
                        gated_units(PS[:, 1, :], ex[:, 0, :, :], actT[:, 0, :, :], link_spilled).then_inc(sem_["dve"], 1)
                        steps_s[0] += 1

            def latent_attention():
                dve.wait_ge(s["odd_in"], 32)
                dve.memset(qrS, 0.0).then_inc(s["qrS_zero"], 1)
                for t in range(NT):
                    key = ("oin", t)
                    r = ROWS[t]
                    o = pair(key)
                    m = rms[0:r, t % 2, :]
                    tab = rope_t[0:r, t, :]
                    kr = rows[0:r, t, P:ROW_W]
                    tm = tmpm[0:r, 0:32]
                    dve.wait_ge(s["sq_done"], t + 1)
                    dve.tensor_scalar(m[:, 2:3], m[:, 0:1], 1.0 / 256, EPS, ALU.mult, ALU.add)
                    dve.wait_ge(s["rstd_ready"], variance(dve.tensor_scalar(m[:, 3:4], m[:, 1:2], 1.0 / 128, EPS, ALU.mult, ALU.add)))
                    dve.tensor_scalar(cqn[0:r, t % 2, :], o[0:r, 0:256], m[:, 2:3], None, ALU.mult)
                    dve.scalar_tensor_tensor(rows[0:r, t, 0:P], o[0:r, 256:384], m[:, 3:4], kvg[0:r, :], ALU.mult, ALU.mult)
                    dve.tensor_tensor(kr, o[0:r, 384:416], tab[:, 0:32], ALU.mult)
                    dve.tensor_tensor(tm[:, 0:16], o[0:r, 400:416], tab[:, 32:48], ALU.mult)
                    free(dve.tensor_tensor(tm[:, 16:32], o[0:r, 384:400], tab[:, 48:64], ALU.mult), key)
                    taken(dve, key)
                    link(dve.tensor_tensor(kr, kr, tm, ALU.add))
                    dve.tensor_copy(kr4[0:r, t % 2, :].rearrange("p (a b) -> p a b", a=4),
                                    kr.unsqueeze(1).to_broadcast([r, 4, 32])).then_inc(s["oin_ready"], 1)

                def rotate(t):
                    key = ("qrope", t)
                    r = ROWS[t]
                    full(dve, key)
                    if t:
                        dve.wait_ge(s["qrtok_ready"], t)
                    o = pair(key)[0:r, 0:256].rearrange("p (h e) -> p h e", h=8)
                    tab = rope_t[0:r, t, :].unsqueeze(1)
                    q = qr_tok[0:r, t % 2, :].rearrange("p (h e) -> p h e", h=8)
                    u = scratch[0:r, 0:256].rearrange("p (h e) -> p h e", h=8)
                    dve.tensor_tensor(q, o, tab[:, :, 0:32].to_broadcast([r, 8, 32]), ALU.mult)
                    dve.tensor_tensor(u[:, :, 0:16], o[:, :, 16:32], tab[:, :, 32:48].to_broadcast([r, 8, 16]), ALU.mult)
                    free(dve.tensor_tensor(u[:, :, 16:32], o[:, :, 0:16], tab[:, :, 48:64].to_broadcast([r, 8, 16]), ALU.mult), key)
                    taken(dve, key)
                    if t < 4:
                        dve.tensor_tensor(q, q, u, ALU.add).then_inc(s["qrtok_ready"], 1)
                    else:
                        link(dve.tensor_tensor(q, q, u, ALU.add))
                        dve.tensor_copy(qr_rep[0:8, :, :].rearrange("p h (a e) -> p h a e", a=4),
                                        q.unsqueeze(2).to_broadcast([8, 8, 4, 32])).then_inc(s["qrtok_ready"], 1)

                def take(key, dst, src):
                    full(dve, key)
                    free(dve.tensor_copy(dst, src), key)

                for j in (0, 2):
                    take(("qn", j), halves(qnT[:, j, :]), halves(pair(("qn", j))))
                rotate(0)
                for h in (0, 2, 4, 6):
                    take(("ql", h), halves(q_lat[:, h, :]), halves(pair(("ql", h))))
                for t in range(1, NT):
                    rotate(t)
                attention("mla")
                for b in (0, 2, 4, 6):
                    take(("pcT", b), ckvp[:, b % 2, :], pair(("pcT", b)))
                row_softmax(("pR",), srow, 64, 1032, SCALE["mla"], False, more=("pN",))

            norm(0)
            attention("mem0")
            row_softmax(("msR", 0), sRm, 32, 256, 0.125, False)
            norm(1)
            dve.wait_ge(s["router_in"], 16 * 8)
            experts(0)
            norm(2)
            latent_attention()
            norm(3)
            attention("mem1")
            row_softmax(("msR", 1), sRm, 32, 256, 0.125, False)
            norm(4)
            experts(1)
            norm(5)


_INS = ["x_prompt", "x_sample", "mem_prompt", "cache_swa_k", "cache_swa_v", "state_ret", "cache_mla", "page_table",
        "cache_mem_k", "cache_mem_v", "w_in_even", "swa_sink", "ret_gn_g", "ret_gn_b", "w_out_even", "w_in_odd",
        "mla_q_norm", "mla_kv_norm", "w_uq", "w_uk", "w_uv", "w_out_odd", "w_mem_q", "w_mem_k", "w_mem_v", "w_mem_o",
        "moe_w_group", "moe_b_group", "moe_w_router", "moe_b_router", "moe_w_in", "moe_w_out", "ln_g", "ln_b"]
_OUTS = [(1, 512, 1024), (8, 1, 1024), (1, 1, 128, 2, 64), (1, 1, 128, 2, 64), (1, 1, 8, 64, 64), (1, 1, 512, 160),
         (2, 1, 256, 4, 64), (2, 1, 256, 4, 64), (1, 8, 128, 2, 64), (1, 8, 128, 2, 64), (1, 8, 8, 64, 64), (1, 8, 1, 160)]


def kernel(**inputs):
    import numpy as _np
    import concourse.bacc as _bacc
    from concourse import mybir as _mybir
    from concourse.bass_utils import run_bass_kernel_spmd as _run

    nc = _bacc.Bacc("TRN2", target_bir_lowering=False, num_devices=1)
    arrays, io = {}, {}
    given = {name: _np.ascontiguousarray(inputs[name]) for name in _INS}
    w_in, w_uq = given.pop("w_in_even"), given.pop("w_uq")
    given["w_in_even"] = w_in
    given["w_ka_twice"] = _np.ascontiguousarray(w_in[0][:, 512:640].reshape(1024, 2, 1, 64).repeat(2, 2).reshape(1024, 256))
    sink = given.pop("swa_sink")[0]
    given["sink_by_bank"] = _np.ascontiguousarray(sink[[0, 2, 1, 3, 4, 6, 5, 7]])
    given["sink_rows"] = _np.tile(sink, 8)
    per_head = w_uq[0].reshape(256, 8, 96)
    given["w_uq_split"] = _np.concatenate([per_head[:, :, :64].reshape(256, 512), per_head[:, :, 64:].reshape(256, 256)], 1)
    given.update({name: _np.ascontiguousarray(a) for name, a in shape_constants().items()})
    for name, a in given.items():
        arrays[f"in_{name}_dram"] = a
        io[name] = nc.dram_tensor(f"in_{name}_dram", a.shape, _mybir.dt.from_np(a.dtype), kind="ExternalInput").ap()
    outs = [nc.dram_tensor(f"out_{i}_dram", shape, _mybir.dt.float32, kind="ExternalOutput").ap()
            for i, shape in enumerate(_OUTS)]
    decoder_step(nc, io, outs)
    r = _run(nc, [arrays], core_ids=[0])
    return tuple(r.results[0][f"out_{i}_dram"] for i in range(len(_OUTS)))
```

```python
from contextlib import ExitStack

import numpy as np

import concourse.bass as bass
from concourse import mybir

F32 = mybir.dt.float32
I32 = mybir.dt.int32
U32 = mybir.dt.uint32
ALU = mybir.AluOpType
ACT = mybir.ActivationFunctionType
AX = mybir.AxisListType

P = 128
D = 1024
KD = D // P
SEQ = 512
DB = 8
T = SEQ + DB
HALF = T // 2
NT = 5
ROWS = [128, 128, 128, 128, 8]
PAST = 1024
DEPTH = 2
ALPHA = (2 * DEPTH) ** 0.25
EPS = 1e-5
NEG = -1e30
NE = 16
NPAGE = 8
ROW_W = 160
SLOTS = 5
ARENA = 21300
PIECE = 2048
EXTRA_SLOTS = 4
CAP = 96
SPILL = 2 * T // (CAP + 1)
NB = NE + SPILL
SHARE = 4
POOL_GAINS = (0, 2)
STEPS = (T - 1) // CAP
LIMITS, TOKENS, FILLED, IOTA, OWN = 44, 52, 57, 60, 192


def tile_cols(t):
    return slice(t * P, t * P + ROWS[t])


def shape_constants():
    f = np.float32
    pos = np.concatenate([np.arange(SEQ), np.full(DB, PAST)]).astype(f)
    inv64 = (f(10000.0) ** (-np.arange(0, 64, 2, dtype=f) / f(64))).astype(f)
    ang = (pos[None, :] * inv64[:, None]).astype(f)
    cos, sin = np.cos(ang).astype(f), np.sin(ang).astype(f)
    cos_f = np.tile(cos, (4, 1))
    sin_f = np.concatenate([-sin, sin, -sin, sin], 0)
    inv32 = (f(10000.0) ** (-np.arange(0, 32, 2, dtype=f) / f(32))).astype(f)
    ang2 = (pos[:, None] * inv32[None, :]).astype(f)
    c2, s2 = np.cos(ang2).astype(f), np.sin(ang2).astype(f)
    tab = np.zeros((NT * P, 64), f)
    tab[:T] = np.concatenate([c2, c2, -s2, s2], 1)
    rope_t = tab.reshape(NT, P, 64).transpose(1, 0, 2)
    q = np.arange(P)[:, None]
    s = np.arange(2 * P)[None, :]
    band = np.where((q + P - s >= 0) & (q + P - s < P), 0.0, NEG).astype(f)
    h = np.arange(8, dtype=f)
    lg = np.log1p(-np.exp2(f(-5.0) - h)).astype(f)
    by_bank = [0, 2, 4, 6, 1, 3, 5, 7]
    i = np.arange(P, dtype=f)
    diff = i[None, :] - i[:, None]
    decay = np.where(diff[:, None, :] >= 0,
                     np.exp(np.maximum(diff, 0)[:, None, :] * lg[None, :, None]), 0.0) * 0.125
    hp = (2 * np.arange(4)[None, :] + (np.arange(P) // 64)[:, None])
    qdec = np.exp((i[None, None, :] + 1) * lg[hp][:, :, None])
    kdec = np.exp((P - 1 - i)[:, None] * lg[None, :]) * 0.125
    sdec = np.exp(P * lg[hp])
    sdec1 = np.exp(lg[hp])
    vmask = np.eye(8)
    iota4 = np.tile(np.arange(4) - 8.0, (P, 1))
    small = np.zeros((P, 208), f)
    small[:, 0:8] = kdec
    small[:, 8:12] = sdec
    small[:, 12:16] = sdec1
    token = 4 * np.arange(2)[None, :, None] + np.arange(P)[:, None, None] // 32
    small[:, OWN:OWN + 16] = np.where(token == np.arange(DB)[None, None, :], 0.0, NEG).reshape(P, 16)
    small[:8, 24:32] = vmask
    small[:, 32:36] = iota4
    small[:, 36:44] = -0.5
    small[:, IOTA:IOTA + P] = i
    small[:, LIMITS:LIMITS + STEPS] = CAP * np.arange(1, STEPS + 1)
    small[:DB, FILLED] = 1.0
    small[:, TOKENS:TOKENS + NT] = i[:, None] + P * np.arange(NT)[None, :]
    route = np.zeros((P, 4, P), f)
    route[:, 0] = i[:, None] < i[None, :]
    route[:, 1] = 1.0
    before = np.arange(NE)[None, :] < np.arange(NE)[:, None]
    route[:, 2:4] = before.reshape(1, 2, P)
    return {
        "c_ident": np.eye(P, dtype=f),
        "c_cos": cos_f.astype(f), "c_sin": sin_f.astype(f),
        "c_rope": np.ascontiguousarray(rope_t, f),
        "c_band": band,
        "c_decay": np.ascontiguousarray(decay.astype(f)[:, by_bank]), "c_qdec": qdec.astype(f), "c_small": small,
        "c_route": route, "c_no_row": np.zeros((1, 1, D), f),
    }


SWA_BLOCKS = [(n, 4 * kv, 4, 128 if n == 0 else 256) for n in range(4) for kv in range(2)]
MEM_BLOCKS = [(n, 0, 4, 256) for n in range(4)]
MLA_BLOCKS = [(n, h, 2, 128 * (n + 1)) for n in range(4) for h in range(0, 8, 2)]


def pipelined(first, second, third, n):
    out = [(first, 0)] + ([(first, 1)] if n > 1 else [])
    for i in range(n):
        out.append((second, i))
        if i + 2 < n:
            out.append((first, i + 2))
        out.append((third, i))
    return out


SWA_WEAVE = [[("qr", 1)], [("qr", 2)], [("qr", 3)], [("kr", 0)], [("kr", 1)], [("kr", 2)], [("kr", 3)],
             [("vr", 0, 0), ("vr", 0, 1)], []]
SWA_SAMPLE = [("kwT",), ("vr", 1, 0), ("vr", 1, 1), ("swS",), ("g", 0, 0), ("swR",), ("g", 0, 1), ("g", 1, 0), ("swT",),
              ("swO",), ("g", 1, 1)]
RET_SAMPLE = [("skT",), ("y", 0, 0), ("retG", 3), ("sU", 0), ("sU", 1), ("y", 0, 1), ("sU", 2), ("sU", 3), ("y", 0, 2),
              ("sO",), ("sOt",), ("xT", 0, 0), ("y", 0, 3), ("retG", 4), ("xT", 0, 1), ("y", 0, 4),
              ("xT", 0, 2), ("xT", 0, 3), ("xT", 0, 4)]

PAGE_ORDER = [("pcT", 0), ("pcT", 1), ("pS", 0), ("row", 0), ("pcT", 2), ("row", 1), ("pcT", 3), ("row", 2), ("pcT", 4),
              ("row", 3), ("pcT", 5), ("pS", 1), ("row", 4), ("pcT", 6), ("row", 5), ("pT", 0), ("pcT", 7), ("row", 6),
              ("row", 7), ("pTn", 0), ("pO", 0), ("pT", 1), ("pTn", 1), ("pO", 1), ("pOt",)]


def project_and_norm(i):
    order = [("y", i, 0), ("y", i, 1)]
    for t in range(2, NT):
        order += [("y", i, t), ("xT", i, t - 2)]
    return order + [("xT", i, NT - 2), ("xT", i, NT - 1)]


def memory_tail(l):
    i = 3 * l + 1
    y = [("y", i, t) for t in range(NT)]
    x = [("xT", i, t) for t in range(NT)]
    return y[0:2] + [("msT", l), y[2], x[0], ("msO", l), y[3], x[1], y[4], ("rt", l), x[2], x[3], x[4]]


def expert_order():
    out = [("X", 0), ("X", 1), ("H", 0)]
    for e in range(NE):
        out += [("X", e + 2)] if e + 2 < NE else []
        out += [("H", e + 1)] if e + 1 < NE else []
        out += [("Y", e)]
    return out


def woven(order, between):
    out = []
    for step, i in order:
        out.append(("swa" + step, i))
        if (step, i) == ("S", 1):
            out += between[0]
        elif step == "O":
            out += between[i + 1]
    return out


def psum_jobs():
    jobs = []
    jobs += [("xT", -1, t) for t in range(NT)]
    jobs += [("memF", 0, m) for m in range(2)] + [("mkv", 0, m) for m in range(2)] + [("mkT", 0)]
    jobs += [("qa", j) for j in range(4)] + [("ka", 0), ("ka", 1), ("va",)]
    jobs += [("kaTok",), ("qr", 0)]
    jobs += woven(pipelined("S", "T", "O", len(SWA_BLOCKS)), SWA_WEAVE)
    jobs += SWA_SAMPLE
    for n in range(4):
        jobs += [("retS", n), ("retK", n), ("retO", n), ("retU", n)]
        if n:
            jobs += [("retG", n - 1)]
    jobs += RET_SAMPLE
    for l in range(DEPTH):
        if l == 1:
            jobs += [("ukT",)]
            for t in range(NT):
                jobs += [("oin", t)] + ([("oinT", t - 1)] if t else [])
            jobs += [("oinT", 4)]
            jobs += [("qn", j) for j in range(4)]
            jobs += [("qrope", 0)]
            jobs += [("ql", h) for h in range(8)]
            for t in range(NT):
                jobs += ([("qrope", t)] if t else []) + ([("qrT", t - 1)] if t else [])
            jobs += [("qrT", 4)]
            jobs += [("mla" + s, i) for s, i in pipelined("S", "T", "O", len(MLA_BLOCKS))]
            jobs += [("pkT", 0), ("pkT", 1), ("pN",)] + [key for key in PAGE_ORDER if key[0] != "row"]
            jobs += [("uv", j) for j in range(4)]
        if l:
            jobs += project_and_norm(3 * l)
        jobs += [("mq", l, j) for j in range(2)]
        jobs += [("mem" + s, l, i) for s, i in pipelined("S", "T", "O", len(MEM_BLOCKS))]
        jobs += [("kcT", l, 0), ("kcT", l, 1), ("msS", l), ("kcT", l, 2), ("kcT", l, 3)]
        jobs += memory_tail(l)
        if l == 0:
            jobs += [("memF", 1, 0), ("memF", 1, 1), ("rank", l), ("mkv", 1, 0), ("table", l)]
        else:
            jobs += [("rank", l), ("table", l)]
        jobs += [("moe" + s, l, e) for s, e in expert_order()]
        if l == 0:
            jobs += [("mkv", 1, 1), ("mkT", 1)]
        if l == 0:
            jobs += [("xT", 2, t) for t in range(NT)]
    return jobs


def decoder_step(nc, io, outs):
    (y_prompt, y_sample, swa_k_p, swa_v_p, ret_p, mla_p, mem_k_p, mem_v_p,
     swa_k_s, swa_v_s, ret_s, mla_s) = outs

    JOBS = psum_jobs()
    J = {key: n for n, key in enumerate(JOBS)}
    assert len(J) == len(JOBS)

    W = []

    def piece(name, src, shape, last):
        W.append((name, src, shape, last))

    def memory_pieces(l):
        for w in ("k", "v"):
            piece(("m" + w, l), io["w_mem_" + w][l].rearrange("(k p) n -> p k n", p=P), (8, 256), ("mkv", l, 1))

    memory_pieces(0)
    ein_last = [("qa", 1), ("qa", 3), ("va",), ("qr", 1), ("qr", 3), ("kr", 1), ("kr", 3),
                ("vr", 0, 1), ("vr", 1, 1), ("g", 0, 1), ("g", 1, 1)]
    for i, last in enumerate(ein_last):
        if i == 2:
            piece(("ka",), io["w_ka_twice"].rearrange("(k p) n -> p k n", p=P), (8, 256), ("ka", 1))
            piece(("va",), io["w_in_even"][0, :, 640:768].rearrange("(k p) n -> p k n", p=P), (8, 128), last)
            continue
        piece(("ein", i), io["w_in_even"][0, :, 256 * i:256 * i + 256].rearrange("(k p) n -> p k n", p=P), (8, 256), last)
    for l in range(DEPTH):
        if l == 0:
            for i in range(4):
                piece(("out", l, i), io["w_out_even"][0, 256 * i:256 * i + 256].rearrange("(k p) n -> p k n", p=P),
                      (2, 1024), ("y", 0, 4))
        else:
            piece(("uk",), io["w_uk"][0].rearrange("c h n -> c (h n)"), (512,), ("ukT",))
            for i in range(2):
                piece(("oin", i), io["w_in_odd"][0, 512 * i:512 * i + 512].rearrange("(k p) n -> p k n", p=P),
                      (4, 416), ("oin", 4))
            piece(("uq",), io["w_uq_split"].rearrange("(k p) n -> p k n", p=P), (2, 768), ("qrope", 4))
            piece(("uv",), io["w_uv"][0].rearrange("c h n -> c (h n)"), (512,), ("uv", 3))
            for i in range(2):
                piece(("out", l, i), io["w_out_odd"][0, 256 * i:256 * i + 256].rearrange("(k p) n -> p k n", p=P),
                      (2, 1024), ("y", 3, 4))
        piece(("mq", l), io["w_mem_q"][l].rearrange("(k p) n -> p k n", p=P), (8, 256), ("mq", l, 1))
        piece(("mo", l), io["w_mem_o"][l].rearrange("(k p) n -> p k n", p=P), (2, 1024), ("y", 3 * l + 1, 4))
        if l == 0:
            memory_pieces(1)
        for e in range(NE):
            for i in range(2):
                piece(("wi", l, e, i), io["moe_w_in"][l, e, 512 * i:512 * i + 512].rearrange("(k p) n -> p k n", p=P),
                      (4, 512), ("moeH", l, e))
            piece(("wo", l, e), io["moe_w_out"][l, e].rearrange("(k p) n -> p k n", p=P), (2, 1024), ("moeY", l, e))
    WI = {w[0]: n for n, w in enumerate(W)}
    PLACE, held = [], {}
    for n, (name, src, shape, last) in enumerate(W):
        slots = range(SLOTS + EXTRA_SLOTS if name[0] in ("wi", "wo") else SLOTS)
        slot = min(slots, key=lambda q: J[W[held[q][-1]][3]] if q in held else -1)
        before = held.setdefault(slot, [])
        PLACE.append((slot, len(before), before[-1] if before else None))
        before.append(n)

    x_rows = nc.dram_tensor("x_rows", (T, D), F32, kind="Internal").ap()
    y_rows = nc.dram_tensor("y_rows", (CAP * NB, D), F32, kind="Internal").ap()

    with ExitStack() as ctx:
        def sb(name, shape, dt=F32):
            return ctx.enter_context(nc.sbuf_tensor(name, shape, dt))

        def sem(name):
            return ctx.enter_context(nc.semaphore(name))

        PS = ctx.enter_context(nc.psum_tensor("PS", [P, 4, 1024], F32))

        ring = sb("ring", [P, SLOTS, PIECE])
        x = sb("x", [P, NT, D])
        xT = sb("xT", [P, KD, T])
        oT = xT
        ident = sb("ident", [P, P])
        cosf = sb("cosf", [P, T])
        sinf = sb("sinf", [P, T])
        rope_t = sb("rope_t", [P, NT, 64])
        band = sb("band", [P, 256])
        decay = sb("decay", [P, 8, P])
        qdec = sb("qdec", [P, 4, P])
        small = sb("small", [P, 208])
        lnc = sb("lnc", [P, 3 * DEPTH, 2, KD])
        route = qdec
        places = sb("places", [P, 2, NT], U32)
        block_tokens = sb("block_tokens", [CAP, NB], U32)
        spill = sb("spill", [1, 1 + SPILL], I32)
        lnb = sb("lnb", [P, 2, D])
        mkT = sb("mkT", [P, DEPTH, 2, 256])
        mv = sb("mv", [P, DEPTH, 2, 256])
        wr = sb("wr", [P, DEPTH, KD, 20])
        rb = sb("rb", [P, DEPTH, 20])
        ptab = sb("ptab", [1, 64], I32)
        pbuf = sb("pbuf", [P, 2, 1024])
        pT = sb("pT", [P, 2, 1024])
        rowmax = sb("rowmax", [P, 2, 4])
        negmax = sb("negmax", [P, 2, 4])
        rowsum = sb("rowsum", [P, 2, 4])
        sinke = sb("sinke", [P, 2, 4])
        sinkb = sb("sinkb", [P, 8])
        sinkr = sb("sinkr", [64, 1])
        st = sb("st", [P, 32])
        bns = sb("bns", [P, 2, 6])
        mv_t = sb("mv_t", [P, 2, 2])
        rstd = sb("rstd", [P, 2, 1])
        rms = sb("rms", [P, 2, 4])
        arena = sb("arena", [P, ARENA])

        at = [0]

        def part(*dims, at0=None):
            n = int(np.prod(dims))
            o = at[0] if at0 is None else at0
            if at0 is None:
                at[0] += n
                assert at[0] <= ARENA, at[0]
            v = arena[:, o:o + n]
            names = "abcde"[:len(dims)]
            if len(dims) > 1:
                v = v.rearrange("p (" + " ".join(names) + ") -> p " + " ".join(names),
                                **{c: d for c, d in zip(names, dims)})
            return v

        qaT = part(4, T)
        kaD = part(2, T)
        qrT = part(4, T)
        krT = part(4, T)
        v_tok = part(NT, 640)
        g_s = part(NT, 512)
        swap0 = at[0]
        swapb = part(2, T)
        retP = part(8, P, at0=swap0)
        vmk = [part(8, P, at0=swap0), part(8, P, at0=at[0])]
        kd = part(512)
        qd = part(4, P)
        S = part(4, 64)
        o_t = part(2, 512)
        o_u = part(512)
        gng = lnb[:, :, 0:512]
        mk = (part(2, 256, at0=at[0]), pbuf[:, 0, 0:512].rearrange("p (m n) -> p m n", m=2))
        Kw = part(8, P)
        Vw = part(8, P)
        ka_tok = part(P)
        ks_tok = part(512)
        sTs = part(64)
        sRs = part(P)
        pTs_sw = part(64)
        soT = part(4, 8)
        o_swa = (lnb[:, :, 512:1024], part(2, 512))
        o_swa_s = part(4, 8)
        qas = part(4, 8)
        Ss = pT[:, :, :].rearrange("p a (b c) -> p (a b c)", b=2).rearrange("p (b j e) -> p b j e", b=8, j=4)
        mem_tok = (arena[:, 2048:4096].rearrange("p (m d) -> p m d", m=2), pbuf[:, :, :])
        memF = (part(KD, 256, at0=0), pT[:, :, :].rearrange("p a (k q) -> p (a k) q", q=256))
        at[0] = 0
        qmT = part(2, T)
        Kc = part(8, 2, 256)
        Vc = part(8, 2, 256)
        KcT = part(2, 2, 2, 256)
        q_wide = part(2, DB, 32)
        sRm = part(2, 256)
        pTm = part(2, 2, P)
        at[0] = 0
        xs = part(3, D)
        xsT = part(2, KD, CAP)
        ex = part(2, 2, CAP)
        actT = part(2, 2, CAP)
        ybuf = part(2, D)
        L = part(NT, 20)
        rA = part(NT, 4)
        rB = part(NT, 4)
        oh = part(NT, 4)
        oh1 = part(NT, 4)
        oh2 = part(NT, 4)
        el4 = part(NT, 4)
        prod = part(NT, 16)
        rs = part(12, NT)
        picks = part(2, NT, NE)
        picked = part(NT, NE)
        so_far = part(NT + 1, NE)
        sel = part(2, NT, NE)
        more = part(NE, STEPS)
        pre = part(NE, NE)
        pl = part(6, 2, NT)
        per_e = part(3, NE)
        sp_f = part(1 + SPILL)
        hot_place = part(2 * NT, CAP)
        hot_block = part(2 * NT, NB)
        assert at[0] <= ARENA - EXTRA_SLOTS * PIECE
        y_of = part(2, NT, D)
        at[0] = 0
        cqn = part(2, 256)
        kr4 = part(2, P)
        cqT = part(2, T)
        rows = part(NT, ROW_W)
        ckvT = part(T)
        krT4 = part(T)
        qn_at = at[0]
        qnT = part(4, T)
        q_lat = part(8, T)
        ctxT = q_lat
        qr_tok = part(2, 256)
        qr_at = at[0]
        qrT2 = part(2, T)
        qrS = decay[:, :, :].rearrange("p (a b) (c e) -> p a (b c) e", a=4, e=32)
        qlS = part(DB, 32)
        kvg = part(P)
        qg = part(2)
        ukT = part(4, P)
        scratch = part(384)
        tmpm = part(64)
        nat = part(64, P)
        natr = lnb[:, :, :].rearrange("p a n -> p (a n)")
        krp = part(16, P, at0=qn_at)
        srow = [part(1032, at0=0), part(1032, at0=qr_at - 512)]
        pTn = part(2, P, at0=1032)
        ctx_row = part(2, P, at0=1288)
        qr_rep = part(8, P, at0=768)
        pTp = pT[:, :, :].rearrange("p a (g r) -> p a g r", g=NPAGE)
        ckvp = pbuf

        names = ["mem_loaded", "const_in", "ident_in", "router_in", "sink_in", "gn_in", "cache_in",
                 "state_in", "newk_in", "kc_in", "vc_in", "odd_in", "ptab_in", "pages_in", "ln_in", "stored",
                 "var_ready", "rstd_ready", "x_ready", "last_ready", "ln_norm", "swapped", "rope_done", "negmax_ready", "probs_ready",
                 "vec_step", "pool_step", "g_exp", "qd_ready", "vm_ready", "gated_ready",
                 "row_neg", "row_exp", "row_probs", "router_neg", "router_exp", "moe_exp",
                 "moe_done", "picks_ready", "places_ready", "route_in", "no_rows", "lnc_in",
                 "x_out", "x_stored", "xT_shared", "q_wide_zero", "q_wide_ready", "states_out", "y_scaled", "combined", "sq_done", "qrS_zero", "oin_ready", "qrtok_ready"]
        s = {n: sem(n) for n in names}
        pair_full = [sem(f"pair_full{i}") for i in range(4)]
        pair_free = [sem(f"pair_free{i}") for i in range(4)]
        slot_landed = [sem(f"slot_landed{i}") for i in range(SLOTS + EXTRA_SLOTS)]
        x_in = [sem(f"x_in{t}") for t in range(NT)]
        xs_in = [sem(f"xs_in{i}") for i in range(3)]
        y_out = [sem(f"y_out{i}") for i in range(2)]
        y_in = [sem(f"y_in{t}") for t in range(NT)]
        spill_s = [{n: sem(f"spill{l}_{n}") for n in ("weights_in", "xs_in", "pe", "act", "dve", "y_out")} for l in range(DEPTH)]
        n_stored = [0]

        def pair(key):
            return PS[:, J[key] % 4, :]

        def full(eng, key):
            n = J[key]
            eng.wait_ge(pair_full[n % 4], n // 4 + 1)

        def free(ins, key):
            ins.then_inc(pair_free[J[key] % 4], 1)

        def taken(eng, key):
            n = J[key]
            eng.wait_ge(pair_free[n % 4], n // 4 + 1)

        def chunk_cols(k, r):
            c = 512 * (k // SHARE) + (k % SHARE) * r
            return slice(c, c + r)

        def wview(name):
            n = WI[name]
            shape, slot = W[n][2], PLACE[n][0]
            size = int(np.prod(shape))
            at_ = ARENA - (SLOTS + EXTRA_SLOTS - slot) * PIECE
            v = ring[:, slot, 0:size] if slot < SLOTS else arena[:, at_:at_ + size]
            if len(shape) == 2:
                v = v.rearrange("p (a b) -> p a b", a=shape[0])
            return v

        def landed(eng, name):
            n = WI[name]
            eng.wait_ge(slot_landed[PLACE[n][0]], 16 * (PLACE[n][1] + 1))

        def uses(n, bufs, l, i):
            return l * len(range(i % bufs, n, bufs)) + i // bufs + 1

        def spilled(eng, l):
            taken(eng, ("table", l))
            count = eng.value_load(spill[0:1, 0:1], min_val=0, max_val=SPILL)
            return eng.If(count > 0)

        def bank_pos(h):
            return 2 * (h % 2) + h // 2

        ATT = [("swa", i, b) for i, b in enumerate(SWA_BLOCKS)]
        ATT += [("mem0", i, b) for i, b in enumerate(MEM_BLOCKS)]
        ATT += [("mla", i, b) for i, b in enumerate(MLA_BLOCKS)]
        ATT += [("mem1", i, b) for i, b in enumerate(MEM_BLOCKS)]
        A0 = {}
        for n, (k, i, b) in enumerate(ATT):
            A0.setdefault(k, n)
        BLOCKS = {"swa": SWA_BLOCKS, "mem0": MEM_BLOCKS, "mem1": MEM_BLOCKS, "mla": MLA_BLOCKS}

        def att_key(kind, step, i):
            return ("mem" + step, int(kind[3]), i) if kind.startswith("mem") else (kind + step, i)

        SCALE = {"swa": 0.125, "mem0": 0.125, "mem1": 0.125, "mla": 96.0 ** -0.5}

        block = ctx.enter_context(nc.Block())

        @block.sync
        def _(sp):
            def load(dst, src, signal):
                sp.dma_start(dst, src).then_inc(s[signal], 16)

            load(ident[:, :], io["c_ident"], "ident_in")
            for t in range(NT):
                src = io["x_prompt"][0, t * P:t * P + P] if t < 4 else io["x_sample"].rearrange("b s d -> (b s) d")
                sp.dma_start(x[0:ROWS[t], t, :], src).then_inc(x_in[t], 16)
            load(mem_tok[0],
                 io["mem_prompt"][0].rearrange("(m p) d -> p m d", p=P), "mem_loaded")

            def load_piece(n):
                name, src, shape, last = W[n]
                slot, use, before = PLACE[n]
                if before is not None:
                    full(sp, W[before][3])
                if slot >= SLOTS:
                    sp.wait_ge(s["x_ready"], NT * 3 * name[1] + 1)
                sp.dma_start(wview(name), src).then_inc(slot_landed[slot], 16)

            def spilled_weights(l, n):
                sem_ = spill_s[l]
                with spilled(sp, l):
                    for slot in range(3):
                        full(sp, W[max(m for m in range(n) if PLACE[m][0] == slot)][3])
                    for j in range(SPILL):
                        if j:
                            sp.wait_ge(sem_["pe"], 3 * j)
                        e = sp.value_load(spill[0:1, 1 + j:2 + j], min_val=0, max_val=NE - 1)
                        sp.dma_start(ring[:, 0:2, :].rearrange("p a (k n) -> p (a k) n", n=512),
                                     io["moe_w_in"][l, bass.ds(e, 1)].rearrange("o (k p) n -> p (o k) n", p=P)
                                     ).then_inc(sem_["weights_in"], 16)
                        sp.dma_start(ring[:, 2, :].rearrange("p (k n) -> p k n", k=2),
                                     io["moe_w_out"][l, bass.ds(e, 1)].rearrange("o (k p) n -> p (o k) n", p=P)
                                     ).then_inc(sem_["weights_in"], 16)
                    sp.wait_ge(sem_["pe"], 3 * SPILL)

            pages_before = WI[("out", 1, 0)]
            for n in range(len(W)):
                if W[n][0] == ("uk",):
                    spilled_weights(0, n)
                if n == pages_before:
                    sp.wait_ge(s["ptab_in"], 16)
                    sp.wait_ge(s["moe_done"], 1)
                    for b in range(DB):
                        for pg in range(NPAGE):
                            i = b * NPAGE + pg
                            r = sp.value_load(ptab[0:1, i:i + 1], min_val=0, max_val=79)
                            page = io["cache_mla"][0, bass.ds(r, 1)].rearrange("o p r -> p (o r)")
                            sp.dma_start(nat[:, i, :], page[:, 0:P]).then_inc(s["pages_in"], 16)
                            sp.dma_start(natr[:, 32 * i:32 * i + 32], page[:, P:ROW_W]).then_inc(s["pages_in"], 16)
                load_piece(n)
            spilled_weights(1, len(W))

        @block.gpsimd
        def _(pool):
            step = [0]

            def load(dst, src, signal):
                pool.dma_start(dst, src).then_inc(s[signal], 16)

            def store(dst, src):
                pool.dma_start(dst, src).then_inc(s["stored"], 16)
                n_stored[0] += 1

            def load_ln(i):
                load(lnb[:, 0, :], io["ln_g"][i // 3, i % 3].partition_broadcast(P), "ln_in")
                load(lnb[:, 1, :], io["ln_b"][i // 3, i % 3].partition_broadcast(P), "ln_in")

            n_rstd = [0]

            def power(v):
                n_rstd[0] += 1
                pool.wait_ge(s["var_ready"], n_rstd[0])
                pool.tensor_tensor(v, v, small[0:v.shape[0], 36:36 + v.shape[1]], ALU.pow).then_inc(s["rstd_ready"], 1)

            def powers(i):
                for t in range(NT):
                    power(rstd[0:ROWS[t], t % 2, 0:1])

            def gains(i, t):
                if t == 0:
                    pool.wait_ge(s["ln_in"], 32 * (i + 1))
                    if i % 3 == 1:
                        pool.wait_ge(s["x_out"], 16 * NT * (i // 3 + 1))
                full(pool, ("xT", i, t))
                r = ROWS[t]
                pool.tensor_tensor(x[0:r, t, :], x[0:r, t, :], lnb[0:r, 0, :], ALU.mult).then_inc(s["pool_step"], 1)
                step[0] += 1
                pool.wait_ge(s["pool_step"], step[0])
                pool.tensor_tensor(x[0:r, t, :], x[0:r, t, :], lnb[0:r, 1, :], ALU.add).then_inc(s["x_ready"], 1)

            def dispatch(l):
                for t in range(NT):
                    pool.wait_ge(s["ln_norm"], NT * (3 * l + 1) + t + 1)
                    pool.dma_start(x_rows[t * P:t * P + ROWS[t], :], x[0:ROWS[t], t, :]).then_inc(s["x_out"], 16)
                pool.wait_ge(s["x_out"], 16 * NT * (l + 1))
                taken(pool, ("table", l))

                def rows_in(buf, b, signal):
                    pool.indirect_dma_start(xs[0:CAP, buf, :], None, x_rows[:, :],
                                            bass.IndirectOffsetOnAxis(ap=block_tokens[:, b:b + 1], axis=0)).then_inc(signal, 16)

                for e in range(NE):
                    if e >= 3:
                        full(pool, ("moeX", l, e - 3))
                    rows_in(e % 3, e, xs_in[e % 3])
                    if 3 <= e < 3 + NT:
                        gains(3 * l + 1, e - 3)
                pool.wait_ge(s["x_ready"], NT * (3 * l + 2))
                load_ln(3 * l + 2)
                sem_ = spill_s[l]
                with spilled(pool, l):
                    full(pool, ("moeX", l, NE - 1))
                    for j in range(SPILL):
                        if j:
                            pool.wait_ge(sem_["pe"], 3 * j)
                        rows_in(0, NE + j, sem_["xs_in"])
                    pool.wait_ge(sem_["y_out"], 16 * SPILL)
                for i in range(2):
                    pool.wait_ge(y_out[i], 16 * NE // 2 * (l + 1))
                pool.wait_ge(s["no_rows"], 16)
                for t in range(NT):
                    r = ROWS[t]
                    for c in range(2):
                        pool.indirect_dma_start(y_of[0:r, c, t, :], None, y_rows[:, :],
                                                bass.IndirectOffsetOnAxis(ap=places[0:r, c, t:t + 1], axis=0)).then_inc(y_in[t], 16)

            load(cosf[:, :], io["c_cos"], "const_in")
            load(sinf[:, :], io["c_sin"], "const_in")
            load(band[:, :], io["c_band"], "const_in")
            load(decay[:, :, :], io["c_decay"], "const_in")
            load(qdec[:, :, :], io["c_qdec"], "const_in")
            load(small[:, :], io["c_small"], "const_in")
            load(rope_t[:, :, :], io["c_rope"], "const_in")
            load(sinkb[:, :], io["sink_by_bank"].partition_broadcast(P), "sink_in")
            load(sinkr[:, :], io["sink_rows"].rearrange("(r o) -> r o", o=1), "sink_in")
            for l in range(DEPTH):
                load(wr[:, l, :, 0:4], io["moe_w_group"][l].rearrange("(k p) n -> p k n", p=P), "router_in")
                load(wr[:, l, :, 4:20], io["moe_w_router"][l].rearrange("(k p) n -> p k n", p=P), "router_in")
                load(rb[:, l, 0:4], io["moe_b_group"][l].partition_broadcast(P), "router_in")
                load(rb[:, l, 4:20], io["moe_b_router"][l].partition_broadcast(P), "router_in")
            load(lnc[:, :, :, :], io["ln_by_feature"], "lnc_in")
            pool.dma_start(y_rows.rearrange("(s b) d -> s b d", b=NB)[:, NE:, :], io["c_no_row"].to_broadcast([CAP, SPILL, D])
                           ).then_inc(s["no_rows"], 16)
            load(ptab[:, :], io["page_table"].rearrange("(o b) g -> o (b g)", o=1), "ptab_in")

            def memory_out(l):
                for m in range(2):
                    taken(pool, ("mkv", l, m))
                    store(mem_k_p[l, 0, m * P:m * P + P].rearrange("s h d -> s (h d)"), mk[l][:, m, :])
                    store(mem_v_p[l, 0, m * P:m * P + P].rearrange("s h d -> s (h d)"), mv[:, l, m, :])

            memory_out(0)
            pool.wait_ge(s["stored"], 16 * n_stored[0])

            load(gng[:, 0, :], io["ret_gn_g"][0].partition_broadcast(P), "gn_in")
            load(gng[:, 1, :], io["ret_gn_b"][0].partition_broadcast(P), "gn_in")
            full(pool, ("mkT", 0))
            for dst, name in ((Kw, "cache_swa_k"), (Vw, "cache_swa_v")):
                load(dst[0:127, :, :], io[name][0, :, 1:128].rearrange("b s h d -> s b (h d)"), "cache_in")
            taken(pool, ("va",))
            taken(pool, ("kaTok",))
            for b in range(DB):
                load(Kw[127:128, b, :], sRs[b:b + 1, :], "newk_in")
                load(Vw[127:128, b, :], v_tok[b:b + 1, 4, 0:128], "newk_in")
            store(swa_k_p[0, 0].rearrange("s h d -> s (h d)"), ka_tok[:, :])
            store(swa_v_p[0, 0].rearrange("s h d -> s (h d)"), v_tok[:, 3, 0:128])
            pool.wait_ge(s["cache_in"], 32)
            pool.wait_ge(s["newk_in"], 16 * 16)
            for src, dst in ((Kw, swa_k_s), (Vw, swa_v_s)):
                store(dst[0].rearrange("b s h d -> s b (h d)"), src[:, :, :])
            full(pool, ("swO",))
            for par in range(2):
                for b in range(DB):
                    load(Ss[par * 64:par * 64 + 64, b, :, :],
                         io["state_ret"][0, b].rearrange("(j t) k e -> t k j e", t=2)[par], "state_in")
            pool.wait_ge(s["rope_done"], 14)
            pool.wait_ge(s["const_in"], 16 * 7)
            for n in range(1, 4):
                if n > 1:
                    full(pool, ("retO", n - 1))
                pool.tensor_tensor(qd, qrT[:, :, tile_cols(n)], qdec[:, :, :], ALU.mult).then_inc(s["qd_ready"], 1)
                power(st[:, 16:24])
            power(st[:, 16:24])
            pool.wait_ge(s["qd_ready"], 3)
            load(route[:, :, :], io["c_route"], "route_in")
            full(pool, ("retU", 3))
            for j in range(4):
                if j >= 2:
                    full(pool, ("sU", j - 2))
                pool.tensor_tensor(vmk[j % 2][0:8, :, :], v_tok[0:8, 4, 128 + j * P:256 + j * P].unsqueeze(1).to_broadcast([8, 8, P]),
                                   small[0:8, 24:32].unsqueeze(2).to_broadcast([8, 8, P]), ALU.mult).then_inc(s["vm_ready"], 1)
            pool.wait_ge(s["stored"], 16 * n_stored[0])
            power(rstd[0:ROWS[0], 0, 0:1])
            power(rstd[0:ROWS[1], 1, 0:1])
            power(rstd[0:ROWS[2], 0, 0:1])
            power(st[0:8, 16:24])
            for t in range(3, NT):
                power(rstd[0:ROWS[t], t % 2, 0:1])
            pool.wait_ge(s["gated_ready"], 5)
            full(pool, ("y", 0, 4))
            load_ln(0)

            for l in range(DEPTH):
                if l == 1:
                    for t in range(NT):
                        pool.wait_ge(s["oin_ready"], t + 1)
                        dst = mla_p[0, 0, t * P:t * P + P] if t < 4 else mla_s[0].rearrange("b s r -> (b s) r")
                        store(dst, rows[0:ROWS[t], t, :])
                    full(pool, ("pkT", 1))
                    load_ln(3)
                    pool.wait_ge(s["stored"], 16 * n_stored[0])
                    powers(3 * l)
                else:
                    pool.wait_ge(s["states_out"], 16 * 2 * (DB + 1))
                for b in range(DB):
                    for dst, name, sg in ((Kc, "cache_mem_k", "kc_in"), (Vc, "cache_mem_v", "vc_in")):
                        load(dst[:, b, :, :], io[name][l, b].rearrange("(c p) h d -> p c (h d)", p=P), sg)
                for t in range(NT):
                    gains(3 * l, t)
                pool.wait_ge(s["x_ready"], NT * (3 * l + 1))
                load_ln(3 * l + 1)
                powers(3 * l + 1)
                dispatch(l)
                if l == 0:
                    powers(2)
                    load(kvg[:, :], io["mla_kv_norm"][0].partition_broadcast(P), "odd_in")
                    pool.dma_start(qg[:, :], io["mla_q_norm"][0].rearrange("(k p) -> p k", p=P),
                                   allow_slow_non_contiguous=True).then_inc(s["odd_in"], 16)
                    for t in range(NT):
                        if t:
                            power(rms[0:ROWS[t - 1], (t - 1) % 2, 2:4])
                        gains(2, t)
                    power(rms[0:ROWS[NT - 1], (NT - 1) % 2, 2:4])
                    memory_out(1)
                    pool.wait_ge(s["x_ready"], NT * 3)
                    pool.wait_ge(s["stored"], 16 * n_stored[0])
                    pool.nop().then_inc(s["moe_done"], 1)
            power(rstd[0:ROWS[0], 0, 0:1])
            for t in range(NT):
                if t + 1 < NT:
                    power(rstd[0:ROWS[t + 1], (t + 1) % 2, 0:1])
                if t == NT - 1:
                    break
                r = ROWS[t]
                pool.wait_ge(s["ln_norm"], NT * 5 + t + 1)
                if t in POOL_GAINS:
                    pool.tensor_tensor(x[0:r, t, :], x[0:r, t, :], lnb[0:r, 0, :], ALU.mult).then_inc(s["pool_step"], 1)
                    step[0] += 1
                    pool.wait_ge(s["pool_step"], step[0])
                pool.tensor_tensor(x[0:r, t, :], x[0:r, t, :], lnb[0:r, 1, :], ALU.add).then_inc(s["x_ready"], 1)
            pool.wait_ge(s["stored"], 16 * n_stored[0])

        @block.tensor
        def _(pe):
            def open_(key):
                n = J[key]
                if n >= 4:
                    pe.wait_ge(pair_free[n % 4], n // 4)
                return PS[:, n % 4, :]

            def close(mm, key):
                mm.then_inc(pair_full[J[key] % 4], 1)

            def transpose_x(i, t):
                key = ("xT", i, t)
                o = open_(key)
                r = ROWS[t]
                pe.wait_ge(x_in[t], 16) if i < 0 else pe.wait_ge(s["ln_norm"], NT * i + t + 1)
                for k in range(KD):
                    mm = pe.transpose(o[:, chunk_cols(k, r)], x[0:r, t, k * P:k * P + P], ident[0:r, 0:r])
                close(mm, key)

            def by_feature(key, lhs, rhs, nk, out_rows=slice(0, P), start=True, last=True):
                o = pair(key)
                for k in range(nk):
                    for h in range(2):
                        mm = pe.matmul(o[out_rows, 512 * h:512 * h + HALF], lhs(k), rhs(k)[:, HALF * h:HALF * h + HALF],
                                       start=(k == 0), stop=(k == nk - 1))
                return mm

            def attention(kind, score, apply, between=lambda n: None):
                blocks = BLOCKS[kind]
                base = A0[kind]

                def step_s(i):
                    key = att_key(kind, "S", i)
                    o = open_(key)
                    close(score(i, o, blocks[i]), key)

                def step_t(i):
                    key = att_key(kind, "T", i)
                    o = open_(key)
                    g, w = blocks[i][2:]
                    pe.wait_ge(s["probs_ready"], base + i + 1)
                    b = pbuf[:, (base + i) % 2, :].rearrange("p (g w) -> p g w", g=g)
                    for c in range(w // P):
                        for h in range(g):
                            col = (c * g + h) * P
                            mm = pe.transpose(o[:, col:col + P], b[:, h, c * P:c * P + P], ident[:, :])
                    close(mm, key)

                def step_o(i):
                    key = att_key(kind, "O", i)
                    o = open_(key)
                    taken(pe, att_key(kind, "T", i))
                    g, w = blocks[i][2:]
                    v = pT[:, (base + i) % 2, :].rearrange("p (c g q) -> p c g q", g=g, q=P)
                    close(apply(i, o, blocks[i], v), key)

                steps = {"S": step_s, "T": step_t, "O": step_o}
                for st_, i in pipelined("S", "T", "O", len(blocks)):
                    steps[st_](i)
                    if (st_, i) == ("S", 1):
                        between(0)
                    elif st_ == "O":
                        between(i + 1)

            pe.wait_ge(s["ident_in"], 16)
            for t in range(NT):
                transpose_x(-1, t)
            def memory_features(l, m):
                key = ("memF", l, m)
                o = open_(key)
                pe.wait_ge(s["mem_loaded"], 16 * (l + 1))
                for k in range(KD):
                    mm = pe.transpose(o[:, k * P:k * P + P], mem_tok[l][:, m, k * P:k * P + P], ident[:, :])
                close(mm, key)

            def memory_keys_values(l, m):
                key = ("mkv", l, m)
                o = open_(key)
                taken(pe, ("memF", l, 1))
                for c, w in enumerate("kv"):
                    landed(pe, ("m" + w, l))
                    for k in range(KD):
                        mm = pe.matmul(o[:, 512 * c:512 * c + 256], memF[l][:, k, m * P:m * P + P],
                                       wview(("m" + w, l))[:, k, :], start=(k == 0), stop=(k == KD - 1))
                close(mm, key)

            def memory_keys_back(l):
                key = ("mkT", l)
                o = open_(key)
                taken(pe, ("mkv", l, 1))
                for c in range(2):
                    for m in range(2):
                        mm = pe.transpose(o[:, c * 256 + m * P:c * 256 + m * P + P], mk[l][:, m, c * P:c * P + P], ident[:, :])
                close(mm, key)

            for m in range(2):
                memory_features(0, m)
            for m in range(2):
                memory_keys_values(0, m)
            memory_keys_back(0)

            taken(pe, ("xT", -1, 4))
            xk = lambda k: xT[:, k, :]

            def chunk(key, name, lhs):
                open_(key)
                landed(pe, name)
                close(by_feature(key, lhs, xk, KD), key)

            def plain(name, j):
                w = wview(name)
                return lambda k: w[:, k, j * P:j * P + P]

            def tokens(key, name, tiles, cols):
                o = open_(key)
                landed(pe, name)
                w = wview(name)
                width = cols.stop - cols.start
                for n, t in enumerate(tiles):
                    for k in range(KD):
                        mm = pe.matmul(o[0:ROWS[t], n * width:n * width + width], xT[:, k, tile_cols(t)], w[:, k, cols],
                                       start=(k == 0), stop=(k == KD - 1))
                close(mm, key)

            def chunks(what, i, j):
                name = ("ein", i + j // 2)
                chunk((what, j), name, plain(name, j % 2))

            for j in range(4):
                chunks("qa", 0, j)
            for kv in range(2):
                chunk(("ka", kv), ("ka",), plain(("ka",), kv))
            tokens(("va",), ("va",), range(NT), slice(0, P))
            def project(key):
                if key[0] in ("qr", "kr"):
                    chunks(key[0], 3 if key[0] == "qr" else 5, key[1])
                else:
                    name = ("ein", 7 + 2 * ("vr", "g").index(key[0]) + key[1])
                    tokens(key, name, range(4) if key[2] == 0 else range(4, 5), slice(0, 256))

            key = ("kaTok",)
            o = open_(key)
            pe.wait_ge(s["rope_done"], 6)
            for kv in range(2):
                pe.transpose(o[:, 64 * kv:64 * kv + 64], kaD[0:64, kv, 384:512], ident[0:64, 0:64])
                mm = pe.transpose(o[0:8, 128 + 64 * kv:192 + 64 * kv], kaD[0:64, kv, 512:520], ident[0:64, 0:64])
            close(mm, key)
            taken(pe, ("va",))

            def swa_score(i, o, blk):
                n, h0, g, w = blk
                k0 = max(n - 1, 0) * P
                o = o.rearrange("p (g w) -> p g w", g=g)
                for h in (0, 2, 1, 3):
                    b, c = 64 * (h % 2), (h0 + h) // 2
                    mm = pe.matmul(o[:, bank_pos(h), 0:w], qaT[b:b + 64, c, n * P:n * P + P],
                                   kaD[b:b + 64, h0 // 4, k0:k0 + w], start=True, stop=True)
                return mm

            def swa_apply(i, o, blk, v):
                n, h0, g, w = blk
                t0 = max(n - 1, 0)
                for b in range(2):
                    for c in range(w // P):
                        mm = pe.matmul(o[64 * b:64 * b + 64, 0:256], v_tok[:, t0 + c, 16 * h0:16 * h0 + 64],
                                       v[:, c, 2 * b:2 * b + 2, :], start=(c == 0), stop=(c == w // P - 1))
                return mm

            def between(n):
                for key in SWA_WEAVE[n]:
                    project(key)

            project(("qr", 0))
            attention("swa", swa_score, swa_apply, between)

            pe.wait_ge(s["cache_in"], 32)
            pe.wait_ge(s["newk_in"], 16 * 16)
            def window_keys():
                key = ("kwT",)
                o = open_(key)
                for b in range(DB):
                    mm = pe.transpose(o[:, b * P:b * P + P], Kw[:, b, :], ident[:, :])
                close(mm, key)

            def window_scores():
                key = ("swS",)
                o = open_(key)
                taken(pe, ("kwT",))
                for kv in range(2):
                    for b in range(DB):
                        mm = pe.matmul(o[:, 512 * kv + 4 * b:512 * kv + 4 * b + 4], pbuf[64 * kv:64 * kv + 64, 0, b * P:b * P + P],
                                       qas[64 * kv:64 * kv + 64, :, b], start=True, stop=True)
                close(mm, key)

            n_rows = [0]

            def to_rows(key, src, count, chunks):
                o = open_(key)
                for c in range(chunks):
                    mm = pe.transpose(o[0:count, c * P:c * P + P], src[:, c, :], ident[:, :])
                close(mm, key)

            def from_rows(key, src, count, chunks):
                o = open_(key)
                n_rows[0] += 1
                pe.wait_ge(s["row_probs"], n_rows[0])
                for c in range(chunks):
                    mm = pe.transpose(o[:, c * count:c * count + count], src[0:count, c * P:c * P + P],
                                      ident[0:count, 0:count])
                close(mm, key)

            def window_rows():
                taken(pe, ("swS",))
                to_rows(("swR",), sTs.unsqueeze(1), 64, 1)

            def window_outputs():
                key = ("swO",)
                o = open_(key)
                taken(pe, ("swT",))
                for kv in range(2):
                    for b in range(DB):
                        for h in range(2):
                            c0 = 8 * b + 4 * kv + h
                            mm = pe.matmul(o[64 * h:64 * h + 64, 16 * kv + b:16 * kv + b + 9:8],
                                           Vw[:, b, 64 * kv:64 * kv + 64], pTs_sw[:, c0:c0 + 3:2], start=True, stop=True)
                close(mm, key)

            steps = {"kwT": window_keys, "swS": window_scores, "swR": window_rows,
                     "swT": lambda: from_rows(("swT",), sRs, 64, 1), "swO": window_outputs}
            for key in SWA_SAMPLE:
                if key[0] in steps:
                    steps[key[0]]()
                else:
                    project(key)

            pe.wait_ge(s["rope_done"], 14)
            taken(pe, ("vr", 1, 1))

            def ret_gated(n):
                key = ("retG", n)
                o = open_(key)
                r = ROWS[n]
                pe.wait_ge(s["gated_ready"], n + 1)
                for j in range(4):
                    mm = pe.transpose(o[:, j * r:j * r + r], o_t[0:r, n % 2, j * P:j * P + P], ident[0:r, 0:r])
                close(mm, key)

            for n in range(4):
                cols = tile_cols(n)
                key = ("retS", n)
                o = open_(key)
                for h in (0, 2, 4, 6, 1, 3, 5, 7):
                    b, c = 64 * (h % 2), h // 2
                    k = 512 * (h % 2) + c * P
                    mm = pe.matmul(o[:, k:k + P], krT[b:b + 64, c, cols], qrT[b:b + 64, c, cols], start=True, stop=True)
                close(mm, key)
                key = ("retK", n)
                o = open_(key)
                for c in range(4):
                    mm = pe.transpose(o[:, c * P:c * P + P], krT[:, c, cols], ident[:, :])
                close(mm, key)
                key = ("retO", n)
                o = open_(key)
                taken(pe, ("retS", n))
                if n:
                    taken(pe, ("retU", n - 1))
                    pe.wait_ge(s["qd_ready"], n)
                for h in (0, 2, 4, 6, 1, 3, 5, 7):
                    b, c = 64 * (h % 2), h // 2
                    k = 512 * (h % 2) + 64 * c
                    mm = pe.matmul(o[:, k:k + 64], retP[:, 4 * (h % 2) + c, :], v_tok[:, n, 128 + 64 * h:192 + 64 * h],
                                   start=True, stop=(n == 0))
                    if n:
                        mm = pe.matmul(o[:, k:k + 64], qd[b:b + 64, c, :], S[b:b + 64, c, :], start=False, stop=True)
                close(mm, key)
                key = ("retU", n)
                o = open_(key)
                taken(pe, ("retK", n))
                for c in range(4):
                    mm = pe.matmul(o[:, c * P:c * P + P], kd[:, c * P:c * P + P], v_tok[:, n, 128 + c * P:256 + c * P],
                                   start=True, stop=True)
                close(mm, key)
                if n:
                    ret_gated(n - 1)

            def sample_keys():
                key = ("skT",)
                o = open_(key)
                for c in range(4):
                    mm = pe.transpose(o[0:8, c * P:c * P + P], krT[:, c, 512:520], ident[:, :])
                close(mm, key)

            def state_update(j):
                key = ("sU", j)
                o = open_(key)
                taken(pe, ("skT",))
                pe.wait_ge(s["vm_ready"], j + 1)
                for h in range(2):
                    mm = pe.matmul(o[:, 512 * h:512 * h + 512], ks_tok[0:8, j * P:j * P + P],
                                   vmk[j % 2][0:8, 4 * h:4 * h + 4, :], start=True, stop=True)
                close(mm, key)

            def state_output():
                key = ("sO",)
                o = open_(key)
                taken(pe, ("sU", 3))
                for b in range(DB):
                    for h in range(8):
                        q, c = 64 * (h % 2), h // 2
                        mm = pe.matmul(o[q:q + 64, c * 8 + b:c * 8 + b + 1], Ss[q:q + 64, b, c, :],
                                       qrT[q:q + 64, c, 512 + b:513 + b], start=True, stop=True)
                close(mm, key)

            def state_output_back():
                key = ("sOt",)
                o = open_(key)
                taken(pe, ("sO",))
                for c in range(4):
                    mm = pe.transpose(o[0:8, c * P:c * P + P], soT[:, c, :], ident[:, :])
                close(mm, key)

            def out_part(i, k, t):
                if i or k >= 4:
                    return oT[:, k, tile_cols(t)]
                return o_swa[k // 2][:, k % 2, tile_cols(t)] if t < 4 else o_swa_s[:, k, :]

            def out_proj(i, t, pieces, last):
                taken(pe, last)
                key = ("y", i, t)
                o = open_(key)
                for h in range(2):
                    for n, name in enumerate(pieces):
                        landed(pe, name)
                        w = wview(name)
                        for k in range(2):
                            mm = pe.matmul(o[0:ROWS[t], 512 * h:512 * h + 512], out_part(i, 2 * n + k, t),
                                           w[:, k, 512 * h:512 * h + 512], start=(n == 0 and k == 0),
                                           stop=(n == len(pieces) - 1 and k == 1))
                close(mm, key)

            even_pieces = [("out", 0, i) for i in range(4)]
            steps = {"xT": transpose_x, "skT": sample_keys, "retG": ret_gated, "sU": state_update, "sO": state_output, "sOt": state_output_back,
                     "y": lambda i, t: out_proj(0, t, even_pieces, ("retG", t))}
            for key in RET_SAMPLE:
                steps[key[0]](*key[1:])

            def cross_attention(l):
                taken(pe, ("xT", 3 * l, 4))
                for j in range(2):
                    key = ("mq", l, j)
                    open_(key)
                    landed(pe, ("mq", l))
                    w = wview(("mq", l))
                    close(by_feature(key, lambda k: w[:, k, j * P:j * P + P], xk, KD), key)
                taken(pe, ("mq", l, 1))

                def score(i, o, blk):
                    n = blk[0]
                    for h in (0, 2, 1, 3):
                        b, c = 64 * (h % 2), h // 2
                        k = 256 * bank_pos(h)
                        mm = pe.matmul(o[:, k:k + 256], qmT[b:b + 64, c, n * P:n * P + P],
                                       mkT[b:b + 64, l, c, :], start=True, stop=True)
                    return mm

                def apply(i, o, blk, v):
                    for h in range(4):
                        for c in range(2):
                            mm = pe.matmul(o[64 * (h % 2):64 * (h % 2) + 64, (h // 2) * P:(h // 2) * P + P],
                                           mv[:, l, c, 64 * h:64 * h + 64], v[:, c, bank_pos(h), :], start=(c == 0), stop=(c == 1))
                    return mm

                attention(f"mem{l}", score, apply)

                pe.wait_ge(s["kc_in"], 16 * DB * (l + 1))
                pe.wait_ge(s["q_wide_ready"], l + 1)
                scores = pair(("msS", l))
                for key in (("kcT", l, 0), ("kcT", l, 1), ("msS", l), ("kcT", l, 2), ("kcT", l, 3), None):
                    if key is not None and key[0] == "kcT":
                        g = key[2]
                        o = open_(key)
                        for bb in range(2):
                            for hc in range(2):
                                for c in range(2):
                                    col = bb * 512 + hc * 256 + c * P
                                    mm = pe.transpose(o[:, col:col + P], Kc[:, 2 * g + bb, c, hc * P:hc * P + P], ident[:, :])
                        close(mm, key)
                        continue
                    bank = 0 if key else 1
                    if key:
                        open_(key)
                    for g in (2 * bank, 2 * bank + 1):
                        taken(pe, ("kcT", l, g))
                        for bb in range(2):
                            b = 2 * g + bb
                            r0 = 32 * (b % 4)
                            for hc in range(2):
                                mm = pe.matmul(scores[r0:r0 + 32, 512 * bank:512 * bank + 256], q_wide[:, hc, b, :],
                                               KcT[:, g % 2, bb, hc, :], start=(hc == 0), stop=(hc == 1),
                                               **({"tile_position": (0, 96)} if r0 == 96 else {}))
                        if g == 3:
                            close(mm, ("msS", l))
                out_piece = [("mo", l)]
                def probs_back():
                    key = ("msT", l)
                    o = open_(key)
                    n_rows[0] += 1
                    pe.wait_ge(s["row_probs"], n_rows[0])
                    for bank in range(2):
                        for c in range(2):
                            col = (2 * bank + c) * P
                            mm = pe.transpose(o[:, col:col + P], sRm[:, bank, c * P:c * P + P], ident[:, :])
                    close(mm, key)

                def sample_outputs():
                    key = ("msO", l)
                    o = open_(key)
                    taken(pe, ("msT", l))
                    pe.wait_ge(s["vc_in"], 16 * DB * (l + 1))
                    for b in range(DB):
                        for h in range(4):
                            for c in range(2):
                                mm = pe.matmul(o[64 * (h % 2):64 * (h % 2) + 64, 8 * (h // 2) + b:8 * (h // 2) + b + 1],
                                               Vc[:, b, c, 64 * h:64 * h + 64], pTm[:, b // 4, c, 32 * (b % 4) + h:32 * (b % 4) + h + 1],
                                               start=(c == 0), stop=(c == 1))
                    close(mm, key)

                logits = router_logits(l)
                prompt_done = att_key(f"mem{l}", "O", len(MEM_BLOCKS) - 1)
                for key in memory_tail(l):
                    if key[0] == "msT":
                        probs_back()
                    elif key[0] == "msO":
                        sample_outputs()
                    elif key[0] == "y":
                        out_proj(key[1], key[2], out_piece, prompt_done if key[2] < 4 else ("msO", l))
                    elif key[0] == "rt":
                        open_(key)
                        logits(0)
                        logits(1)
                    else:
                        transpose_x(*key[1:])
                        if key[2] > 2:
                            logits(key[2] - 1)
                logits(NT - 1)

            def router_logits(l):
                key = ("rt", l)

                def tile(t):
                    if t == 0:
                        pe.wait_ge(s["router_in"], 16 * 8)
                    taken(pe, ("xT", 3 * l + 1, t))
                    for k in range(KD):
                        mm = pe.matmul(pair(key)[0:ROWS[t], t * 32:t * 32 + 20], xT[:, k, tile_cols(t)], wr[:, l, k, :],
                                       start=(k == 0), stop=(k == KD - 1))
                    if t == NT - 1:
                        close(mm, key)

                return tile

            def experts(l):
                if l == 0:
                    for m in range(2):
                        memory_features(1, m)
                key = ("rank", l)
                o = open_(key)
                pe.wait_ge(s["route_in"], 16)
                pe.wait_ge(s["picks_ready"], l + 1)
                for i in range(2):
                    mm = pe.matmul(o[:, 512 * i:512 * i + NT * NE], route[:, i, :], picked.rearrange("p t e -> p (t e)"),
                                   start=True, stop=True)
                close(mm, key)
                if l == 0:
                    memory_keys_values(1, 0)
                key = ("table", l)
                o = open_(key)
                pe.wait_ge(s["places_ready"], l + 1)
                for n in range(2 * NT):
                    r = ROWS[n % NT]
                    mm = pe.matmul(o[0:CAP, 0:NB], hot_place[0:r, n, :], hot_block[0:r, n, :], start=(n == 0), stop=(n == 2 * NT - 1))
                close(mm, key)

                def rows_to_features(o, src):
                    for k in range(KD):
                        mm = pe.transpose(o[:, chunk_cols(k, CAP)], src[0:CAP, k * P:k * P + P], ident[0:CAP, 0:CAP])
                    return mm

                def hidden(o, w, xT_):
                    for c in range(4):
                        col = 512 * (c // 2) + CAP * (c % 2)
                        for k in range(KD):
                            mm = pe.matmul(o[:, col:col + CAP], w(k)[:, c * P:c * P + P], xT_[:, k, :], start=(k == 0), stop=(k == KD - 1))
                    return mm

                def output(o, w, a):
                    for h in range(2):
                        for c in range(2):
                            mm = pe.matmul(o[0:CAP, 512 * h:512 * h + 512], a[:, c, :], w[:, c, 512 * h:512 * h + 512],
                                           start=(c == 0), stop=(c == 1))
                    return mm

                def step_x(e):
                    key = ("moeX", l, e)
                    o = open_(key)
                    pe.wait_ge(xs_in[e % 3], 16 * uses(NE, 3, l, e))
                    close(rows_to_features(o, xs[:, e % 3, :]), key)

                def step_h(e):
                    key = ("moeH", l, e)
                    o = open_(key)
                    taken(pe, ("moeX", l, e))
                    for c in range(2):
                        landed(pe, ("wi", l, e, c))
                    w = [wview(("wi", l, e, c)) for c in range(2)]
                    close(hidden(o, lambda k: w[k // 4][:, k % 4, :], xsT[:, e % 2, :, :]), key)

                def step_y(e):
                    key = ("moeY", l, e)
                    o = open_(key)
                    landed(pe, ("wo", l, e))
                    taken(pe, ("moeH", l, e))
                    close(output(o, wview(("wo", l, e)), actT[:, e % 2, :, :]), key)

                steps = {"X": step_x, "H": step_h, "Y": step_y}
                for st_, e in expert_order():
                    steps[st_](e)

                if l == 0:
                    memory_keys_values(1, 1)
                sem_ = spill_s[l]
                with spilled(pe, l):
                    if l == 0:
                        taken(pe, ("mkv", 1, 1))
                    for e in range(NE - 3, NE):
                        taken(pe, ("moeY", l, e))
                    taken(pe, ("moeH", l, NE - 1))
                    win = ring[:, 0:2, :].rearrange("p a (k n) -> p (a k) n", n=512)
                    for j in range(SPILL):
                        pe.wait_ge(sem_["xs_in"], 16 * (j + 1))
                        rows_to_features(PS[:, 0, :], xs[:, 0, :]).then_inc(sem_["pe"], 1)
                        pe.wait_ge(sem_["act"], 3 * j + 1)
                        pe.wait_ge(sem_["weights_in"], 32 * (j + 1))
                        hidden(PS[:, 1, :], lambda k: win[:, k, :], xsT[:, 0, :, :]).then_inc(sem_["pe"], 1)
                        pe.wait_ge(sem_["dve"], 4 * (j + 1))
                        if j:
                            pe.wait_ge(sem_["act"], 3 * j)
                        output(PS[:, 2, :], ring[:, 2, :].rearrange("p (k n) -> p k n", k=2), actT[:, 0, :, :]).then_inc(sem_["pe"], 1)

            def latent_attention():
                taken(pe, ("xT", 2, 4))
                key = ("ukT",)
                o = open_(key)
                landed(pe, ("uk",))
                for c in range(4):
                    mm = pe.transpose(o[:, c * P:c * P + P], wview(("uk",))[:, c * P:c * P + P], ident[:, :])
                close(mm, key)

                def oin_back(t):
                    key = ("oinT", t)
                    o = open_(key)
                    r = ROWS[t]
                    pe.wait_ge(s["oin_ready"], t + 1)
                    for c, src in enumerate((cqn[0:r, t % 2, 0:P], cqn[0:r, t % 2, P:2 * P], rows[0:r, t, 0:P], kr4[0:r, t % 2, :])):
                        mm = pe.transpose(o[:, c * P:c * P + r], src, ident[0:r, 0:r])
                    close(mm, key)

                for t in range(NT):
                    key = ("oin", t)
                    o = open_(key)
                    for c in range(2):
                        landed(pe, ("oin", c))
                        for k in range(4):
                            mm = pe.matmul(o[0:ROWS[t], 0:416], xT[:, 4 * c + k, tile_cols(t)], wview(("oin", c))[:, k, :],
                                           start=(c == 0 and k == 0), stop=(c == 1 and k == 3))
                    close(mm, key)
                    if t:
                        oin_back(t - 1)
                oin_back(4)
                taken(pe, ("oinT", 4))
                landed(pe, ("uq",))
                uq = wview(("uq",))
                cqk = lambda k: cqT[:, k, :]
                for j in range(4):
                    key = ("qn", j)
                    open_(key)
                    close(by_feature(key, lambda k: uq[:, k, j * P:j * P + P], cqk, 2), key)

                def q_rope(t):
                    key = ("qrope", t)
                    o = open_(key)
                    for k in range(2):
                        mm = pe.matmul(o[0:ROWS[t], 0:256], cqT[:, k, tile_cols(t)], uq[:, k, 512:768],
                                       start=(k == 0), stop=(k == 1))
                    close(mm, key)

                def q_rope_back(t):
                    key = ("qrT", t)
                    o = open_(key)
                    pe.wait_ge(s["qrtok_ready"], t + 1)
                    if t < 4:
                        for c in range(2):
                            mm = pe.transpose(o[:, c * P:c * P + P], qr_tok[:, t % 2, c * P:c * P + P], ident[:, :])
                    else:
                        for h in range(8):
                            mm = pe.transpose(o[:, 8 * h:8 * h + 8], qr_rep[0:8, h, :], ident[0:8, 0:8])
                    close(mm, key)

                q_rope(0)
                taken(pe, ("ukT",))
                taken(pe, ("qn", 2))
                taken(pe, ("qn", 3))
                for h in range(8):
                    key = ("ql", h)
                    open_(key)
                    b, c = 64 * (h % 2), h // 2
                    close(by_feature(key, lambda k: ukT[b:b + 64, c, :], lambda k: qnT[b:b + 64, c, :], 1), key)
                for t in range(1, NT):
                    q_rope(t)
                    q_rope_back(t - 1)
                q_rope_back(4)
                taken(pe, ("qrT", 4))
                taken(pe, ("ql", 6))
                taken(pe, ("ql", 7))

                def score(i, o, blk):
                    n, h0, g, w = blk
                    o = o.rearrange("p (g w) -> p g w", g=g)
                    for h in range(h0, h0 + g):
                        b, c = 32 * (h % 4), h // 4
                        pe.matmul(o[:, h - h0, 0:w], q_lat[:, h, n * P:n * P + P], ckvT[:, 0:w], start=True, stop=False)
                        mm = pe.matmul(o[:, h - h0, 0:w], qrT2[b:b + 32, c, n * P:n * P + P], krT4[b:b + 32, 0:w],
                                       start=False, stop=True, **({"tile_position": (b, 0)} if b == 96 else {}))
                    return mm

                def apply(i, o, blk, v):
                    n, h0, g, w = blk
                    for c in range(n + 1):
                        mm = pe.matmul(o[:, 0:g * P], rows[:, c, 0:P], v[:, c, :, :], start=(c == 0), stop=(c == n))
                    return mm

                attention("mla", score, apply)

                pe.wait_ge(s["pages_in"], 16 * 128)
                for g in range(2):
                    key = ("pkT", g)
                    o = open_(key)
                    for c in range(8):
                        mm = pe.transpose(o[:, c * P:c * P + P], natr[:, (8 * g + c) * P:(8 * g + c + 1) * P], ident[:, :])
                    close(mm, key)

                wide = lambda r0: {"tile_position": (0, 96)} if r0 == 96 else {}
                key = ("pN",)
                o = open_(key)
                for i in range(2):
                    pe.matmul(o[:, 512 * i:512 * i + 8], qlS[:, 4 * i:4 * i + 4, :].rearrange("p b h -> p (b h)"), ckvT[:, 512:520],
                              start=True, stop=False)
                    mm = pe.matmul(o[:, 512 * i:512 * i + 8], qrS[:, 0, 4 * i:4 * i + 4, :].rearrange("p b h -> p (b h)"),
                                   krT4[:, 512:520], start=False, stop=True)
                close(mm, key)

                def page_latents(b):
                    key = ("pcT", b)
                    o = open_(key)
                    for pg in range(NPAGE):
                        mm = pe.transpose(o[:, pg * P:pg * P + P], nat[:, 8 * b + pg, 0:P], ident[:, :])
                    close(mm, key)

                def page_scores(b):
                    key = ("pS", b // 4)
                    r0 = 32 * (b % 4)
                    o = pair(key)[r0:r0 + 32, :]
                    taken(pe, ("pcT", b))
                    taken(pe, ("pkT", 1))
                    for h in range(2):
                        pe.matmul(o[:, 512 * h:512 * h + 512], qlS[:, b, :], ckvp[:, b % 2, 512 * h:512 * h + 512],
                                  start=True, stop=False, skip_group_check=True, **wide(r0))
                        for pg in range(4):
                            col = 512 * h + pg * P
                            mm = pe.matmul(o[:, col:col + P], qrS[:, pg, b, :], krp[:, 2 * b + h, :],
                                           start=False, stop=(pg == 3), skip_group_check=True, **wide(r0))
                    if b % 4 == 3:
                        close(mm, key)

                def page_probs(i):
                    key = ("pT", i)
                    o = open_(key)
                    n_rows[0] += 1
                    pe.wait_ge(s["row_probs"], n_rows[0])
                    for pg in range(NPAGE):
                        mm = pe.transpose(o[:, pg * P:pg * P + P], srow[i][:, pg * P:pg * P + P], ident[:, :])
                    close(mm, key)

                def new_probs(i):
                    key = ("pTn", i)
                    o = open_(key)
                    close(pe.transpose(o[0:8, 0:P], srow[i][:, 1024:1032], ident[:, :]), key)

                def page_outputs(i):
                    key = ("pO", i)
                    o = open_(key)
                    taken(pe, ("pTn", i))
                    pe.matmul(o[:, 0:P], pTn[0:8, i, :], rows[0:8, 4, 0:P], start=True, stop=False, skip_group_check=True)
                    for b in range(4 * i, 4 * i + 4):
                        r0 = 32 * (b % 4)
                        for pg in range(NPAGE):
                            mm = pe.matmul(o[r0:r0 + 32, 0:P], pTp[:, i, pg, r0:r0 + 32], nat[:, 8 * b + pg, 0:P],
                                           start=False, stop=(b % 4 == 3 and pg == NPAGE - 1), skip_group_check=True, **wide(r0))
                    close(mm, key)

                def outputs_back():
                    key = ("pOt",)
                    o = open_(key)
                    taken(pe, ("pO", 1))
                    for i in range(2):
                        mm = pe.transpose(o[:, i * P:i * P + P], ctx_row[:, i, :], ident[:, :])
                    close(mm, key)

                steps = {"pcT": page_latents, "pS": lambda i: open_(("pS", i)), "row": page_scores, "pT": page_probs,
                         "pTn": new_probs, "pO": page_outputs, "pOt": outputs_back}
                for key in PAGE_ORDER:
                    steps[key[0]](*key[1:])
                taken(pe, ("pOt",))
                landed(pe, ("uv",))
                for j in range(4):
                    key = ("uv", j)
                    open_(key)
                    for q in range(2):
                        h = 2 * j + q
                        mm = by_feature(key, lambda k: wview(("uv",))[:, 64 * h:64 * h + 64], lambda k: ctxT[:, h, :], 1,
                                        out_rows=slice(64 * q, 64 * q + 64))
                    close(mm, key)

            cross_attention(0)
            experts(0)
            memory_keys_back(1)
            for t in range(NT):
                transpose_x(2, t)
            latent_attention()
            for key in project_and_norm(3):
                if key[0] == "y":
                    out_proj(3, key[2], [("out", 1, i) for i in range(2)], ("uv", 3))
                else:
                    transpose_x(*key[1:])
            cross_attention(1)
            experts(1)

        CHUNKS = [(("qa", j), qaT[:, j, :]) for j in range(4)] + [(("ka", j), kaD[:, j, :]) for j in range(2)]
        CHUNKS += [(("qr", j), qrT[:, j, :]) for j in range(4)] + [(("kr", j), krT[:, j, :]) for j in range(4)]

        def halves(ap):
            if ap.shape[1] == 1024:
                return ap.rearrange("p (a b) -> p a b", a=2)[:, :, 0:HALF]
            return ap.rearrange("p (a b) -> p a b", a=2)

        def score_view(kind, i):
            g, w = BLOCKS[kind][i][2:]
            return pair(att_key(kind, "S", i)).rearrange("p (g w) -> p g w", g=g)[:, :, 0:w]

        def prob_view(kind, i):
            g, w = BLOCKS[kind][i][2:]
            return pbuf[:, (A0[kind] + i) % 2, :].rearrange("p (g w) -> p g w", g=g)[:, :, 0:w]

        def gate_views(i, m):
            o = pair(("g", i, m))
            if m == 0:
                return g_s[:, 0:4, 256 * i:256 * i + 256], o.rearrange("p (t n) -> p t n", t=4)
            return g_s[0:8, 4, 256 * i:256 * i + 256], o[0:8, 0:256]

        @block.scalar
        def _(act):
            def copy(dst, src):
                return act.activation(dst, src, ACT.Copy)

            def take(key, dst, src):
                full(act, key)
                free(copy(dst, src(pair(key)) if callable(src) else src), key)

            def gained(dst, src, i, chunks=range(KD)):
                for k in chunks:
                    ins = act.activation(dst(k), src(k), ACT.Identity, scale=lnc[:, i, 0, k:k + 1], bias=lnc[:, i, 1, k:k + 1])
                return ins

            def take_xT(i, tiles=range(NT)):
                for t in tiles:
                    r = ROWS[t]
                    if i >= 0:
                        key = ("xT", i, t)
                        full(act, key)
                        dst, src = lambda k: xT[:, k, tile_cols(t)], lambda k: pair(key)[:, chunk_cols(k, r)]
                        if i == 2:
                            free(gained(dst, src, i), key)
                            continue
                        gained(dst, src, i, range(SHARE - 1))
                        act.wait_ge(s["xT_shared"], NT * (i - i // 3) + t + 1)
                        free(gained(dst, src, i, range(SHARE - 1, SHARE)), key)
                        continue
                    take(("xT", i, t), xT[:, :, tile_cols(t)].rearrange("p (a k) q -> p a k q", a=2),
                         lambda o: o.rearrange("p (a n) -> p a n", a=2)[:, :, 0:SHARE * r].rearrange("p a (k q) -> p a k q", k=SHARE))

            take_xT(-1)
            def take_memory_features(l):
                for m in range(2):
                    take(("memF", l, m), memF[l][:, :, m * P:m * P + P], lambda o: o.rearrange("p (k q) -> p k q", k=KD))

            def take_memory(l, m):
                key = ("mkv", l, m)
                full(act, key)
                copy(mk[l][:, m, :], pair(key)[:, 0:256])
                free(copy(mv[:, l, m, :], pair(key)[:, 512:768]), key)

            def take_memory_keys(l):
                take(("mkT", l), mkT[:, l, :, :], lambda o: o[:, 0:512].rearrange("p (c q) -> p c q", c=2))

            take_memory_features(0)
            for m in range(2):
                take_memory(0, m)
            take_memory_keys(0)

            def swap(i):
                key = CHUNKS[i][0]
                full(act, key)
                if i >= 2:
                    act.wait_ge(s["rope_done"], i - 1)
                for q in range(4):
                    a, b = 32 * q, 32 * (q ^ 1)
                    ins = copy(halves(swapb[a:a + 32, i % 2, :]), halves(pair(key)[b:b + 32, :]))
                ins.then_inc(s["swapped"], 1)

            for i in range(6):
                swap(i)
            key = ("va",)
            full(act, key)
            copy(v_tok[:, 0:4, 0:P], pair(key)[:, 0:512].rearrange("p (t n) -> p t n", t=4))
            free(copy(v_tok[0:8, 4, 0:P], pair(key)[0:8, 512:640]), key)
            def take_projected(key):
                if key[0] == "qr":
                    swap(6 + key[1])
                elif key[0] == "kr":
                    swap(10 + key[1])
                elif key[0] == "vr":
                    i = key[1]
                    if key[2] == 0:
                        take(key, v_tok[:, 0:4, P + 256 * i:P + 256 * i + 256], lambda o: o.rearrange("p (t n) -> p t n", t=4))
                    else:
                        take(key, v_tok[0:8, 4, P + 256 * i:P + 256 * i + 256], lambda o: o[0:8, 0:256])
                else:
                    full(act, key)
                    g, o = gate_views(*key[1:])
                    act.activation(g, o, ACT.Exp, scale=-1.0).then_inc(s["g_exp"], 1)

            def between(n):
                for key in SWA_WEAVE[n]:
                    take_projected(key)

            key = ("kaTok",)
            full(act, key)
            copy(ka_tok[:, :], pair(key)[:, 0:P])
            free(copy(sRs[0:8, :], pair(key)[0:8, P:2 * P]), key)
            take_projected(("qr", 0))

            def attention(kind, between=lambda n: None):
                base = A0[kind]
                blocks = BLOCKS[kind]

                def exps(i):
                    n = base + i
                    g = blocks[i][2]
                    act.wait_ge(s["negmax_ready"], n + 1)
                    if kind == "swa":
                        act.activation(sinke[:, n % 2, :], sinke[:, n % 2, :], ACT.Exp)
                    for h in range(g):
                        ins = act.activation(prob_view(kind, i)[:, h, :], score_view(kind, i)[:, h, :], ACT.Exp,
                                             bias=negmax[:, n % 2, h:h + 1], scale=SCALE[kind],
                                             accum_out=rowsum[:, n % 2, h:h + 1])
                    free(ins, att_key(kind, "S", i))

                def outputs(i):
                    n, h0, g, w = blocks[i]
                    cols = g * w
                    take(att_key(kind, "T", i), pT[:, (base + i) % 2, 0:cols], lambda o: o[:, 0:cols])
                    if kind == "mla":
                        take(att_key(kind, "O", i), ctxT[:, h0:h0 + g, tile_cols(n)],
                             lambda o: o[:, 0:g * P].rearrange("p (g q) -> p g q", g=g))
                    elif kind == "swa":
                        take(att_key(kind, "O", i), o_swa[h0 // 4][:, :, tile_cols(n)],
                             lambda o: o[:, 0:256].rearrange("p (c q) -> p c q", c=2))
                    else:
                        take(att_key(kind, "O", i), oT[:, h0 // 2:h0 // 2 + 2, tile_cols(n)],
                             lambda o: o[:, 0:256].rearrange("p (c q) -> p c q", c=2))

                exps(0)
                for i in range(len(blocks)):
                    if i + 1 < len(blocks):
                        exps(i + 1)
                    between(i)
                    outputs(i)

            n_rows = [0]

            def row_exps(dst, count, w, scale, sink):
                n_rows[0] += 1
                act.wait_ge(s["row_neg"], n_rows[0])
                if sink:
                    act.activation(st[0:count, 27:28], st[0:count, 27:28], ACT.Exp)
                act.activation(dst[0:count, 0:w], dst[0:count, 0:w], ACT.Exp, bias=st[0:count, 26:27], scale=scale,
                               accum_out=st[0:count, 28:29]).then_inc(s["row_exp"], 1)

            attention("swa", between)
            for kv in range(2):
                for h in range(2):
                    copy(qas[64 * kv:64 * kv + 64, h::2, :], qaT[64 * h:64 * h + 64, 2 * kv:2 * kv + 2, 512:520])
            for key in SWA_SAMPLE:
                if key[0] in ("vr", "g"):
                    take_projected(key)
                elif key == ("kwT",):
                    take(key, pbuf[:, 0, :], lambda o: o)
                elif key == ("swS",):
                    take(key, sTs.rearrange("p (b k h) -> p k b h", b=8, k=2),
                         lambda o: o.rearrange("p (k n) -> p k n", k=2)[:, :, 0:32].rearrange("p k (b h) -> p k b h", b=8))
                elif key == ("swT",):
                    row_exps(sRs, 64, P, 0.125, True)
                    take(key, pTs_sw, lambda o: o[:, 0:64])
                elif key == ("swO",):
                    take(key, o_swa_s, lambda o: o[:, 0:32].rearrange("p (c b) -> p c b", c=4))

            def take_gated(n):
                r = ROWS[n]
                take(("retG", n), oT[:, 4:8, tile_cols(n)], lambda o: o[:, 0:4 * r].rearrange("p (c q) -> p c q", c=4))

            for n in range(3):
                take_gated(n)
            full(act, ("skT",))
            free(act.activation(ks_tok[0:8, :], pair(("skT",))[0:8, 0:512], ACT.Copy, scale=0.125), ("skT",))
            take_gated(3)
            take(("sO",), soT, lambda o: o[:, 0:32].rearrange("p (c b) -> p c b", c=4))
            taken(act, ("sU", 3))
            for par in range(2):
                for b in range(DB):
                    act.dma_start(ret_s[0, b].rearrange("(j t) k e -> t k j e", t=2)[par],
                                  Ss[par * 64:par * 64 + 64, b, :, :]).then_inc(s["states_out"], 16)
                act.dma_start(ret_p[0, 0].rearrange("(j t) k e -> t k j e", t=2)[par], S[par * 64:par * 64 + 64, :, :]
                              ).then_inc(s["states_out"], 16)
            take_gated(4)

            def cross_attention(l):
                for j in range(2):
                    take(("mq", l, j), halves(qmT[:, j, :]), halves)
                act.wait_ge(s["states_out"], 16 * 2 * (DB + 1))
                attention(f"mem{l}")
                if l == 0:
                    act.dma_start(mem_tok[1], io["mem_prompt"][0].rearrange("(m p) d -> p m d", p=P)).then_inc(s["mem_loaded"], 16)

                act.wait_ge(s["q_wide_zero"], l + 1)
                for h in range(4):
                    q = 64 * (h % 2)
                    ins = copy(q_wide[q:q + 64, h // 2, :, h], qmT[q:q + 64, h // 2, 512:520])
                ins.then_inc(s["q_wide_ready"], 1)
                for g in range(4):
                    take(("kcT", l, g), KcT[:, g % 2, :, :, :], lambda o: o.rearrange("p (a b c) -> p a b c", a=2, b=2))
                key = ("msS", l)
                n_rows[0] += 1
                act.wait_ge(s["row_neg"], n_rows[0])
                for i in range(2):
                    ins = act.activation(sRm[:, i, :], pair(key)[:, 512 * i:512 * i + 256], ACT.Exp, bias=st[:, 26 + i:27 + i],
                                         scale=0.125, accum_out=st[:, 28 + i:29 + i])
                free(ins, key)
                take(("msT", l), pTm, lambda o: o[:, 0:512].rearrange("p (i c r) -> p i c r", i=2, c=2))
                take_xT(3 * l + 1, range(1))
                take(("msO", l), oT[:, 0:2, 512:520], lambda o: o[:, 0:16].rearrange("p (c b) -> p c b", c=2))

            def experts(l):
                if l == 0:
                    take_memory_features(1)
                for n in range(2):
                    act.wait_ge(s["router_neg"], 2 * l + n + 1)
                    v = (rA, rs[:, 5:6, :])[n]
                    act.activation(v, v, ACT.Exp).then_inc(s["router_exp"], 1)
                if l == 0:
                    take_memory(1, 0)

                def features(o):
                    return lambda k: o[:, chunk_cols(k, CAP)]

                def step_x(e):
                    key = ("moeX", l, e)
                    full(act, key)
                    if e >= 2:
                        full(act, ("moeH", l, e - 2))
                    free(gained(lambda k: xsT[:, e % 2, k, :], features(pair(key)), 3 * l + 1), key)

                def step_h(e):
                    key = ("moeH", l, e)
                    full(act, key)
                    if e >= 2:
                        taken(act, ("moeH", l, e - 2))
                    act.activation(ex[:, e % 2, :, :], pair(key)[:, 0:2 * CAP].rearrange("p (c q) -> p c q", c=2), ACT.Exp, scale=-1.0
                                   ).then_inc(s["moe_exp"], 1)

                def step_y(e):
                    key = ("moeY", l, e)
                    if e >= 2:
                        act.wait_ge(y_out[e % 2], 16 * uses(NE, 2, l, e - 2))
                    take(key, ybuf[0:CAP, e % 2, :], lambda o: o[0:CAP, :])
                    taken(act, key)
                    act.dma_start(y_rows.rearrange("(s b) d -> s b d", b=NB)[:, e, :], ybuf[0:CAP, e % 2, :]).then_inc(y_out[e % 2], 16)

                steps = {"X": step_x, "H": step_h, "Y": step_y}
                for st_, e in expert_order():
                    steps[st_](e)

                if l == 0:
                    take_memory(1, 1)
                sem_ = spill_s[l]
                with spilled(act, l):
                    act.wait_ge(y_out[0], 16 * uses(NE, 2, l, NE - 2))
                    for j in range(SPILL):
                        act.wait_ge(sem_["pe"], 3 * j + 1)
                        gained(lambda k: xsT[:, 0, k, :], features(PS[:, 0, :]), 3 * l + 1).then_inc(sem_["act"], 1)
                        act.wait_ge(sem_["pe"], 3 * j + 2)
                        act.activation(ex[:, 0, :, :], PS[:, 1, 0:2 * CAP].rearrange("p (c q) -> p c q", c=2), ACT.Exp, scale=-1.0
                                       ).then_inc(sem_["act"], 1)
                        act.wait_ge(sem_["pe"], 3 * j + 3)
                        if j:
                            act.wait_ge(sem_["y_out"], 16 * j)
                        copy(ybuf[0:CAP, 0, :], PS[0:CAP, 2, :]).then_inc(sem_["act"], 1)
                        act.wait_ge(sem_["act"], 3 * j + 3)
                        act.dma_start(y_rows.rearrange("(s b) d -> s b d", b=NB)[:, NE + j, :], ybuf[0:CAP, 0, :]
                                      ).then_inc(sem_["y_out"], 16)

                if l == 0:
                    take_memory_keys(1)
                for t in range(NT):
                    r = ROWS[t]
                    act.wait_ge(y_in[t], 32 * (l + 1))
                    v = y_of[0:r, 0, t, :]
                    act.activation(v, v, ACT.Copy, scale=rs[0:r, 8, t:t + 1]).then_inc(s["y_scaled"], 1)

            def latent_attention():
                take(("ukT",), ukT, lambda o: o[:, 0:512].rearrange("p (c q) -> p c q", c=4))
                act.wait_ge(s["odd_in"], 32)

                def back(t):
                    key = ("oinT", t)
                    full(act, key)
                    o = pair(key)
                    r = ROWS[t]
                    for c in range(2):
                        act.activation(cqT[:, c, tile_cols(t)], o[:, c * P:c * P + r], ACT.Copy, scale=qg[:, c:c + 1])
                    copy(ckvT[:, tile_cols(t)], o[:, 2 * P:2 * P + r])
                    free(copy(krT4[:, tile_cols(t)], o[:, 3 * P:3 * P + r]), key)

                for t in range(NT):
                    key = ("oin", t)
                    r = ROWS[t]
                    full(act, key)
                    if t:
                        act.wait_ge(s["sq_done"], t)
                    act.activation(scratch[0:r, 0:256], pair(key)[0:r, 0:256], ACT.Square, accum_out=rms[0:r, t % 2, 0:1])
                    act.activation(scratch[0:r, 256:384], pair(key)[0:r, 256:384], ACT.Square,
                                   accum_out=rms[0:r, t % 2, 1:2]).then_inc(s["sq_done"], 1)
                    if t:
                        back(t - 1)
                back(4)
                for j in (1, 3):
                    take(("qn", j), halves(qnT[:, j, :]), halves)
                for h in (1, 3, 5, 7):
                    take(("ql", h), halves(q_lat[:, h, :]), halves)
                for t in range(4):
                    take(("qrT", t), qrT2[:, :, tile_cols(t)], lambda o: o[:, 0:256].rearrange("p (c q) -> p c q", c=2))
                taken(act, ("ql", 6))
                taken(act, ("ql", 7))
                act.wait_ge(s["qrS_zero"], 1)
                copy(qlS[:, :, 0:8], q_lat[:, :, 512:520].rearrange("p h b -> p b h"))
                full(act, ("qrT", 4))
                for q in range(4):
                    ins = copy(qrS[32 * q:32 * q + 32, q, :, 0:8], pair(("qrT", 4))[32 * q:32 * q + 32, 0:64].rearrange("p (h b) -> p b h", h=8))
                free(ins, ("qrT", 4))
                act.wait_ge(s["moe_done"], 1)
                attention("mla")
                for g in range(2):
                    take(("pkT", g), krp[:, 8 * g:8 * g + 8, :], lambda o: o.rearrange("p (c q) -> p c q", c=8))

                def page_latents(b):
                    if b % 2:
                        take(("pcT", b), ckvp[:, b % 2, :], lambda o: o)

                def page_exps(i):
                    key = ("pS", i)
                    n_rows[0] += 1
                    act.wait_ge(s["row_neg"], n_rows[0])
                    v = srow[i]
                    act.activation(v[:, 1024:1032], v[:, 1024:1032], ACT.Exp, bias=st[:, 26:27], scale=SCALE["mla"], accum_out=st[:, 29:30])
                    free(act.activation(v[:, 0:1024], pair(key), ACT.Exp, bias=st[:, 26:27], scale=SCALE["mla"],
                                        accum_out=st[:, 28:29]), key)

                steps = {"pcT": page_latents, "pS": lambda i: None,
                         "row": lambda b: page_exps(b // 4) if b % 4 == 3 else None,
                         "pT": lambda i: take(("pT", i), pTp[:, i, :, :], lambda o: o.rearrange("p (g r) -> p g r", g=NPAGE)),
                         "pTn": lambda i: take(("pTn", i), pTn[0:8, i, :], lambda o: o[0:8, 0:P]),
                         "pO": lambda i: take(("pO", i), ctx_row[:, i, :], lambda o: o[:, 0:P])}
                for key in PAGE_ORDER[:-1]:
                    steps[key[0]](*key[1:])
                key = ("pOt",)
                full(act, key)
                for i in range(2):
                    ins = copy(ctxT[:, :, 512 + 4 * i:516 + 4 * i].rearrange("p h b -> p b h"),
                               pair(key)[:, i * P:i * P + P].rearrange("p (b h) -> p b h", b=4)[:, :, 0:8])
                free(ins, key)
                for j in range(4):
                    take(("uv", j), halves(oT[:, j, :]), halves)

            act.wait_ge(s["lnc_in"], 16)
            take_xT(0)
            cross_attention(0)
            take_xT(1, range(1, NT))
            experts(0)
            take_xT(2)
            latent_attention()
            take_xT(3)
            cross_attention(1)
            take_xT(4, range(1, NT))
            experts(1)
            for t in range(NT):
                if t < NT - 1:
                    act.wait_ge(s["x_ready"], NT * 5 + t + 1)
                else:
                    act.wait_ge(s["last_ready"], 1)
                dst = y_prompt[0, t * P:t * P + P] if t < 4 else y_sample.rearrange("b s d -> (b s) d")
                act.dma_start(dst, x[0:ROWS[t], t, :]).then_inc(s["x_stored"], 16)
            act.wait_ge(s["x_stored"], 16 * NT)

        @block.vector
        def _(dve):
            steps = [0]

            def link(ins):
                ins.then_inc(s["vec_step"], 1)
                steps[0] += 1
                dve.wait_ge(s["vec_step"], steps[0])

            dve.wait_ge(s["const_in"], 16 * 7)
            def rotate_chunk(i):
                key, dst = CHUNKS[i]
                full(dve, key)
                dve.wait_ge(s["swapped"], i + 1)
                d = halves(dst)
                free(dve.tensor_tensor(d, halves(pair(key)), halves(cosf[:, :]), ALU.mult), key)
                link(dve.tensor_tensor(swapb[:, i % 2, :], swapb[:, i % 2, :], sinf[:, :], ALU.mult))
                dve.tensor_tensor(dst, dst, swapb[:, i % 2, :], ALU.add).then_inc(s["rope_done"], 1)

            def gate(i, m):
                g, o = gate_views(i, m)
                dve.wait_ge(s["g_exp"], 2 * i + m + 1)
                link(dve.tensor_scalar(g, g, 1.0, None, ALU.add))
                link(dve.reciprocal(g, g))
                free(dve.tensor_tensor(g, o, g, ALU.mult), ("g", i, m))

            def between(n):
                for key in SWA_WEAVE[n]:
                    if key[0] in ("qr", "kr"):
                        rotate_chunk((6 if key[0] == "qr" else 10) + key[1])

            for i in range(7):
                rotate_chunk(i)

            def attention(kind, between=lambda n: None):
                base = A0[kind]
                blocks = BLOCKS[kind]

                def maxima(i):
                    n = base + i
                    m = n % 2
                    t, h0, g, w = blocks[i]
                    full(dve, att_key(kind, "S", i))
                    v = score_view(kind, i)
                    if kind == "swa":
                        link(dve.tensor_tensor(v, v, band[:, 256 - w:256].unsqueeze(1).to_broadcast([P, g, w]), ALU.add))
                    if kind == "mla":
                        d = v[:, :, w - P:w]
                        link(dve.tensor_tensor(d, d, band[:, P:256].unsqueeze(1).to_broadcast([P, g, P]), ALU.add))
                    link(dve.tensor_reduce(rowmax[:, m, 0:g], v, AX.X, ALU.max))
                    if kind == "swa":
                        sk = sinkb[:, h0:h0 + g]
                        link(dve.scalar_tensor_tensor(rowmax[:, m, 0:g], rowmax[:, m, 0:g], SCALE[kind], sk, ALU.mult, ALU.max))
                        dve.tensor_scalar(negmax[:, m, 0:g], rowmax[:, m, 0:g], -1.0, None, ALU.mult)
                        dve.tensor_tensor(sinke[:, m, 0:g], sk, rowmax[:, m, 0:g], ALU.subtract).then_inc(s["negmax_ready"], 1)
                    else:
                        dve.tensor_scalar(negmax[:, m, 0:g], rowmax[:, m, 0:g], -SCALE[kind], None, ALU.mult
                                          ).then_inc(s["negmax_ready"], 1)

                def scale(i):
                    m = (base + i) % 2
                    g = blocks[i][2]
                    taken(dve, att_key(kind, "S", i))
                    rsum = rowsum[:, m, 0:g]
                    if kind == "swa":
                        link(dve.tensor_tensor(rsum, rsum, sinke[:, m, 0:g], ALU.add))
                    link(dve.reciprocal(rsum, rsum))
                    for h in range(g):
                        v = prob_view(kind, i)[:, h, :]
                        ins = dve.tensor_scalar(v, v, rowsum[:, m, h:h + 1], None, ALU.mult)
                    ins.then_inc(s["probs_ready"], 1)

                maxima(0)
                for i in range(len(blocks)):
                    if i + 1 < len(blocks):
                        maxima(i + 1)
                    scale(i)
                    between(i)

            n_rows = [0]

            def window_rows_softmax():
                key = ("swR",)
                full(dve, key)
                v = sRs[0:64, :]
                free(dve.tensor_copy(v, pair(key)[0:64, 0:P]), key)
                taken(dve, key)
                c = lambda i: st[0:64, i:i + 1]
                link(dve.tensor_reduce(c(24), v, AX.X, ALU.max))
                link(dve.scalar_tensor_tensor(c(25), c(24), SCALE["swa"], sinkr[:, :], ALU.mult, ALU.max))
                dve.tensor_scalar(c(26), c(25), -1.0, None, ALU.mult)
                dve.tensor_tensor(c(27), sinkr[:, :], c(25), ALU.subtract).then_inc(s["row_neg"], 1)
                dve.wait_ge(s["row_exp"], 1)
                link(dve.tensor_tensor(c(28), c(28), c(27), ALU.add))
                link(dve.reciprocal(c(29), c(28)))
                dve.tensor_scalar(v, v, c(29), None, ALU.mult).then_inc(s["row_probs"], 1)

            def memory_rows_softmax(l):
                key = ("msS", l)
                full(dve, key)
                link(dve.tensor_reduce(st[:, 24:26], pair(key).rearrange("p (i w) -> p i w", i=2)[:, :, 0:256], AX.X, ALU.max))
                dve.tensor_scalar(st[:, 26:28], st[:, 24:26], -SCALE["mem0"], None, ALU.mult).then_inc(s["row_neg"], 1)
                taken(dve, key)
                link(dve.reciprocal(st[:, 30:32], st[:, 28:30]))
                for i in range(2):
                    ins = dve.tensor_scalar(sRm[:, i, :], sRm[:, i, :], st[:, 30 + i:31 + i], None, ALU.mult)
                ins.then_inc(s["row_probs"], 1)

            dve.wait_ge(s["sink_in"], 32)
            attention("swa", between)
            gate(0, 0)
            window_rows_softmax()
            for i, m in ((0, 1), (1, 0), (1, 1)):
                gate(i, m)

            n_rstd = [0]

            def variance(ins):
                ins.then_inc(s["var_ready"], 1)
                n_rstd[0] += 1
                return n_rstd[0]

            def decayed_scores(n):
                full(dve, ("retS", n))
                free(dve.tensor_tensor(retP, pair(("retS", n)).rearrange("p (h q) -> p h q", h=8), decay[:, :, :], ALU.mult), ("retS", n))

            def decayed_keys(n):
                full(dve, ("retK", n))
                free(dve.tensor_tensor(kd.rearrange("p (h e) -> p h e", h=8), pair(("retK", n))[:, 0:512].rearrange("p (h e) -> p h e", h=8),
                                       small[:, 0:8].unsqueeze(2).to_broadcast([P, 8, 64]), ALU.mult), ("retK", n))

            def new_state(n):
                key = ("retU", n)
                full(dve, key)
                u = pair(key)[:, 0:512].rearrange("p (j e) -> p j e", j=4)
                if n == 0:
                    dve.tensor_copy(S[0:64, :, :], u[0:64, :, 0:64])
                    free(dve.tensor_copy(S[64:P, :, :], u[64:P, :, 64:P]), key)
                    return
                taken(dve, ("retU", n - 1))
                link(dve.tensor_tensor(S, S, small[:, 8:12].unsqueeze(2).to_broadcast([P, 4, 64]), ALU.mult))
                dve.tensor_tensor(S[0:64, :, :], u[0:64, :, 0:64], S[0:64, :, :], ALU.add)
                free(dve.tensor_tensor(S[64:P, :, :], u[64:P, :, 64:P], S[64:P, :, :], ALU.add), key)

            def head_views(n):
                r = ROWS[n]
                flat = o_t[0:r, n % 2, :]
                return flat, flat.rearrange("p (h e) -> p h e", h=8), st[0:r, 8:16], st[0:r, 16:24]

            def centred(n):
                key = ("retO", n) if n < 4 else ("sOt",)
                r = ROWS[n]
                full(dve, key)
                if n >= 2:
                    full(dve, ("retG", n - 2))
                flat, heads, mean, var = head_views(n)
                by_bank = flat.rearrange("p (c q e) -> p q c e", c=4, q=2)
                if n < 4:
                    o = pair(key)[0:r, :].rearrange("p (q n) -> p q n", q=2)[:, :, 0:256].rearrange("p q (c e) -> p q c e", c=4)
                else:
                    o = pair(key)[0:r, 0:512].rearrange("p (c q e) -> p q c e", c=4, q=2)
                mean_b = mean.rearrange("p (c q) -> p q c", q=2)
                link(dve.tensor_reduce(mean_b, o, AX.X, ALU.add))
                link(dve.tensor_scalar(mean, mean, 1.0 / 64, None, ALU.mult))
                free(dve.tensor_tensor(by_bank, o, mean_b.unsqueeze(3).to_broadcast([r, 2, 4, 64]), ALU.subtract), key)

            def gated(n):
                r = ROWS[n]
                flat, heads, mean, var = head_views(n)
                sqr = o_u[0:r, :].rearrange("p (h e) -> p h e", h=8)
                wide = lambda a: a.unsqueeze(2).to_broadcast([r, 8, 64])
                taken(dve, ("retO", n) if n < 4 else ("sOt",))
                link(dve.tensor_tensor(sqr, heads, heads, ALU.mult))
                link(dve.tensor_reduce(var, sqr, AX.X, ALU.add))
                dve.wait_ge(s["rstd_ready"], variance(dve.tensor_scalar(var, var, 1.0 / 64, EPS, ALU.mult, ALU.add)))
                link(dve.tensor_tensor(heads, heads, wide(var), ALU.mult))
                link(dve.tensor_tensor(flat, flat, gng[0:r, 0, :], ALU.mult))
                link(dve.tensor_tensor(flat, flat, gng[0:r, 1, :], ALU.add))
                dve.tensor_tensor(flat, flat, g_s[0:r, n, :], ALU.mult).then_inc(s["gated_ready"], 1)

            dve.wait_ge(s["gn_in"], 32)
            taken(dve, ("g", 1, 1))
            for n in range(4):
                if n:
                    centred(n - 1)
                decayed_scores(n)
                decayed_keys(n)
                if n:
                    gated(n - 1)
                new_state(n)
            centred(3)
            gated(3)
            dve.wait_ge(s["state_in"], 16 * 16)

            def new_sample_state(j):
                key = ("sU", j)
                full(dve, key)
                u = pair(key).rearrange("p (b e) -> p b e", b=DB)
                for q in (0, 64):
                    ins = dve.scalar_tensor_tensor(Ss[q:q + 64, :, j, :], Ss[q:q + 64, :, j, :], small[q:q + 64, 12 + j:13 + j],
                                                   u[q:q + 64, :, q:q + 64], ALU.mult, ALU.add)
                free(ins, key)

            def norm(i):
                def stats(t):
                    r = ROWS[t]
                    xt = x[0:r, t, :]
                    if i:
                        dve.wait_ge(s["x_ready"], NT * (i - 1) + t + 1)
                    else:
                        dve.wait_ge(x_in[t], 16)
                    if i % 3 < 2:
                        key = ("y", i, t)
                        full(dve, key)
                        free(dve.scalar_tensor_tensor(xt, xt, ALPHA, pair(key)[0:r, :], ALU.mult, ALU.add), key)
                        taken(dve, key)
                    else:
                        n = NT * (i // 3) + t + 1
                        dve.wait_ge(s["y_scaled"], n)
                        y1, y2 = (y_of[0:r, c, t, :] for c in range(2))
                        link(dve.scalar_tensor_tensor(y1, y2, rs[0:r, 9, t:t + 1], y1, ALU.mult, ALU.add))
                        dve.scalar_tensor_tensor(xt, xt, ALPHA, y1, ALU.mult, ALU.add).then_inc(s["combined"], 1)
                        dve.wait_ge(s["combined"], n)
                    dve.bn_stats(bns[0:r, 0, :], xt[:, 0:512])
                    link(dve.bn_stats(bns[0:r, 1, :], xt[:, 512:1024]))
                    link(dve.bn_aggr(mv_t[0:r, t % 2, :], bns[0:r, :, :]))
                    return variance(dve.tensor_scalar(rstd[0:r, t % 2, 0:1], mv_t[0:r, t % 2, 1:2], EPS, None, ALU.add))

                def normalise(t, n):
                    r = ROWS[t]
                    xt = x[0:r, t, :]
                    dve.wait_ge(s["rstd_ready"], n)
                    ins = dve.tensor_scalar(xt, xt, mv_t[0:r, t % 2, 0:1], rstd[0:r, t % 2, 0:1], ALU.subtract, ALU.mult)
                    if i == 3 * DEPTH - 1 and t not in POOL_GAINS:
                        link(ins)
                        dve.wait_ge(s["ln_in"], 32 * (i + 1))
                        ins = dve.tensor_tensor(xt, xt, lnb[0:r, 0, :], ALU.mult)
                    if i == 3 * DEPTH - 1 and t == NT - 1:
                        link(ins)
                        dve.tensor_tensor(xt, xt, lnb[0:r, 1, :], ALU.add).then_inc(s["last_ready"], 1)
                    else:
                        ins.then_inc(s["ln_norm"], 1)

                def to_xT(t):
                    key = ("xT", i, t)
                    r = ROWS[t]
                    full(dve, key)
                    for k in range(SHARE, KD):
                        ins = dve.tensor_scalar(xT[:, k, tile_cols(t)], pair(key)[:, chunk_cols(k, r)], lnc[:, i, 0, k:k + 1],
                                                lnc[:, i, 1, k:k + 1], ALU.mult, ALU.add)
                    ins.then_inc(s["xT_shared"], 1)

                if i == 0:
                    for j in range(2):
                        new_sample_state(j)
                n = stats(0)
                if i == 0:
                    for j in range(2, 4):
                        new_sample_state(j)
                for t in range(NT):
                    more = stats(t + 1) if t + 1 < NT else None
                    normalise(t, n)
                    n = more
                    if i == 0 and t == 1:
                        centred(4)
                        gated(4)
                    if i % 3 < 2 and t:
                        to_xT(t - 1)
                if i % 3 < 2:
                    to_xT(NT - 1)

            def first_max(out, m, v, tmp):
                mb = m.unsqueeze(2).to_broadcast([P, NT, 4])
                io4 = small[:, 32:36].unsqueeze(1).to_broadcast([P, NT, 4])
                link(dve.tensor_tensor(tmp, v, mb, ALU.is_equal))
                link(dve.tensor_tensor(tmp, tmp, io4, ALU.mult))
                link(dve.tensor_reduce(rs[:, 11, :], tmp, AX.X, ALU.min))
                link(dve.tensor_tensor(out, rs[:, 11, :].unsqueeze(2).to_broadcast([P, NT, 4]), io4, ALU.is_equal))

            def router(l):
                key = ("rt", l)
                link(dve.memset(L, 0.0))
                full(dve, key)
                o = pair(key)[:, 0:NT * 32].rearrange("p (t n) -> p t n", t=NT)
                dve.tensor_tensor(L[:, 0:4, :], o[:, 0:4, 0:20], rb[:, l, :].unsqueeze(1).to_broadcast([P, 4, 20]), ALU.add)
                free(dve.tensor_tensor(L[0:8, 4, :], o[0:8, 4, 0:20], rb[0:8, l, :], ALU.add), key)
                taken(dve, key)
                gl = L[:, :, 0:4]
                wide = lambda i: rs[:, i, :].unsqueeze(2).to_broadcast([P, NT, 4])
                link(dve.tensor_reduce(rs[:, 0, :], gl, AX.X, ALU.max))
                first_max(oh, rs[:, 0, :], gl, rB)
                dve.tensor_tensor(rA, gl, wide(0), ALU.subtract).then_inc(s["router_neg"], 1)
                pr = prod.rearrange("p t (g e) -> p t g e", g=4)
                link(dve.tensor_tensor(pr, L[:, :, 4:20].rearrange("p t (g e) -> p t g e", g=4),
                                       oh.unsqueeze(3).to_broadcast([P, NT, 4, 4]), ALU.mult))
                link(dve.tensor_reduce(el4, prod.rearrange("p t (g e) -> p t e g", g=4), AX.X, ALU.add))
                link(dve.tensor_reduce(rs[:, 1, :], el4, AX.X, ALU.max))
                first_max(oh1, rs[:, 1, :], el4, rB)
                link(dve.scalar_tensor_tensor(el4, oh1, NEG, el4, ALU.mult, ALU.add))
                link(dve.tensor_reduce(rs[:, 2, :], el4, AX.X, ALU.max))
                first_max(oh2, rs[:, 2, :], el4, rB)
                dve.tensor_tensor(rs[:, 5, :], rs[:, 2, :], rs[:, 1, :], ALU.subtract).then_inc(s["router_neg"], 1)
                for c, o_c in enumerate((oh1, oh2)):
                    link(dve.tensor_tensor(picks[:, c].rearrange("p t (g e) -> p t g e", g=4), oh.unsqueeze(3).to_broadcast([P, NT, 4, 4]),
                                           o_c.unsqueeze(2).to_broadcast([P, NT, 4, 4]), ALU.mult))
                link(dve.tensor_tensor(picked, picks[:, 0], picks[:, 1], ALU.add))
                dve.tensor_tensor(picked[:, NT - 1, :], picked[:, NT - 1, :], small[:, FILLED:FILLED + 1].to_broadcast([P, NE]), ALU.mult
                                  ).then_inc(s["picks_ready"], 1)
                dve.wait_ge(s["router_exp"], 2 * l + 2)
                link(dve.tensor_reduce(rs[:, 6, :], rA, AX.X, ALU.add))
                link(dve.scalar_tensor_tensor(rs[:, 7, :], rs[:, 5, :], 1.0, rs[:, 6, :], ALU.add, ALU.mult))
                link(dve.reciprocal(rs[:, 8, :], rs[:, 7, :]))
                link(dve.tensor_tensor(rs[:, 9, :], rs[:, 8, :], rs[:, 5, :], ALU.mult))
                rank, expert, before, step, blk, place = (pl[:, i] for i in range(6))
                sel_of = lambda v: v.unsqueeze(1).to_broadcast([P, 2 * NT, NE])
                picks_f, sel_f = (v.rearrange("p c t e -> p (c t) e") for v in (picks, sel))
                flat = lambda v: v.rearrange("p c t -> p (c t)")
                link(dve.tensor_tensor(sel_f, picks_f, sel_of(small[:, IOTA:IOTA + NE]), ALU.mult))
                link(dve.tensor_reduce(flat(expert), sel_f, AX.X, ALU.add))
                key = ("rank", l)
                full(dve, key)
                o = pair(key)
                limits = small[:, LIMITS:LIMITS + STEPS]
                spills, spills_before, spills_to = (per_e[:, i, :] for i in range(3))
                ranks = o[:, 0:NT * NE].rearrange("p (t e) -> p t e", t=NT)
                of_tile = o[:, 512:512 + NT * NE].rearrange("p (t e) -> p t e", t=NT)
                link(dve.tensor_copy(so_far[:, 1, :], of_tile[:, 0, :]))
                for t in range(1, NT):
                    link(dve.tensor_tensor(so_far[:, t + 1, :], so_far[:, t, :], of_tile[:, t, :], ALU.add))
                link(dve.tensor_tensor(so_far[:, 1:NT, :], so_far[:, 1:NT, :], ranks[:, 1:NT, :], ALU.add))
                free(dve.tensor_copy(so_far[:, 0, :], ranks[:, 0, :]), key)
                link(dve.tensor_tensor(more, so_far[:, NT, :].unsqueeze(2).to_broadcast([P, NE, STEPS]),
                                       limits.unsqueeze(1).to_broadcast([P, NE, STEPS]), ALU.is_gt))
                taken(dve, key)
                link(dve.tensor_reduce(spills, more, AX.X, ALU.add))
                link(dve.tensor_tensor(pre, spills.unsqueeze(1).to_broadcast([P, NE, NE]),
                                       route[:, 2:4, :].rearrange("p a (b c) -> p (a b) c", c=NE), ALU.mult))
                link(dve.tensor_reduce(spills_before, pre, AX.X, ALU.add))
                link(dve.tensor_tensor(spills_to, spills_before, spills, ALU.add))
                link(dve.tensor_tensor(sel, picks, so_far[:, 0:NT, :].unsqueeze(1).to_broadcast([P, 2, NT, NE]), ALU.mult))
                link(dve.tensor_reduce(flat(rank), sel_f, AX.X, ALU.add))
                link(dve.tensor_tensor(sel_f, picks_f, sel_of(spills_before), ALU.mult))
                link(dve.tensor_reduce(flat(before), sel_f, AX.X, ALU.add))
                m = more.rearrange("p e s -> p (e s)")[:, 0:2 * NT * STEPS].rearrange("p (n s) -> p n s", s=STEPS)
                link(dve.tensor_tensor(m, flat(rank).unsqueeze(2).to_broadcast([P, 2 * NT, STEPS]),
                                       limits.unsqueeze(1).to_broadcast([P, 2 * NT, STEPS]), ALU.is_ge))
                link(dve.tensor_reduce(flat(step), m, AX.X, ALU.add))
                link(dve.tensor_tensor(blk, before, step, ALU.add))
                link(dve.scalar_tensor_tensor(blk, blk, float(NE - 1), expert, ALU.add, ALU.subtract))
                link(dve.tensor_scalar(before, step, 1.0, None, ALU.min))
                link(dve.tensor_tensor(blk, blk, before, ALU.mult))
                link(dve.tensor_tensor(blk, blk, expert, ALU.add))
                link(dve.scalar_tensor_tensor(place, step, -float(CAP), rank, ALU.mult, ALU.add))
                link(dve.tensor_tensor(hot_block, flat(blk).unsqueeze(2).to_broadcast([P, 2 * NT, NB]),
                                       small[:, IOTA:IOTA + NB].unsqueeze(1).to_broadcast([P, 2 * NT, NB]), ALU.is_equal))
                numbers = small[:, TOKENS:TOKENS + NT]
                for c in range(2):
                    hb = hot_block[:, NT * c:NT * c + NT, :]
                    dve.tensor_tensor(hb, hb, numbers.unsqueeze(2).to_broadcast([P, NT, NB]), ALU.mult)
                dve.tensor_tensor(hot_place, flat(place).unsqueeze(2).to_broadcast([P, 2 * NT, CAP]),
                                  small[:, IOTA:IOTA + CAP].unsqueeze(1).to_broadcast([P, 2 * NT, CAP]), ALU.is_equal
                                  ).then_inc(s["places_ready"], 1)
                link(dve.scalar_tensor_tensor(places[:, :, :], place, float(NB), blk, ALU.mult, ALU.add))
                sel1 = pre.rearrange("p a b -> p (a b)")[0:1, 0:SPILL * NE].rearrange("p (j e) -> p j e", e=NE)
                link(dve.tensor_tensor(sel1, spills_to[0:1, :].unsqueeze(1).to_broadcast([1, SPILL, NE]),
                                       small[0:1, IOTA:IOTA + SPILL].unsqueeze(2).to_broadcast([1, SPILL, NE]), ALU.is_le))
                link(dve.tensor_copy(sp_f[0:1, 0:1], spills_to[0:1, NE - 1:NE]))
                link(dve.tensor_reduce(sp_f[0:1, 1:], sel1, AX.X, ALU.add))
                link(dve.tensor_scalar(spill[:, :], sp_f[0:1, :], float(NE - 1), None, ALU.min))
                key = ("table", l)
                full(dve, key)
                free(dve.tensor_copy(block_tokens[:, :], pair(key)[0:CAP, 0:NB]), key)

            def experts(l):
                router(l)

                def gated_units(o, sg, dst, link=link):
                    a, b = (o[:, 512 * i:512 * i + 2 * CAP].rearrange("p (c q) -> p c q", c=2) for i in range(2))
                    link(dve.tensor_scalar(sg, sg, 1.0, None, ALU.add))
                    link(dve.reciprocal(sg, sg))
                    link(dve.tensor_tensor(sg, a, sg, ALU.mult))
                    return dve.tensor_tensor(dst, b, sg, ALU.mult)

                for e in range(NE):
                    key = ("moeH", l, e)
                    dve.wait_ge(s["moe_exp"], NE * l + e + 1)
                    if e >= 2:
                        full(dve, ("moeY", l, e - 2))
                    free(gated_units(pair(key), ex[:, e % 2, :, :], actT[:, e % 2, :, :]), key)
                sem_ = spill_s[l]

                def link_spilled(ins):
                    ins.then_inc(sem_["dve"], 1)
                    steps_s[0] += 1
                    dve.wait_ge(sem_["dve"], steps_s[0])

                with spilled(dve, l):
                    steps_s = [0]
                    full(dve, ("moeY", l, NE - 1))
                    for j in range(SPILL):
                        dve.wait_ge(sem_["act"], 3 * j + 2)
                        gated_units(PS[:, 1, :], ex[:, 0, :, :], actT[:, 0, :, :], link_spilled).then_inc(sem_["dve"], 1)
                        steps_s[0] += 1

            def latent_attention():
                dve.wait_ge(s["odd_in"], 32)
                dve.memset(qlS, 0.0)
                dve.memset(qrS, 0.0).then_inc(s["qrS_zero"], 1)
                for t in range(NT):
                    key = ("oin", t)
                    r = ROWS[t]
                    o = pair(key)
                    m = rms[0:r, t % 2, :]
                    tab = rope_t[0:r, t, :]
                    kr = rows[0:r, t, P:ROW_W]
                    tm = tmpm[0:r, 0:32]
                    dve.wait_ge(s["sq_done"], t + 1)
                    dve.tensor_scalar(m[:, 2:3], m[:, 0:1], 1.0 / 256, EPS, ALU.mult, ALU.add)
                    dve.wait_ge(s["rstd_ready"], variance(dve.tensor_scalar(m[:, 3:4], m[:, 1:2], 1.0 / 128, EPS, ALU.mult, ALU.add)))
                    dve.tensor_scalar(cqn[0:r, t % 2, :], o[0:r, 0:256], m[:, 2:3], None, ALU.mult)
                    dve.scalar_tensor_tensor(rows[0:r, t, 0:P], o[0:r, 256:384], m[:, 3:4], kvg[0:r, :], ALU.mult, ALU.mult)
                    dve.tensor_tensor(kr, o[0:r, 384:416], tab[:, 0:32], ALU.mult)
                    dve.tensor_tensor(tm[:, 0:16], o[0:r, 400:416], tab[:, 32:48], ALU.mult)
                    free(dve.tensor_tensor(tm[:, 16:32], o[0:r, 384:400], tab[:, 48:64], ALU.mult), key)
                    taken(dve, key)
                    link(dve.tensor_tensor(kr, kr, tm, ALU.add))
                    dve.tensor_copy(kr4[0:r, t % 2, :].rearrange("p (a b) -> p a b", a=4),
                                    kr.unsqueeze(1).to_broadcast([r, 4, 32])).then_inc(s["oin_ready"], 1)

                def rotate(t):
                    key = ("qrope", t)
                    r = ROWS[t]
                    full(dve, key)
                    if t:
                        dve.wait_ge(s["qrtok_ready"], t)
                    o = pair(key)[0:r, 0:256].rearrange("p (h e) -> p h e", h=8)
                    tab = rope_t[0:r, t, :].unsqueeze(1)
                    q = qr_tok[0:r, t % 2, :].rearrange("p (h e) -> p h e", h=8)
                    u = scratch[0:r, 0:256].rearrange("p (h e) -> p h e", h=8)
                    dve.tensor_tensor(q, o, tab[:, :, 0:32].to_broadcast([r, 8, 32]), ALU.mult)
                    dve.tensor_tensor(u[:, :, 0:16], o[:, :, 16:32], tab[:, :, 32:48].to_broadcast([r, 8, 16]), ALU.mult)
                    free(dve.tensor_tensor(u[:, :, 16:32], o[:, :, 0:16], tab[:, :, 48:64].to_broadcast([r, 8, 16]), ALU.mult), key)
                    taken(dve, key)
                    if t < 4:
                        dve.tensor_tensor(q, q, u, ALU.add).then_inc(s["qrtok_ready"], 1)
                    else:
                        link(dve.tensor_tensor(q, q, u, ALU.add))
                        dve.tensor_copy(qr_rep[0:8, :, :].rearrange("p h (a e) -> p h a e", a=4),
                                        q.unsqueeze(2).to_broadcast([8, 8, 4, 32])).then_inc(s["qrtok_ready"], 1)

                def take(key, dst, src):
                    full(dve, key)
                    free(dve.tensor_copy(dst, src), key)

                for j in (0, 2):
                    take(("qn", j), halves(qnT[:, j, :]), halves(pair(("qn", j))))
                rotate(0)
                for h in (0, 2, 4, 6):
                    take(("ql", h), halves(q_lat[:, h, :]), halves(pair(("ql", h))))
                for t in range(1, NT):
                    rotate(t)
                attention("mla")
                key = ("pN",)
                full(dve, key)
                for i in range(2):
                    own = small[:, OWN + 8 * i:OWN + 8 * i + 8]
                    ins = dve.tensor_tensor(srow[i][:, 1024:1032], pair(key)[:, 512 * i:512 * i + 8], own, ALU.add)
                free(ins, key)
                taken(dve, key)

                def page_maxima(i):
                    key = ("pS", i)
                    full(dve, key)
                    dve.tensor_reduce(st[:, 24:25], pair(key), AX.X, ALU.max)
                    link(dve.tensor_reduce(st[:, 25:26], srow[i][:, 1024:1032], AX.X, ALU.max))
                    link(dve.tensor_tensor(st[:, 24:25], st[:, 24:25], st[:, 25:26], ALU.max))
                    dve.tensor_scalar(st[:, 26:27], st[:, 24:25], -SCALE["mla"], None, ALU.mult).then_inc(s["row_neg"], 1)

                def page_scale(i):
                    taken(dve, ("pS", i))
                    link(dve.tensor_tensor(st[:, 28:29], st[:, 28:29], st[:, 29:30], ALU.add))
                    link(dve.reciprocal(st[:, 30:31], st[:, 28:29]))
                    dve.tensor_scalar(srow[i], srow[i], st[:, 30:31], None, ALU.mult).then_inc(s["row_probs"], 1)

                def page_latents(b):
                    if b % 2 == 0:
                        take(("pcT", b), ckvp[:, b % 2, :], pair(("pcT", b)))

                for b in (0, 2, 4):
                    page_latents(b)
                page_maxima(0)
                page_scale(0)
                page_latents(6)
                page_maxima(1)
                page_scale(1)

            def wide_queries(l):
                dve.memset(q_wide, 0.0).then_inc(s["q_wide_zero"], 1)

            dve.wait_ge(s["lnc_in"], 16)
            norm(0)
            wide_queries(0)
            attention("mem0")
            memory_rows_softmax(0)
            norm(1)
            dve.wait_ge(s["router_in"], 16 * 8)
            experts(0)
            norm(2)
            latent_attention()
            norm(3)
            wide_queries(1)
            attention("mem1")
            memory_rows_softmax(1)
            norm(4)
            experts(1)
            norm(5)


_INS = ["x_prompt", "x_sample", "mem_prompt", "cache_swa_k", "cache_swa_v", "state_ret", "cache_mla", "page_table",
        "cache_mem_k", "cache_mem_v", "w_in_even", "swa_sink", "ret_gn_g", "ret_gn_b", "w_out_even", "w_in_odd",
        "mla_q_norm", "mla_kv_norm", "w_uq", "w_uk", "w_uv", "w_out_odd", "w_mem_q", "w_mem_k", "w_mem_v", "w_mem_o",
        "moe_w_group", "moe_b_group", "moe_w_router", "moe_b_router", "moe_w_in", "moe_w_out", "ln_g", "ln_b"]
_OUTS = [(1, 512, 1024), (8, 1, 1024), (1, 1, 128, 2, 64), (1, 1, 128, 2, 64), (1, 1, 8, 64, 64), (1, 1, 512, 160),
         (2, 1, 256, 4, 64), (2, 1, 256, 4, 64), (1, 8, 128, 2, 64), (1, 8, 128, 2, 64), (1, 8, 8, 64, 64), (1, 8, 1, 160)]


def kernel(**inputs):
    import numpy as _np
    import concourse.bacc as _bacc
    from concourse import mybir as _mybir
    from concourse.bass_utils import run_bass_kernel_spmd as _run

    nc = _bacc.Bacc("TRN2", target_bir_lowering=False, num_devices=1)
    arrays, io = {}, {}
    given = {name: _np.ascontiguousarray(inputs[name]) for name in _INS}
    w_in, w_uq = given.pop("w_in_even"), given.pop("w_uq")
    given["w_in_even"] = w_in
    given["w_ka_twice"] = _np.ascontiguousarray(w_in[0][:, 512:640].reshape(1024, 2, 1, 64).repeat(2, 2).reshape(1024, 256))
    sink = given.pop("swa_sink")[0]
    given["sink_by_bank"] = _np.ascontiguousarray(sink[[0, 2, 1, 3, 4, 6, 5, 7]])
    given["sink_rows"] = _np.tile(sink, 8)
    per_head = w_uq[0].reshape(256, 8, 96)
    ln_g, ln_b = (given[n].reshape(3 * DEPTH, 1, KD, P) for n in ("ln_g", "ln_b"))
    given["ln_by_feature"] = _np.ascontiguousarray(_np.concatenate([ln_g, ln_b], 1).transpose(3, 0, 1, 2))
    given["w_uq_split"] = _np.concatenate([per_head[:, :, :64].reshape(256, 512), per_head[:, :, 64:].reshape(256, 256)], 1)
    given.update({name: _np.ascontiguousarray(a) for name, a in shape_constants().items()})
    for name, a in given.items():
        arrays[f"in_{name}_dram"] = a
        io[name] = nc.dram_tensor(f"in_{name}_dram", a.shape, _mybir.dt.from_np(a.dtype), kind="ExternalInput").ap()
    outs = [nc.dram_tensor(f"out_{i}_dram", shape, _mybir.dt.float32, kind="ExternalOutput").ap()
            for i, shape in enumerate(_OUTS)]
    decoder_step(nc, io, outs)
    r = _run(nc, [arrays], core_ids=[0])
    return tuple(r.results[0][f"out_{i}_dram"] for i in range(len(_OUTS)))
```
